# Optimizing a Trainium2 kernel written in Bass

```python
import math
import jax, jax.numpy as jnp
from jax import lax
import numpy as np

D_MODEL = 1024
BATCH = 1
SEQ = 1024
DEPTH = 1

D_SSM = D_MODEL
SSM_GROUP = 16
N_SSM_GROUPS = D_SSM // SSM_GROUP
SSM_STATE = 64
DT_MIN = 1e-3
DT_MAX = 1e-1
D_CONV = D_MODEL
CONV_WIDTH = 31
D_FF = ((8 * D_MODEL // 3 + 127) // 128) * 128
FFN_RESIDUAL_SCALE = 0.5
D_IN_PROJ = D_SSM + 2 * D_CONV + 2 * D_MODEL
RMS_EPS = 1e-6
LN_EPS = 1e-5

kernel_name = "macaron_s5_conformer_gated_hybrid"

def rms_norm(x, g):
    xf = x.astype(jnp.float32)
    y = xf * lax.rsqrt(jnp.mean(xf * xf, axis=-1, keepdims=True) + RMS_EPS)
    return (y * g.astype(jnp.float32)).astype(x.dtype)

def layer_norm(x, g, b):
    xf = x.astype(jnp.float32)
    mu = jnp.mean(xf, axis=-1, keepdims=True)
    xc = xf - mu
    var = jnp.mean(xc * xc, axis=-1, keepdims=True)
    y = xc * lax.rsqrt(var + LN_EPS) * g.astype(jnp.float32) + b.astype(jnp.float32)
    return y.astype(x.dtype)

def swiglu_ffn(h, w_up, w_down):
    gate, up = jnp.split(h @ w_up, 2, axis=-1)
    return (jax.nn.silu(gate) * up) @ w_down

def _ssm_combine(left, right):
    a1r, a1i, b1r, b1i = left
    a2r, a2i, b2r, b2i = right
    ar = a2r * a1r - a2i * a1i
    ai = a2r * a1i + a2i * a1r
    br = a2r * b1r - a2i * b1i + b2r
    bi = a2r * b1i + a2i * b1r + b2i
    return (ar, ai, br, bi)

def s5_ssm(u, a_re, a_im, log_dt, b_re, b_im, c_re, c_im, d_skip):
    f32 = jnp.float32
    bsz, seq, _ = u.shape
    ug = u.astype(f32).reshape(bsz, seq, N_SSM_GROUPS, SSM_GROUP)
    dt = jnp.exp(log_dt.astype(f32))[:, None]
    ar = a_re.astype(f32)
    ai = a_im.astype(f32)
    mag = jnp.exp(dt * ar)
    abar_re = mag * jnp.cos(dt * ai)
    abar_im = mag * jnp.sin(dt * ai)
    den = ar * ar + ai * ai
    nr = abar_re - 1.0
    ni = abar_im
    f_re = (nr * ar + ni * ai) / den
    f_im = (ni * ar - nr * ai) / den
    br_ = b_re.astype(f32)
    bi_ = b_im.astype(f32)
    bb_re = f_re[..., None] * br_ - f_im[..., None] * bi_
    bb_im = f_re[..., None] * bi_ + f_im[..., None] * br_
    bu_re = jnp.einsum('blgi,gpi->blgp', ug, bb_re)
    bu_im = jnp.einsum('blgi,gpi->blgp', ug, bb_im)
    a_seq_re = jnp.broadcast_to(abar_re[None, None], (1, seq, N_SSM_GROUPS, SSM_STATE))
    a_seq_im = jnp.broadcast_to(abar_im[None, None], (1, seq, N_SSM_GROUPS, SSM_STATE))
    _, _, s_re, s_im = lax.associative_scan(
        _ssm_combine, (a_seq_re, a_seq_im, bu_re, bu_im), axis=1)
    y = (jnp.einsum('blgp,gop->blgo', s_re, c_re.astype(f32))
         - jnp.einsum('blgp,gop->blgo', s_im, c_im.astype(f32)))
    y = y.reshape(bsz, seq, D_SSM) + d_skip.astype(f32) * u.astype(f32)
    return y.astype(u.dtype)

def conformer_conv(v, w_dw, b_dw, ln_g, ln_b, w_pw):
    val, gate = jnp.split(v, 2, axis=-1)
    z = val * jax.nn.sigmoid(gate)
    z = lax.conv_general_dilated(
        z, w_dw, window_strides=(1,), padding=[(CONV_WIDTH - 1, 0)],
        dimension_numbers=('NWC', 'WIO', 'NWC'),
        feature_group_count=D_CONV) + b_dw
    z = jax.nn.silu(layer_norm(z, ln_g, ln_b))
    return z @ w_pw

def setup_inputs(seed: int = 0) -> dict:
    key = jax.random.key(seed)
    ks = jax.random.split(key, 25)
    f32 = jnp.float32

    def nrm(k, shape, scale):
        return jax.random.normal(k, shape, f32) * scale

    def gain(k, shape):
        return 1.0 + 0.02 * jax.random.normal(k, shape, f32)

    n_idx = jnp.arange(SSM_STATE, dtype=f32)
    a_re = -0.5 + 0.01 * jax.random.normal(ks[6], (DEPTH, N_SSM_GROUPS, SSM_STATE), f32)
    a_im = math.pi * n_idx + 0.01 * jax.random.normal(ks[7], (DEPTH, N_SSM_GROUPS, SSM_STATE), f32)
    log_dt = jax.random.uniform(ks[8], (DEPTH, N_SSM_GROUPS), f32,
                                minval=math.log(DT_MIN), maxval=math.log(DT_MAX))
    cplx = math.sqrt(0.5)
    return {
        "x": jax.random.normal(ks[0], (BATCH, SEQ, D_MODEL), f32),
        "norm_ffn1_g": gain(ks[1], (DEPTH, D_MODEL)),
        "w_ffn1_up": nrm(ks[2], (DEPTH, D_MODEL, 2 * D_FF), D_MODEL ** -0.5),
        "w_ffn1_down": nrm(ks[3], (DEPTH, D_FF, D_MODEL), D_FF ** -0.5),
        "norm_mix_g": gain(ks[4], (DEPTH, D_MODEL)),
        "w_in": nrm(ks[5], (DEPTH, D_MODEL, D_IN_PROJ), D_MODEL ** -0.5),
        "ssm_a_re": a_re,
        "ssm_a_im": a_im,
        "ssm_log_dt": log_dt,
        "ssm_b_re": nrm(ks[9], (DEPTH, N_SSM_GROUPS, SSM_STATE, SSM_GROUP), cplx * SSM_GROUP ** -0.5),
        "ssm_b_im": nrm(ks[10], (DEPTH, N_SSM_GROUPS, SSM_STATE, SSM_GROUP), cplx * SSM_GROUP ** -0.5),
        "ssm_c_re": nrm(ks[11], (DEPTH, N_SSM_GROUPS, SSM_GROUP, SSM_STATE), cplx * SSM_STATE ** -0.5),
        "ssm_c_im": nrm(ks[12], (DEPTH, N_SSM_GROUPS, SSM_GROUP, SSM_STATE), cplx * SSM_STATE ** -0.5),
        "ssm_d": nrm(ks[13], (DEPTH, D_SSM), 1.0),
        "w_ssm_glu": nrm(ks[14], (DEPTH, D_SSM, 2 * D_MODEL), D_SSM ** -0.5),
        "conv_dw_w": nrm(ks[15], (DEPTH, CONV_WIDTH, 1, D_CONV), CONV_WIDTH ** -0.5),
        "conv_dw_b": nrm(ks[16], (DEPTH, D_CONV), 0.02),
        "conv_ln_g": gain(ks[17], (DEPTH, D_CONV)),
        "conv_ln_b": nrm(ks[18], (DEPTH, D_CONV), 0.02),
        "w_conv_pw": nrm(ks[19], (DEPTH, D_CONV, D_MODEL), D_CONV ** -0.5),
        "w_out": nrm(ks[20], (DEPTH, D_MODEL, D_MODEL), D_MODEL ** -0.5),
        "norm_ffn2_g": gain(ks[21], (DEPTH, D_MODEL)),
        "w_ffn2_up": nrm(ks[22], (DEPTH, D_MODEL, 2 * D_FF), D_MODEL ** -0.5),
        "w_ffn2_down": nrm(ks[23], (DEPTH, D_FF, D_MODEL), D_FF ** -0.5),
        "norm_final_g": gain(ks[24], (D_MODEL,)),
    }

def reference(x, norm_ffn1_g, w_ffn1_up, w_ffn1_down, norm_mix_g, w_in,
              ssm_a_re, ssm_a_im, ssm_log_dt, ssm_b_re, ssm_b_im, ssm_c_re, ssm_c_im,
              ssm_d, w_ssm_glu, conv_dw_w, conv_dw_b, conv_ln_g, conv_ln_b, w_conv_pw,
              w_out, norm_ffn2_g, w_ffn2_up, w_ffn2_down, norm_final_g):
    for l in range(DEPTH):
        h = rms_norm(x, norm_ffn1_g[l])
        x = x + FFN_RESIDUAL_SCALE * swiglu_ffn(h, w_ffn1_up[l], w_ffn1_down[l])

        h = rms_norm(x, norm_mix_g[l])
        proj = h @ w_in[l]
        u_ssm, v_conv, gate_logits = jnp.split(proj, [D_SSM, D_SSM + 2 * D_CONV], axis=-1)

        y_ssm = s5_ssm(u_ssm, ssm_a_re[l], ssm_a_im[l], ssm_log_dt[l], ssm_b_re[l],
                       ssm_b_im[l], ssm_c_re[l], ssm_c_im[l], ssm_d[l])
        glu_val, glu_gate = jnp.split(jax.nn.gelu(y_ssm) @ w_ssm_glu[l], 2, axis=-1)
        y_a = glu_val * jax.nn.sigmoid(glu_gate)

        y_b = conformer_conv(v_conv, conv_dw_w[l], conv_dw_b[l], conv_ln_g[l],
                             conv_ln_b[l], w_conv_pw[l])

        g_a, g_b = jnp.split(jax.nn.sigmoid(gate_logits), 2, axis=-1)
        x = x + (g_a * y_a + g_b * y_b) @ w_out[l]

        h = rms_norm(x, norm_ffn2_g[l])
        x = x + FFN_RESIDUAL_SCALE * swiglu_ffn(h, w_ffn2_up[l], w_ffn2_down[l])
    return rms_norm(x, norm_final_g)


_drawn_inputs = setup_inputs


def setup_inputs(seed=0):
    import zlib

    import numpy as np

    out = dict(_drawn_inputs(seed))
    spreads = {}
    factors = {'norm_ffn1_g': 6.062,
     'norm_mix_g': 27.988,
     'ssm_a_re': 64.0,
     'ssm_a_im': 42.112,
     'ssm_log_dt': 42.36,
     'ssm_b_re': 59.08,
     'ssm_b_im': 58.672,
     'ssm_c_re': 59.312,
     'ssm_c_im': 58.888,
     'conv_dw_b': 35.108,
     'conv_ln_g': 191.244,
     'conv_ln_b': 193.179,
     'norm_ffn2_g': 30.176,
     'norm_final_g': 23.205}
    for name, (base, spread) in spreads.items():
        noise = np.random.default_rng([zlib.crc32(name.encode()), seed]).standard_normal(out[name].shape)
        drawn = base * np.exp(spread * noise) if base else spread * noise
        out[name] = __import__('jax').numpy.asarray(drawn.astype(out[name].dtype))
    for name, factor in factors.items():
        out[name] = (out[name] * factor).astype(out[name].dtype)
    return out
```

```python
from contextlib import ExitStack
import math

import numpy as np
import concourse.bass as bass
from concourse import mybir
from concourse.alu_op_type import AluOpType as ALU

F32 = mybir.dt.float32
F32R = mybir.dt.float32r
I32 = mybir.dt.int32
ACT = mybir.ActivationFunctionType

P = 128
D = 1024
L = 1024
KT = D // P
DFF = ((8 * D // 3 + 127) // 128) * 128
FT = DFF // P
FI = FT // 2
HW = 512
J = 8
C = L // J
SG = 16
NS = 64
NG = D // SG
GQ = P // SG
PR = GQ // 2
NP = NG // 2
TAPS = 31
PAD = 4
ZB = 2 * J - 1

RMS_EPS = 1e-6
LN_EPS = 1e-5
GELU_A = 0.044715
GELU_S = 2.0 * math.sqrt(2.0 / math.pi)
RINT = 12582912.0
RSQRT_SEED = 1597463007.0

T_BAR, T_BAI = 0, PR * J * SG
T_CAR = 2 * PR * J * SG
T_CAI = T_CAR + PR * (J + 1) * SG
T_COS = T_CAI + PR * (J + 1) * SG
T_SIN = T_COS + PR * C
T_M8 = T_SIN + PR * C
T_ALL = T_M8 + PR


def pieces(x, bits, n):
    out = []
    for _ in range(n - 1):
        e = math.floor(math.log2(abs(x)))
        s = 2.0 ** (bits - 1 - e)
        v = math.floor(abs(x) * s) / s * (1 if x > 0 else -1)
        out.append(v)
        x -= v
    out.append(float(np.float32(x)))
    return out


class Count:

    def __init__(self, sem):
        self.sem, self.n = sem, 0

    def up(self, ins, by=1):
        ins.then_inc(self.sem, by)
        self.n += by
        return self.n


def build(nc, x, norm_ffn1_g, w_ffn1_up, w_ffn1_down, norm_mix_g, w_in, ssm_a_re, ssm_a_im, ssm_log_dt,
          ssm_b_re, ssm_b_im, ssm_c_re, ssm_c_im, ssm_d, w_ssm_glu, conv_dw_w, conv_dw_b, conv_ln_g,
          conv_ln_b, w_conv_pw, w_out, norm_ffn2_g, w_ffn2_up, w_ffn2_down, norm_final_g, out):
    ctx = ExitStack()

    def sb(name, shape, dt=F32):
        return ctx.enter_context(nc.sbuf_tensor(name, shape, dt))

    def sem(name):
        return ctx.enter_context(nc.semaphore(name))

    def sems(name, n):
        return [sem(f"{name}{i}") for i in range(n)]

    def scratch(name, shape):
        return nc.dram_tensor(name, shape, F32).ap()

    d_x = scratch("d_x", [KT, P, L])
    d_tab = scratch("d_tab", [KT, P, T_ALL])
    d_u = scratch("d_u", [P, L])
    d_y = scratch("d_y", [P, L])
    d_gelu = scratch("d_gelu", [KT, P, L])
    d_conv = scratch("d_conv", [KT, P, L])
    d_ga = scratch("d_ga", [KT, P, L])
    d_gb = scratch("d_gb", [KT, P, L])
    d_ma = scratch("d_ma", [KT, P, L])

    XT = sb("XT", [P, KT, L])
    Hhi = sb("Hhi", [P, KT, L], F32R)
    Hlo = sb("Hlo", [P, KT, L], F32R)
    Wraw = sb("Wraw", [P, 2, KT, P])
    Whi = [sb(f"Whi{s}", [P, 2, KT, P], F32R) for s in range(2)]
    Wlo = [sb(f"Wlo{s}", [P, 2, KT, P], F32R) for s in range(2)]
    Draw = sb("Draw", [P, D])
    Dhi = sb("Dhi", [P, 2, D], F32R)
    Dlo = sb("Dlo", [P, 2, D], F32R)
    Ahi = sb("Ahi", [P, 2, L], F32R)
    Alo = sb("Alo", [P, 2, L], F32R)
    G = [sb(f"G{h}", [P, HW]) for h in range(2)]
    TAB = sb("TAB", [P, T_ALL])
    RT = sb("RT", [P, 2, PR, P])
    S = sb("S", [P, 2, PR, C + 1])
    TMP = sb("TMP", [P, 3, HW])
    ones = sb("ones", [P, P])
    ident = sb("ident", [P, P])
    par = sb("par", [P, 3, NP])
    vecs = sb("vecs", [P, 7 * KT])
    wdw = sb("wdw", [P, KT, TAPS])
    dvec = sb("dvec", [SG, NG])
    wq = sb("wq", [P, TAPS + 1])
    dq = sb("dq", [SG, GQ])

    xf = XT[:, :, :].rearrange("p k n -> p (k n)")
    Z = xf[:, 0:ZB * (PAD + C)].rearrange("p (b c) -> p b c", b=ZB)
    o = ZB * (PAD + C)
    CV, UY, UGf, YC, MTf, KKf = [xf[:, o + i * L:o + (i + 1) * L] for i in range(6)]
    UG = UGf.rearrange("p (g c) -> p g c", g=GQ)
    MT = MTf.rearrange("p (g n) -> p g n", g=GQ)
    KK = KKf.rearrange("p (g n) -> p g n", g=GQ)
    nrm = TAB[:, 0:6 * HW].rearrange("p (a n) -> p a n", a=6)
    SQ, RS, NV, NT = [nrm[:, 0, :], nrm[:, 1, :]], [nrm[:, 2, :], nrm[:, 3, :]], nrm[:, 4, :], nrm[:, 5, :]
    tmp12 = TAB[:, 0:12 * 8 * NP].rearrange("p (a e r) -> p a e r", a=12, e=8)
    rt = RT[:, :, :, :].rearrange("p a b c -> p (a b c)")
    sf = S[:, :, :, :].rearrange("p a b c -> p (a b c)")
    tf = TMP[:, :, :].rearrange("p a n -> p (a n)")
    prow = tf[0:NP, 0:3 * P].rearrange("r (a n) -> r a n", a=3)
    rows = tf[0:NG, 3 * P:4 * P + SG]
    ldt = tf[0:NP, 4 * P + SG:4 * P + SG + 2]
    Bb = rt.rearrange("p (a r i) -> p a r i", a=2, i=SG)
    CT = sf[:, 0:2 * NP * SG].rearrange("p (a r i) -> p a r i", a=2, i=SG)
    Cnat = [rt, sf[:, 0:L]]
    PW = tf[:, 0:2 * NP * (J + 1)].rearrange("p (a t r) -> p a t r", a=2, t=J + 1)
    E0 = 2 * NP * (J + 1)
    EE = tf[:, E0:E0 + 14 * NP].rearrange("p (a e r) -> p a e r", a=2, e=7)
    M8 = tf[:, E0 + 14 * NP:E0 + 15 * NP]
    Q0 = E0 + 15 * NP
    pwq = tf[:, Q0:Q0 + 2 * (J + 1) * PR].rearrange("p (a t r) -> p a t r", a=2, t=J + 1)
    Q0 += 2 * (J + 1) * PR
    eeq = tf[:, Q0:Q0 + 14 * PR].rearrange("p (a e r) -> p a e r", a=2, e=7)
    Q0 += 14 * PR
    bbq = tf[:, Q0:Q0 + 2 * PR * SG].rearrange("p (a r i) -> p a r i", a=2, i=SG)
    Q0 += 2 * PR * SG
    ctq = tf[:, Q0:Q0 + 2 * PR * SG].rearrange("p (a r i) -> p a r i", a=2, i=SG)
    assert Q0 + 2 * PR * SG <= 3 * HW
    frfi = sb("frfi", [P, 2, NP])
    Bsc = sb("Bsc", [P, PR * C // 2])
    dd = sb("dd", [SG, GQ, SG])
    BA = TAB[:, T_BAR:T_CAR].rearrange("p (a r n) -> p a r n", a=2, n=J * SG)
    CA = TAB[:, T_CAR:T_COS].rearrange("p (a r n) -> p a r n", a=2, n=(J + 1) * SG)
    COS, SIN = TAB[:, T_COS:T_SIN], TAB[:, T_SIN:T_M8]
    M8q = TAB[:, T_M8:T_ALL]
    GAB = TAB[:, 0:L]
    glb = [RT[:, :, :, :].rearrange("p a b c -> p (a b c)"), TMP[:, :, :].rearrange("p a n -> p (a n)")[:, 0:L]]
    GBB = [TAB[:, L:2 * L], TAB[:, 2 * L:3 * L]]
    MAB = glb
    wflat = Wraw[:, :, :, :].rearrange("p s k n -> p (s k n)")
    xs = fin = [wflat[:, 0:D], wflat[:, D:2 * D], Draw[:, :]]

    PU = [[ctx.enter_context(nc.psum_tensor(f"PU{h}{s}", [P, HW], F32)) for s in range(2)] for h in range(2)]
    PD = [ctx.enter_context(nc.psum_tensor(f"PD{b}", [P, HW], F32)) for b in range(4)]
    PUf = [PU[0][0], PU[0][1], PU[1][0], PU[1][1]]

    R_MIX = FT
    R_GLU = R_MIX + 2 * KT
    R_PW = R_GLU + KT
    R_OUT = R_PW + KT // 2
    R_FFN2 = R_OUT + KT // 2
    R_END = R_FFN2 + FT
    U_MIX, U_FFN2 = FT, FT + KT
    w_raw, w_hi, w_lo = sem("w_raw"), sem("w_hi"), sem("w_lo")
    d_raw, d_hi, d_lo = sem("d_raw"), sem("d_hi"), sem("d_lo")
    gu_full, gu_free = sems("gu_full", 2), sems("gu_free", 2)
    g_ready = sems("g_ready", 2)
    const = sem("const")
    passed = sem("passed")
    x_ld, x_full, x_evac = sems("x_ld", 3), sem("x_full"), sem("x_evac")
    row_ld, row_bc, row_tr, par_in, vec_in = sem("row_ld"), sem("row_bc"), sem("row_tr"), sem("par_in"), sem("vec_in")
    c_ld, c_tr, c_in, b_ld = sem("c_ld"), sem("c_tr"), sem("c_in"), sem("b_ld")
    dw_ld, dw_tr, dw_in = sem("dw_ld"), sem("dw_tr"), sem("dw_in")
    par_chain, par_done = sem("par_chain"), sem("par_done")
    tab_chain, tab_built, tab_saved = sem("tab_chain"), sem("tab_built"), sem("tab_saved")
    norms = {n: {k: sem(f"{n}_{k}") for k in ("sq", "used", "chain", "hn", "hi", "lo")}
             for n in ("nf1", "nmx", "nf2", "nfi")}
    a_hi, a_lo = sems("a_hi", 2), sems("a_lo", 2)
    dn_full, dn_free = sem("dn_full"), sems("dn_free", 4)
    m = {k: sem("m_" + k) for k in (
        "x_saved ba_ld ca_ld rot_ld z z_rep conv cv_saved u_full0 u_full1 u_sb u_saved ug_ld rt_tr rt k_full k_sb k_d "
        "mt_ld delta rot chain y_full y_sb y_saved yc_ld gel gelu gelu_sig gelu_saved ga_w gb_w g_saved0 g_saved1 "
        "wq mt_zero s_zero gchain dd").split()}
    l = {k: sem("l_" + k) for k in (
        "ld sum_in mean cen chain sq var sig ln_sig aff").split()}
    b_ = {k: sem("b_" + k) for k in (
        "gl_ld gl_free gl_hi gl_lo ga_ld t t2 ma_saved p_hi p_lo gb_ld ma_ld m m2 m_hi m_lo xo_ld x xfin fin_tr fin_sb out_saved").split()}
    gl_ld, ma_saved, out_saved = sems("gl_ld", 2), sems("ma_saved", 2), sems("out_saved", 3)
    block = ctx.enter_context(nc.Block())

    cols = lambda w: w[0].rearrange("(k p) n -> p k n", p=P)
    x_rows = x[0].rearrange("(c j) d -> j c d", j=J)
    out_rows = out[0].rearrange("(c j) d -> j c d", j=J)
    hs = [slice(0, HW), slice(HW, L)]
    f32 = lambda ap: ap.bitcast(F32)

    def wait(eng, sem_, value):
        if not isinstance(value, int) or value > 0:
            eng.wait_ge(sem_, value)

    def alone(eng):
        eng.sem_inc(passed, 1)

    @block.sync
    def _(sp):
        for j in range(J):
            if j >= 3:
                sp.wait_ge(x_full, 2 * (j - 2))
            sp.dma_start(xs[j % 3], x_rows[j]).then_inc(x_ld[j % 3], 16)

        def load_pair(src, col0, col1, raw_free):
            if raw_free is not None:
                sp.wait_ge(w_lo, raw_free)
            sp.dma_start(Wraw[:, 0], src[:, :, bass.ds(col0, P)]).then_inc(w_raw, 16)
            sp.dma_start(Wraw[:, 1], src[:, :, bass.ds(col1, P)]).then_inc(w_raw, 16)

        def load_unit(dst, src, raw_free):
            if raw_free is not None:
                sp.wait_ge(d_lo, raw_free)
                alone(sp)
            sp.dma_start(dst, src).then_inc(d_raw, 16)

        def ffn_loads(up, down, r0, u0, first):
            up, down = cols(up), down[0]
            if first:
                sp.wait_ge(x_full, 2 * J)
                load_pair(up, 0, DFF, None)
                load_unit(Draw[:, :], down[0:P, :], None)
                load_pair(up, P, DFF + P, 1)
                load_unit(Draw[:, :], down[P:2 * P, :], 1)
            with sp.Fori(1 if first else 0, FI) as i:
                for s in range(2):
                    load_pair(up, i * (2 * P) + s * P, i * (2 * P) + DFF + s * P, i * 2 + (r0 + s))
                    load_unit(Draw[:, :], down[bass.ds(i * (2 * P) + s * P, P), :], i * 2 + (u0 + s))

        ffn_loads(w_ffn1_up, w_ffn1_down, 0, 0, True)
        wi = cols(w_in)
        def mix_pair(q, s):
            r = q * 2 + (R_MIX + s)
            load_pair(wi, q * P + (1 + 2 * s) * D, q * P + (2 + 2 * s) * D, r)

        def mix_unit(q):
            load_unit(Draw[:, :].rearrange("p (k n) -> p k n", n=P), wi[:, :, bass.ds(q * P, P)], q + U_MIX)

        def glu_pair(p, r):
            load_pair(cols(w_ssm_glu), p * P, p * P + D, r)

        mix_pair(0, 0)
        mix_unit(0)
        mix_pair(0, 1)
        for b in range(4):
            sp.wait_ge(dn_free[b], 4 * FI)
        for h in range(2):
            sp.dma_start(d_x[:, :, hs[h]].rearrange("k p n -> p k n"), XT[:, :, hs[h]]).then_inc(m["x_saved"], 16)

        sp.wait_ge(tab_saved, 16 * KT)
        sp.wait_ge(norms["nmx"]["lo"], 2 * KT)
        sp.dma_start(TAB[:, 0:T_CAR], d_tab[0, :, 0:T_CAR]).then_inc(m["ba_ld"], 16)

        def y_roundtrip(q):
            sp.wait_ge(m["y_sb"], q * 2 + 2)
            dst = d_y.rearrange("(g o) (t c) -> t o g c", g=GQ, t=J)
            for t in range(J):
                sp.dma_start(dst[t], UY[t * SG:(t + 1) * SG, :].rearrange("p (g c) -> p g c", g=GQ))\
                  .then_inc(m["y_saved"], 16)
            sp.wait_ge(m["y_saved"], q * (16 * J) + 16 * J)
            alone(sp)
            wait(sp, m["gelu_saved"], q * 16)
            alone(sp)
            sp.dma_start(YC, d_y).then_inc(m["yc_ld"], 16)

        def gelu_store(q):
            sp.wait_ge(m["gelu"], q * 2 + 2)
            sp.dma_start(d_gelu[q] if isinstance(q, int) else d_gelu[bass.ds(q, 1)].rearrange("a p n -> (a p) n"), YC)\
              .then_inc(m["gelu_saved"], 16)

        def tile_of(t, q):
            return t[q] if isinstance(q, int) else t[bass.ds(q, 1)].rearrange("a p n -> (a p) n")

        def mix_loads(q, first, last):
            if last:
                glu_pair(0, R_GLU)
            else:
                mix_pair(q + 1, 0)
                mix_unit(q + 1)
            if not first:
                sp.wait_ge(m["rot"], q)
            sp.dma_start(TAB[:, T_COS:T_ALL], tile_of(d_tab, q)[:, T_COS:T_ALL]).then_inc(m["rot_ld"], 16)
            if last:
                glu_pair(1, R_GLU + 1)
            else:
                mix_pair(q + 1, 1)
            if not first:
                sp.wait_ge(m["y_full"], q)
            sp.dma_start(TAB[:, T_CAR:T_COS], tile_of(d_tab, q)[:, T_CAR:T_COS]).then_inc(m["ca_ld"], 16)
            if not first:
                y_roundtrip(q - 1)
            sp.wait_ge(m["u_sb"], q * 2 + 2)
            sp.dma_start(d_u, UY).then_inc(m["u_saved"], 16)
            sp.wait_ge(m["u_saved"], q * 16 + 16)
            src = d_u.rearrange("(g i) (j c) -> j i g c", g=GQ, j=J)
            for jr in range(J):
                sp.dma_start(UG[jr * SG:(jr + 1) * SG], src[J - 1 - jr]).then_inc(m["ug_ld"], 16)
            if not last:
                sp.wait_ge(m["k_full"], q + 1)
                sp.dma_start(TAB[:, 0:T_CAR], tile_of(d_tab, q + 1)[:, 0:T_CAR]).then_inc(m["ba_ld"], 16)
            sp.wait_ge(m["k_d"], q + 1)
            for jr in range(J):
                j = J - 1 - jr
                sp.dma_start(MT[jr * SG:(jr + 1) * SG, :, j * SG:P], KK[0:SG, :, 0:(jr + 1) * SG])\
                  .then_inc(m["mt_ld"], 16)
            if not first:
                gelu_store(q - 1)
            for h in range(2):
                for n, dst in enumerate((d_ga, d_gb)):
                    if n == 0:
                        sp.wait_ge(m["ga_w"], q * 2 + (h + 1))
                    else:
                        sp.wait_ge(gu_free[h], q * 2 + (R_MIX + 2))
                    sp.dma_start(tile_of(dst, q)[:, hs[h]], G[n][:, :]).then_inc(m[f"g_saved{n}"], 16)
            sp.wait_ge(m["conv"], q * TAPS + TAPS)
            sp.dma_start(tile_of(d_conv, q), CV).then_inc(m["cv_saved"], 16)

        mix_loads(0, True, False)
        with sp.Fori(1, KT - 1) as q:
            mix_loads(q, False, False)
        mix_loads(KT - 1, False, True)
        y_roundtrip(KT - 1)
        gelu_store(KT - 1)
        sp.wait_ge(m["gelu_saved"], 16 * KT)
        sp.wait_ge(m["cv_saved"], 16 * KT)
        for h in range(2):
            sp.wait_ge(m[f"g_saved{h}"], 32 * KT)

        def gelu_load(k):
            if k >= 2:
                sp.wait_ge(b_["gl_lo"], k - 1)
            sp.dma_start(glb[k % 2], d_gelu[k]).then_inc(gl_ld[k % 2], 16)

        for k in range(KT):
            gelu_load(k)
        for k in range(KT):
            sp.dma_start(XT[:, k, :], d_conv[k]).then_inc(l["ld"], 16)

        def glu_io(p):
            wait(sp, b_["t"], p * 2)
            sp.dma_start(GAB, tile_of(d_ga, p)).then_inc(b_["ga_ld"], 16)
            for h in range(2):
                sp.wait_ge(b_["t"], p * 2 + (h + 1))
                sp.dma_start(tile_of(d_ma, p)[:, hs[h]], G[h][:, :]).then_inc(ma_saved[h], 16)

        sp.wait_ge(m["rot"], KT)
        glu_pair(2, R_GLU + 2)
        glu_io(0)
        with sp.Fori(1, KT - 2) as p:
            glu_pair(p + 2, p + (R_GLU + 2))
            glu_io(p)
        pw, wo = cols(w_conv_pw), cols(w_out)
        for n in range(2):
            load_pair(pw, 2 * n * P, (2 * n + 1) * P, R_PW + n)
            glu_io(KT - 2 + n)
        for h in range(2):
            sp.wait_ge(ma_saved[h], 16 * KT)

        def pw_io(n):
            if n:
                sp.wait_ge(b_["m"], 4 * n)
            for a in range(2):
                sp.dma_start(GBB[a], d_gb[2 * n + a]).then_inc(b_["gb_ld"], 16)
                sp.dma_start(MAB[a], d_ma[2 * n + a]).then_inc(b_["gb_ld"], 16)

        sp.wait_ge(l["sig"], 2 * KT)
        for n in range(KT // 2):
            pw_io(n)
            if n < 2:
                load_pair(pw, 2 * (n + 2) * P, (2 * (n + 2) + 1) * P, R_PW + n + 2)
            else:
                load_pair(wo, 2 * (n - 2) * P, (2 * (n - 2) + 1) * P, R_OUT + n - 2)
        up2, down2 = cols(w_ffn2_up), w_ffn2_down[0]
        for n in range(KT // 2):
            if n == 0:
                sp.wait_ge(b_["m"], 4 * (KT // 2))
            else:
                sp.wait_ge(gu_free[1], R_OUT + n)
            for a in range(2):
                sp.dma_start(GBB[a], d_x[2 * n + a]).then_inc(b_["xo_ld"], 16)
            if n < 2:
                load_pair(wo, 2 * (n + 2) * P, (2 * (n + 2) + 1) * P, R_OUT + n + 2)
            else:
                load_pair(up2, (n - 2) * P, DFF + (n - 2) * P, R_FFN2 + n - 2)
        for s in range(2):
            load_unit(Draw[:, :], down2[s * P:(s + 1) * P, :], U_FFN2 + s)
        with sp.Fori(1, FI) as i:
            for s in range(2):
                load_pair(up2, i * (2 * P) + s * P, i * (2 * P) + DFF + s * P, i * 2 + (R_FFN2 + s))
                load_unit(Draw[:, :], down2[bass.ds(i * (2 * P) + s * P, P), :], i * 2 + (U_FFN2 + s))
        for j in range(J):
            sp.wait_ge(b_["fin_sb"], 2 * (j + 1))
            sp.dma_start(out_rows[j], fin[j % 3]).then_inc(out_saved[j % 3], 16)
        for b in range(3):
            sp.wait_ge(out_saved[b], 16 * len(range(b, J, 3)))
        sp.wait_ge(m["x_saved"], 32)
        sp.wait_ge(m["u_saved"], 16 * KT)
        sp.wait_ge(m["y_saved"], 16 * J * KT)

    @block.gpsimd
    def _(pool):
        g = nc.gpsimd
        g.memset(ones[:, :], 1.0 / D).then_inc(const, 1)
        g.memset(ident[:, :], 0.0).then_inc(const, 1)
        pool.wait_ge(const, 2)
        g.affine_select(out=ident[:, :], in_=ident[:, :], compare_op=ALU.not_equal, fill=1.0, base=0,
                        pattern=[[-1, P]], channel_multiplier=1).then_inc(const, 1)
        n = 0

        def step(ins):
            nonlocal n
            ins.then_inc(tab_chain, 1)
            n += 1
            pool.wait_ge(tab_chain, n)

        def cmul(out_re, out_im, ar, ai, br, bi, t1, t2, do):
            do(g.tensor_tensor(t1, ar, br, ALU.mult))
            do(g.tensor_tensor(t2, ai, bi, ALU.mult))
            do(g.tensor_tensor(out_re, t1, t2, ALU.subtract))
            do(g.tensor_tensor(t1, ar, bi, ALU.mult))
            do(g.tensor_tensor(t2, ai, br, ALU.mult))
            do(g.tensor_tensor(out_im, t1, t2, ALU.add))

        pool.wait_ge(par_done, 1)
        pool.wait_ge(b_ld, 32)
        pool.wait_ge(c_in, 8)
        pool.wait_ge(norms["nf1"]["lo"], 2 * KT)
        fr = frfi[:, 0, :].unsqueeze(2).to_broadcast([P, NP, SG])
        fi = frfi[:, 1, :].unsqueeze(2).to_broadcast([P, NP, SG])
        big = [TAB[:, i * NP * SG:(i + 1) * NP * SG].rearrange("p (r i) -> p r i", i=SG) for i in range(4)]
        step(g.tensor_tensor(big[0], Bb[:, 0], fr, ALU.mult))
        step(g.tensor_tensor(big[1], Bb[:, 1], fi, ALU.mult))
        step(g.tensor_tensor(big[2], Bb[:, 1], fr, ALU.mult))
        step(g.tensor_tensor(big[3], Bb[:, 0], fi, ALU.mult))
        step(g.tensor_tensor(Bb[:, 0], big[0], big[1], ALU.subtract))
        step(g.tensor_tensor(Bb[:, 1], big[2], big[3], ALU.add))
        base = n
        PER = 4 + 1 + 6 + 7 + 2 + 6 * 7

        def tile_table(q):
            n = 0

            def qstep(ins):
                nonlocal n
                ins.then_inc(tab_chain, 1)
                n += 1
                pool.wait_ge(tab_chain, q * PER + (base + n))
                if n in (17, 18, 19):
                    alone(pool)

            r4 = slice(q * PR, (q + 1) * PR) if isinstance(q, int) else bass.ds(q * PR, PR)
            qstep(g.tensor_copy(pwq, PW[:, :, :, r4]))
            qstep(g.tensor_copy(eeq, EE[:, :, :, r4]))
            qstep(g.tensor_copy(bbq, Bb[:, :, r4, :]))
            qstep(g.tensor_copy(ctq, CT[:, :, r4, :]))
            wait(pool, tab_saved, q * 16)
            qstep(g.tensor_copy(M8q, M8[:, r4]))
            pw_ = [[pwq[:, a, 0:nt, :].rearrange("p t r -> p r t").unsqueeze(3).to_broadcast([P, PR, nt, SG])
                    for a in range(2)] for nt in (J, J + 1)]

            def table(view, nt):
                return [view[:, a].rearrange("p r (t i) -> p r t i", i=SG) for a in range(2)]

            def wide(src, nt):
                return [src[:, a].unsqueeze(2).to_broadcast([P, PR, nt, SG]) for a in range(2)]

            ba, ca = table(BA, J), table(CA, J + 1)
            bw, cw = wide(bbq, J), wide(ctq, J + 1)
            sc = TAB[:, T_COS:T_COS + PR * J * SG].rearrange("p (r t i) -> p r t i", r=PR, i=SG)
            qstep(g.tensor_tensor(ba[0], pw_[0][0], bw[0], ALU.mult))
            qstep(g.tensor_tensor(sc, pw_[0][1], bw[1], ALU.mult))
            qstep(g.tensor_tensor(ba[0], ba[0], sc, ALU.subtract))
            qstep(g.tensor_tensor(ba[1], pw_[0][0], bw[1], ALU.mult))
            qstep(g.tensor_tensor(sc, pw_[0][1], bw[0], ALU.mult))
            qstep(g.tensor_tensor(ba[1], ba[1], sc, ALU.add))
            sc9 = TAB[:, T_COS:T_COS + PR * (J + 1) * SG].rearrange("p (r t i) -> p r t i", r=PR, i=SG)
            qstep(g.tensor_tensor(ca[0], pw_[1][0], cw[0], ALU.mult))
            qstep(g.tensor_tensor(sc9, pw_[1][1], cw[1], ALU.mult))
            qstep(g.tensor_tensor(ca[0], ca[0], sc9, ALU.subtract))
            qstep(g.tensor_tensor(ca[1], pw_[1][0], cw[1], ALU.mult))
            qstep(g.tensor_tensor(sc9, pw_[1][1], cw[0], ALU.mult))
            qstep(g.tensor_tensor(ca[1], ca[1], sc9, ALU.add))
            qstep(g.tensor_scalar(ca[1], ca[1], -1.0, None, ALU.mult))
            co = COS.rearrange("p (r c) -> p r c", c=C)
            si = SIN.rearrange("p (r c) -> p r c", c=C)
            qstep(g.memset(co[:, :, 0:1], 1.0))
            qstep(g.memset(si[:, :, 0:1], 0.0))
            for e in range(7):
                w = 2 ** e
                c1, s1 = [eeq[:, a, e, :].unsqueeze(2).to_broadcast([P, PR, w]) for a in range(2)]
                t1 = Bsc[:, 0:PR * w].rearrange("p (r c) -> p r c", c=w)
                c0, s0 = co[:, :, 0:w], si[:, :, 0:w]
                c2, s2 = co[:, :, w:2 * w], si[:, :, w:2 * w]
                qstep(g.tensor_tensor(c2, c0, c1, ALU.mult))
                qstep(g.tensor_tensor(t1, s0, s1, ALU.mult))
                qstep(g.tensor_tensor(c2, c2, t1, ALU.subtract))
                qstep(g.tensor_tensor(s2, s0, c1, ALU.mult))
                qstep(g.tensor_tensor(t1, c0, s1, ALU.mult))
                qstep(g.tensor_tensor(s2, s2, t1, ALU.add))
            assert n == PER, n
            pool.dma_start(d_tab[bass.ds(q, 1)].rearrange("a p n -> (a p) n"), TAB[:, :]).then_inc(tab_saved, 16)

        tile_table(0)
        with pool.Fori(1, KT) as q:
            tile_table(q)
        pool.wait_ge(tab_saved, 16 * KT)

    @block.tensor
    def _(pe):
        mm, tr = nc.tensor.matmul, nc.tensor.transpose

        pe.wait_ge(const, 3)
        pe.wait_ge(row_ld, 16 * 11)
        pe.wait_ge(row_bc, 1)
        for v in range(3):
            tr(PD[0][:, v * NP:(v + 1) * NP], prow[:, v, :], ident[0:NP, 0:NP]).then_inc(row_tr, 1)
        tr(PD[0][:, 96:96 + 7 * KT], rows[0:7 * KT, 0:P], ident[0:7 * KT, 0:7 * KT]).then_inc(row_tr, 1)
        tr(PD[0][0:SG, 160:160 + NG], rows[0:NG, P:P + SG], ident[0:NG, 0:NG]).then_inc(row_tr, 1)
        pe.wait_ge(dw_ld, 32)
        for k in range(KT):
            tr(PD[0][:, 256 + k * TAPS:256 + (k + 1) * TAPS], G[k // 4][0:TAPS, (k % 4) * P:(k % 4 + 1) * P],
               ident[0:TAPS, 0:TAPS]).then_inc(dw_tr, 1)
        pe.wait_ge(c_ld, 64)
        for n in range(4):
            if n == 3:
                pe.wait_ge(vec_in, 2)
                pe.wait_ge(par_in, 1)
                pe.wait_ge(dw_in, 1)
            for t in range(4):
                last = tr(PD[(n + 1) % 4][:, t * P:(t + 1) * P], Cnat[n // 2][:, ((n % 2) * 4 + t) * P:((n % 2) * 4 + t + 1) * P],
                          ident[:, :])
            last.then_inc(c_tr, 1)
        for j in range(J):
            pe.wait_ge(x_ld[j % 3], 16 * (j // 3 + 1))
            for kh in range(2):
                n = 2 * j + kh
                if n >= 4:
                    pe.wait_ge(x_evac, n - 3)
                for k in range(4):
                    last = tr(PUf[n % 4][:, k * P:(k + 1) * P], xs[j % 3][:, (4 * kh + k) * P:(4 * kh + k + 1) * P],
                              ident[:, :])
                last.then_inc(x_full, 1)

        def norm_sums(name, r):
            nm = norms[name]
            if r:
                for h in range(2):
                    pe.wait_ge(gu_free[h], r)
            else:
                pe.wait_ge(x_evac, 2 * J)
            for n in range(2 * KT):
                pe.wait_ge(nm["sq"], n + 1)
                mm(PU[n // KT][0][:, :], ones[:, :], SQ[n % 2], start=n % KT == 0, stop=n % KT == KT - 1)\
                  .then_inc(nm["used"], 1)

        def pair_half(r, s, h, ready):
            if h == 0:
                pe.wait_ge(w_lo, r + 1)
            wait(pe, gu_free[h], r)
            for k in range(KT):
                pe.wait_ge(*ready(k, h))
                for side in range(2):
                    o_ = PU[h][side][:, :]
                    mm(o_, Whi[s][:, side, k, :], Hhi[:, k, hs[h]], start=k == 0, stop=False)
                    mm(o_, Whi[s][:, side, k, :], Hlo[:, k, hs[h]], start=False, stop=False)
                    last = mm(o_, Wlo[s][:, side, k, :], Hhi[:, k, hs[h]], start=False, stop=k == KT - 1)
            last.then_inc(gu_full[h], 1)

        def ffn(n, r0, u0, ready):
            def body(i):
                for s in range(2):
                    for h in range(2):
                        pair_half(i * 2 + (r0 - n * 2 * FI + s), s, h, ready)
                pe.wait_ge(d_lo, i * 2 + (u0 - n * 2 * FI + 2))
                for h in range(2):
                    pe.wait_ge(a_lo[h], i * 2 + 2)
                    for d in range(KT):
                        b = (8 * h + d) % 4
                        wait(pe, dn_free[b], i * 4 + (8 * h + d) // 4)
                        for s in range(2):
                            w = slice(d * P, (d + 1) * P)
                            mm(PD[b][:, :], Dhi[:, s, w], Ahi[:, s, hs[h]], start=s == 0, stop=False)
                            mm(PD[b][:, :], Dhi[:, s, w], Alo[:, s, hs[h]], start=False, stop=False)
                            last = mm(PD[b][:, :], Dlo[:, s, w], Ahi[:, s, hs[h]], start=False, stop=s == 1)
                        last.then_inc(dn_full, 1)

            if n == 0:
                body(0)
            with pe.Fori(n * FI + (n == 0), (n + 1) * FI) as i:
                body(i)

        norm_sums("nf1", 0)
        ffn(0, 0, 0, lambda k, h: (norms["nf1"]["lo"], KT * h + k + 1))
        norm_sums("nmx", R_MIX)

        mix_ready = lambda k, h: (norms["nmx"]["lo"], KT * h + k + 1)

        def s5_outputs(q):
            pe.wait_ge(m["mt_ld"], q * (16 * J) + 16 * J)
            pe.wait_ge(m["rot"], q + 1)
            for pr in range(PR):
                o_ = [PD[2 + g2][:, pr * P:(pr + 1) * P] for g2 in range(2)]
                half = [slice(NS * g2, NS * g2 + NS) for g2 in range(2)]
                for g2 in range(2):
                    mm(o_[g2], MT[:, 2 * pr + g2, :], UG[:, 2 * pr + g2, :], start=True, stop=False)
                for a in range(2):
                    for g2 in range(2):
                        last = mm(o_[g2], CA[half[g2], a, pr, SG:(J + 1) * SG], S[half[g2], a, pr, 0:C],
                                  start=False, stop=a == 1)
            last.then_inc(m["y_full"], 1)

        def mix(q, first):
            for h in range(2):
                pair_half(q * 2 + R_MIX, 0, h, mix_ready)
            if not first:
                s5_outputs(q - 1)
            pe.wait_ge(d_lo, q + (U_MIX + 1))
            if first:
                for b in range(4):
                    pe.wait_ge(dn_free[b], 4 * FI)
            wait(pe, m["k_sb"], q * 2)
            for h in range(2):
                for k in range(KT):
                    w = slice(k * P, (k + 1) * P)
                    mm(PD[h][:, :], Dhi[:, 0, w], Hhi[:, k, hs[h]], start=k == 0, stop=False)
                    mm(PD[h][:, :], Dhi[:, 0, w], Hlo[:, k, hs[h]], start=False, stop=False)
                    last = mm(PD[h][:, :], Dlo[:, 0, w], Hhi[:, k, hs[h]], start=False, stop=k == KT - 1)
                last.then_inc(m[f"u_full{h}"], 1)
            pe.wait_ge(m["ba_ld"], q * 16 + 16)
            wait(pe, m["y_sb"], q * 2)
            for a in range(2):
                for pr in range(PR):
                    last = tr(PD[2 + a][:, pr * P:(pr + 1) * P], BA[:, a, pr, :], ident[:, :])
                last.then_inc(m["rt_tr"], 1)
            pe.wait_ge(m["ca_ld"], q * 16 + 16)
            pe.wait_ge(m["u_sb"], q * 2 + 2)
            alone(pe)
            for g2 in range(2):
                at = slice(NS * g2, NS * g2 + NS)
                for pr in range(PR):
                    for a in range(2):
                        last = mm(PD[g2][0:SG, pr * P:(pr + 1) * P], BA[at, a, pr, 0:SG], CA[at, a, pr, 0:J * SG],
                                  start=a == 0, stop=a == 1)
            last.then_inc(m["k_full"], 1)
            pair_half(q * 2 + (R_MIX + 1), 1, 0, mix_ready)
            pe.wait_ge(m["ug_ld"], q * (16 * J) + 16 * J)
            pe.wait_ge(m["rt"], q * 2 + 2)
            for g in range(GQ):
                at = slice(NS * (g % 2), NS * (g % 2) + NS)
                for a in range(2):
                    last = mm(PD[2 + a][at, (g // 2) * P:(g // 2 + 1) * P], RT[:, a, g // 2, at], UG[:, g, :],
                              start=True, stop=True)
            last.then_inc(m["delta"], 1)
            pair_half(q * 2 + (R_MIX + 1), 1, 1, mix_ready)

        mix(0, True)
        with pe.Fori(1, KT) as q:
            mix(q, False)
        s5_outputs(KT - 1)

        def pairs(n, r0, lo):
            ready = lambda k, h: (lo, k + 1)
            with pe.Fori(0, n // 2) as i:
                for s in range(2):
                    for h in range(2):
                        pair_half(i * 2 + (r0 + s), s, h, ready)

        pairs(KT, R_GLU, b_["gl_lo"])
        pe.wait_ge(l["ld"], 16 * KT)
        pe.wait_ge(m["y_sb"], 2 * KT)
        for h in range(2):
            for k in range(KT):
                last = mm(PD[h][:, :], ones[:, :], XT[:, k, hs[h]], start=k == 0, stop=k == KT - 1)
            last.then_inc(l["mean"], 1)
        for n in range(2 * KT):
            pe.wait_ge(l["sq"], n + 1)
            mm(PD[2 + n // KT][:, :], ones[:, :], SQ[n % 2], start=n % KT == 0, stop=n % KT == KT - 1)\
              .then_inc(l["var"], 1)
        pairs(KT // 2, R_PW, b_["p_lo"])
        pairs(KT // 2, R_OUT, b_["m_lo"])
        norm_sums("nf2", R_FFN2)
        ffn(1, R_FFN2, U_FFN2, lambda k, h: (norms["nf2"]["lo"], KT * h + k + 1))
        norm_sums("nfi", R_END)
        for b in range(4):
            pe.wait_ge(dn_free[b], 8 * FI)
        for j in range(J):
            pe.wait_ge(norms["nfi"]["hn"], KT * (j // 4 + 1))
            for kh in range(2):
                n = 2 * j + kh
                if n >= 4:
                    pe.wait_ge(b_["fin_sb"], n - 3)
                for k in range(4):
                    last = tr(PD[n % 4][:, k * P:(k + 1) * P], XT[:, 4 * kh + k, j * P:(j + 1) * P], ident[:, :])
                last.then_inc(b_["fin_tr"], 1)

    @block.scalar
    def _(act):
        fn = nc.scalar.activation

        small = [(prow[:, 0, :], ssm_a_re[0].rearrange("(r a) p -> r (a p)", a=2)),
                 (prow[:, 1, :], ssm_a_im[0].rearrange("(r a) p -> r (a p)", a=2)),
                 (ldt[:, :], ssm_log_dt[0].rearrange("(r a) -> r a", a=2))]
        vec = [norm_ffn1_g[0], norm_mix_g[0], norm_ffn2_g[0], norm_final_g, conv_dw_b[0], conv_ln_g[0], conv_ln_b[0]]
        small += [(rows[v * KT:(v + 1) * KT, 0:P], a.rearrange("(k p) -> k p", p=P)) for v, a in enumerate(vec)]
        small += [(rows[0:NG, P:P + SG], ssm_d[0].rearrange("(g i) -> g i", i=SG))]
        for dst, src in small:
            act.dma_start(dst, src).then_inc(row_ld, 16)
        for h in range(2):
            act.dma_start(G[h][0:TAPS, :], conv_dw_w[0][:, 0, hs[h]]).then_inc(dw_ld, 16)
        for a, c in enumerate((ssm_c_re, ssm_c_im)):
            nat = Cnat[a].rearrange("p (t n) -> p t n", t=KT)
            for z in range(2):
                act.dma_start(nat[:, :, z * NS:(z + 1) * NS], c[0].rearrange("(t g) o p -> (g o) t p", t=KT))\
                   .then_inc(c_ld, 16)
        act.wait_ge(row_ld, 16 * 11)
        fn(prow[:, 2, :].rearrange("r (a p) -> r a p", a=2), ldt[:, :].unsqueeze(2).to_broadcast([NP, 2, NS]),
           ACT.Copy).then_inc(row_bc, 1)
        act.wait_ge(row_tr, 5)
        act.wait_ge(dw_tr, KT)
        fn(par[:, :, :].rearrange("p a r -> p (a r)"), PD[0][:, 0:96], ACT.Copy).then_inc(par_in, 1)
        fn(vecs[:, :], PD[0][:, 96:96 + 7 * KT], ACT.Copy).then_inc(vec_in, 1)
        fn(dvec[:, :], PD[0][0:SG, 160:160 + NG], ACT.Copy).then_inc(vec_in, 1)
        fn(wdw[:, :, :].rearrange("p k t -> p (k t)"), PD[0][:, 256:256 + KT * TAPS], ACT.Copy).then_inc(dw_in, 1)
        act.wait_ge(c_tr, 4)
        for n in range(4):
            v = PD[(n + 1) % 4][:, :].rearrange("p (r a i) -> p a r i", a=2, i=SG)
            for g2 in range(2):
                at = slice(NS * g2, NS * g2 + NS)
                fn(CT[at, n // 2, (n % 2) * 16:(n % 2) * 16 + 16, :], v[at, g2], ACT.Copy).then_inc(c_in, 1)
        for a, b in enumerate((ssm_b_re, ssm_b_im)):
            act.dma_start(Bb[:, a], b[0].rearrange("(r a) p i -> (a p) r i", a=2)).then_inc(b_ld, 16)
        for n in range(2 * J):
            act.wait_ge(x_full, n + 1)
            fn(XT[:, 4 * (n % 2):4 * (n % 2) + 4, (n // 2) * P:(n // 2 + 1) * P],
               PUf[n % 4][:, :].rearrange("p (k c) -> p k c", c=P), ACT.Copy).then_inc(x_evac, 1)

        def split_pair(r, s, wait_used=True):
            act.wait_ge(w_raw, r * 32 + 32)
            if wait_used:
                act.wait_ge(gu_full[1], r - 1)
            fn(Whi[s][:, :, :, :], Wraw[:, :, :, :], ACT.Copy).then_inc(w_hi, 1)

        def split_unit(u, s, used, value):
            act.wait_ge(d_raw, u * 16 + 16)
            wait(act, used, value)
            fn(Dhi[:, s, :], Draw[:, :], ACT.Copy).then_inc(d_hi, 1)

        def norm(name, xt_ready, split=True):
            nm = norms[name]
            for n in range(2 * KT):
                k, h = n % KT, n // KT
                act.wait_ge(*xt_ready(k, h))
                if n >= 2:
                    act.wait_ge(nm["used"], n - 1)
                fn(SQ[n % 2], XT[:, k, hs[h]], ACT.Square).then_inc(nm["sq"], 1)
            if split:
                for n in range(2 * KT):
                    act.wait_ge(nm["hn"], n + 1)
                    fn(Hhi[:, n % KT, hs[n // KT]], G[n % 2][:, :], ACT.Copy).then_inc(nm["hi"], 1)

        def ffn(n, r0, u0):
            act.wait_ge(norms[("nf1", "nf2")[n]]["lo"], 2 * KT)

            def body(i, last):
                for s in range(2):
                    for h in range(2):
                        act.wait_ge(gu_full[h], i * 2 + (r0 - n * 2 * FI + s + 1))
                        wait(act, a_lo[h], i * 2 + s)
                        fn(G[h][:, :], PU[h][0][:, :], ACT.Silu).then_inc(g_ready[h], 1)
                        if s == 0:
                            split_unit(i * 2 + (u0 - n * 2 * FI + h), h, dn_full, i * 16)
                    if not last:
                        split_pair(i * 2 + (r0 - n * 2 * FI + s + 2), s)

            if n == 0:
                body(0, False)
            with act.Fori(n * FI + (n == 0), (n + 1) * FI - n) as i:
                body(i, False)
            if n:
                body(2 * FI - 1, True)

        split_pair(0, 0, False)
        split_pair(1, 1, False)
        norm("nf1", lambda k, h: (x_evac, J * (h + 1)))
        ffn(0, 0, 0)
        act.wait_ge(tab_saved, 16 * KT)
        norm("nmx", lambda k, h: (dn_free[(8 * h + k) % 4], 4 * (FI - 1) + (8 * h + k) // 4 + 1))

        def mix(q, first):
            r = q * 2 + R_MIX
            if first:
                act.wait_ge(norms["nmx"]["lo"], 2 * KT)
            for h in range(2):
                act.wait_ge(gu_full[h], r + 1)
                wait(act, m[f"g_saved{h}"], q * 32)
                fn(G[h][:, :], PU[h][1][:, :], ACT.Sigmoid).then_inc(g_ready[h], 1)
                if h == 0:
                    if first:
                        split_unit(q + U_MIX, 0, dn_full, 16 * FI)
                    else:
                        split_unit(q + U_MIX, 0, m["u_full1"], q)
            split_pair(r + 2, 0)
            if not first:
                act.wait_ge(m["y_full"], q)
                act.wait_ge(m["u_saved"], q * 16)
                evacuate_y()
            act.wait_ge(gu_free[0], r + 1)
            act.wait_ge(gu_free[1], r + 1)
            if first:
                act.wait_ge(m["mt_zero"], 2)
            fn(Z[:, 0:J - 1, PAD:PAD + C], Z[:, J:ZB, PAD - 1:PAD - 1 + C], ACT.Copy).then_inc(m["z_rep"], 1)
            for h in range(2):
                act.wait_ge(m[f"u_full{h}"], q + 1)
                wait(act, m["y_saved"], q * (16 * J))
                if first:
                    act.wait_ge(m["x_saved"], 32)
                fn(UY[:, hs[h]], PD[h][:, :], ACT.Copy).then_inc(m["u_sb"], 1)
            for a in range(2):
                act.wait_ge(m["rt_tr"], q * 2 + (a + 1))
                fn(RT[:, a].rearrange("p r n -> p (r n)"), PD[2 + a][:, :], ACT.Copy).then_inc(m["rt"], 1)
            act.wait_ge(m["k_full"], q + 1)
            wait(act, m["mt_ld"], q * (16 * J))
            for g2 in range(2):
                fn(KK[0:SG].rearrange("i (r a) n -> i a r n", a=2)[:, g2],
                   PD[g2][0:SG, :].rearrange("i (r n) -> i r n", n=P), ACT.Copy).then_inc(m["k_sb"], 1)
            if not first:
                gelu_sigmoid(q - 1)
            for h in range(2):
                act.wait_ge(gu_full[h], r + 2)
                for n in range(2):
                    if h == 0:
                        act.wait_ge(gu_free[n], r + 1)
                    else:
                        act.wait_ge(m[f"g_saved{n}"], q * 32 + 16)
                    fn(G[n][:, :], PU[h][n][:, :], ACT.Sigmoid).then_inc(m["ga_w"] if n == 0 else gu_free[h], 1)
            split_pair(r + 3, 1)

        def evacuate_y():
            for g2 in range(2):
                fn(UY.rearrange("p (r a c) -> p a r c", a=2, c=C)[:, g2], PD[2 + g2][:, :].rearrange("p (r c) -> p r c", c=C),
                   ACT.Copy).then_inc(m["y_sb"], 1)

        def gelu_sigmoid(q):
            for h in range(2):
                act.wait_ge(m["gel"], q * 2 + (h + 1))
                fn(TMP[:, h, :], TMP[:, h, :], ACT.Sigmoid, scale=GELU_S).then_inc(m["gelu_sig"], 1)

        mix(0, True)
        with act.Fori(1, KT) as q:
            mix(q, False)
        act.wait_ge(m["y_full"], KT)
        act.wait_ge(m["u_saved"], 16 * KT)
        evacuate_y()
        gelu_sigmoid(KT - 1)

        def split_h(src, ready, hi, used):
            act.wait_ge(gu_full[1], used)
            for k in range(KT):
                for w in ready(k):
                    act.wait_ge(*w)
                fn(Hhi[:, k, :], src(k), ACT.Copy).then_inc(hi, 1)

        split_h(lambda k: glb[k % 2], lambda k: [(gl_ld[k % 2], 16 * (k // 2 + 1))], b_["gl_hi"], R_GLU)
        for h in range(2):
            act.wait_ge(m[f"g_saved{h}"], 32 * KT)

        def glu(i):
            for s in range(2):
                for h in range(2):
                    act.wait_ge(gu_full[h], i * 2 + (R_GLU + s + 1))
                    wait(act, ma_saved[h], i * 32 + s * 16)
                    fn(G[h][:, :], PU[h][1][:, :], ACT.Sigmoid).then_inc(g_ready[h], 1)
                split_pair(i * 2 + (R_GLU + s + 2), s)

        glu(0)
        with act.Fori(1, KT // 2) as i:
            glu(i)
        act.wait_ge(b_["t"], 2 * KT)
        for n in range(2 * KT):
            act.wait_ge(l["cen"], n + 1)
            if n >= 2:
                act.wait_ge(l["var"], n - 1)
            fn(SQ[n % 2], XT[:, n % KT, hs[n // KT]], ACT.Square).then_inc(l["sq"], 1)
        act.wait_ge(l["var"], 2 * KT)
        for n in range(2 * KT):
            k, h = n % KT, n // KT
            act.wait_ge(l["sum_in"], n + 1)
            if n >= 2:
                act.wait_ge(l["sig"], n - 1)
            fn(SQ[n % 2], XT[:, k, hs[h]], ACT.Sigmoid, scale=vecs[:, 5 * KT + k:5 * KT + k + 1],
               bias=vecs[:, 6 * KT + k:6 * KT + k + 1]).then_inc(l["ln_sig"], 1)
        split_h(lambda k: XT[:, k, :], lambda k: [(l["sig"], KT + k + 1)], b_["p_hi"], R_PW)
        for n in range(KT // 2):
            act.wait_ge(gu_full[1], R_PW + n + 1)
            split_pair(R_PW + n + 2, n % 2)
        split_h(lambda k: XT[:, k, :], lambda k: [(b_["m"], 4 * (k // 2) + 3 + k % 2)], b_["m_hi"], R_OUT)
        for n in range(KT // 2):
            act.wait_ge(gu_full[1], R_OUT + n + 1)
            split_pair(R_OUT + n + 2, n % 2)
        norm("nf2", lambda k, h: (gu_free[h], R_OUT + k // 2 + 1))
        ffn(1, R_FFN2, U_FFN2)
        norm("nfi", lambda k, h: (dn_free[(8 * h + k) % 4], 4 * (2 * FI - 1) + (8 * h + k) // 4 + 1), False)
        for n in range(2 * J):
            j = n // 2
            act.wait_ge(b_["fin_tr"], n + 1)
            if j >= 3:
                act.wait_ge(out_saved[j % 3], 16 * (j // 3))
            fn(fin[j % 3][:, (n % 2) * HW:(n % 2 + 1) * HW], PD[n % 4][:, :], ACT.Copy).then_inc(b_["fin_sb"], 1)

    @block.vector
    def _(dve):
        v = nc.vector
        tt, ts, stt = v.tensor_tensor, v.tensor_scalar, v.scalar_tensor_tensor

        n_par = 0

        def do(ins):
            nonlocal n_par
            ins.then_inc(par_chain, 1)
            n_par += 1
            dve.wait_ge(par_chain, n_par)

        def slot(i, e=8):
            return tmp12[:, i, 0:e, :]

        def exp(dst, src, e, t0):
            xx, k, kk, p_ = [slot(t0 + i, e) for i in range(4)]
            do(ts(xx, src, -200.0, 200.0, ALU.max, ALU.min))
            do(ts(k, xx, 1.0 / math.log(2.0), RINT, ALU.mult, ALU.add))
            do(ts(k, k, RINT, None, ALU.subtract))
            ln2 = pieces(math.log(2.0), 12, 3)
            for c in ln2:
                do(stt(xx, k, -c, xx, ALU.mult, ALU.add))
            do(ts(p_, xx, 1.0 / 5040.0, None, ALU.mult))
            for c in (1.0 / 720.0, 1.0 / 120.0, 1.0 / 24.0, 1.0 / 6.0, 0.5, 1.0):
                do(stt(p_, p_, c, xx, ALU.add, ALU.mult))
            do(ts(p_, p_, 1.0, None, ALU.add))
            do(ts(kk, k, -126.0, 127.0, ALU.max, ALU.min))
            do(tt(k, k, kk, ALU.subtract))
            do(ts(k, k, -126.0, 127.0, ALU.max, ALU.min))
            for z in (kk, k):
                do(ts(xx.bitcast(I32), z, 127.0, 8388608.0, ALU.add, ALU.mult))
                do(tt(p_, p_, xx, ALU.mult))
            do(v.tensor_copy(dst, p_))

        dve.wait_ge(par_in, 1)
        a_re, a_im = par[:, 0, :], par[:, 1, :]
        ang, dtr, mag = slot(11), slot(10, 2), slot(9, 2)
        one = lambda ap: ap.unsqueeze(1)
        dt = slot(8, 1)
        exp(dt, one(par[:, 2, :]), 1, 0)
        do(tt(dtr[:, 0:1], dt, one(a_re), ALU.mult))
        do(ts(dtr[:, 1:2], dtr[:, 0:1], float(J), None, ALU.mult))
        do(tt(ang[:, 0:1], dt, one(a_im), ALU.mult))
        for e in range(7):
            do(ts(ang[:, e + 1:e + 2], ang[:, 0:1], float(J * 2 ** e), None, ALU.mult))
        exp(mag, dtr, 2, 0)
        k_, r_, r2, sn, cs, t_, q_ = [slot(i) for i in range(7)]
        do(ts(k_, ang, 2.0 / math.pi, RINT, ALU.mult, ALU.add))
        do(ts(k_, k_, RINT, None, ALU.subtract))
        do(v.tensor_copy(r_, ang))
        for c in pieces(math.pi / 2, 8, 4):
            do(stt(r_, k_, -c, r_, ALU.mult, ALU.add))
        do(tt(r2, r_, r_, ALU.mult))
        do(ts(sn, r2, -1.9515295891e-4, 8.3321608736e-3, ALU.mult, ALU.add))
        do(tt(sn, sn, r2, ALU.mult))
        do(stt(sn, sn, -1.6666654611e-1, r2, ALU.add, ALU.mult))
        do(tt(sn, sn, r_, ALU.mult))
        do(tt(sn, sn, r_, ALU.add))
        do(ts(cs, r2, 2.443315711809948e-5, -1.388731625493765e-3, ALU.mult, ALU.add))
        do(tt(cs, cs, r2, ALU.mult))
        do(stt(cs, cs, 4.166664568298827e-2, r2, ALU.add, ALU.mult))
        do(stt(cs, cs, -0.5, r2, ALU.add, ALU.mult))
        do(ts(cs, cs, 1.0, None, ALU.add))
        do(ts(t_, k_, 0.25, RINT, ALU.mult, ALU.add))
        do(ts(t_, t_, RINT, None, ALU.subtract))
        do(stt(k_, t_, -4.0, k_, ALU.mult, ALU.add))
        do(tt(t_, k_, k_, ALU.mult))
        do(ts(r_, t_, 4.0, -1.0, ALU.is_equal, ALU.mult))
        do(ts(r2, t_, 0.0, None, ALU.is_equal))
        do(tt(r_, r_, r2, ALU.add))
        do(ts(t_, t_, 1.0, None, ALU.is_equal))
        do(tt(k_, k_, t_, ALU.mult))
        do(tt(q_, r_, sn, ALU.mult))
        do(tt(t_, k_, cs, ALU.mult))
        do(tt(q_, q_, t_, ALU.add))
        do(tt(t_, r_, cs, ALU.mult))
        do(tt(r2, k_, sn, ALU.mult))
        do(tt(t_, t_, r2, ALU.subtract))
        do(v.tensor_copy(EE[:, 0], t_[:, 1:8]))
        do(v.tensor_copy(EE[:, 1], q_[:, 1:8]))
        do(v.tensor_copy(one(M8), mag[:, 1:2]))
        do(v.memset(PW[:, 0, 0:1], 1.0))
        do(v.memset(PW[:, 1, 0:1], 0.0))
        do(tt(PW[:, 0, 1:2], mag[:, 0:1], t_[:, 0:1], ALU.mult))
        do(tt(PW[:, 1, 1:2], mag[:, 0:1], q_[:, 0:1], ALU.mult))
        for w in (1, 2, 4):
            lo_, hi_ = slice(1, w + 1), slice(w + 1, 2 * w + 1)
            br = PW[:, 0, w:w + 1].to_broadcast([P, w, NP])
            bi = PW[:, 1, w:w + 1].to_broadcast([P, w, NP])
            t1, t2 = slot(0, w), slot(1, w)
            do(tt(t1, PW[:, 0, lo_], br, ALU.mult))
            do(tt(t2, PW[:, 1, lo_], bi, ALU.mult))
            do(tt(PW[:, 0, hi_], t1, t2, ALU.subtract))
            do(tt(t1, PW[:, 0, lo_], bi, ALU.mult))
            do(tt(t2, PW[:, 1, lo_], br, ALU.mult))
            do(tt(PW[:, 1, hi_], t1, t2, ALU.add))
        ar1, ai1 = one(a_re), one(a_im)
        nr, ni = slot(0, 1), PW[:, 1, 1:2]
        t1, t2, den = slot(1, 1), slot(2, 1), slot(3, 1)
        do(ts(nr, PW[:, 0, 1:2], -1.0, None, ALU.add))
        do(tt(t1, ar1, ar1, ALU.mult))
        do(tt(t2, ai1, ai1, ALU.mult))
        do(tt(den, t1, t2, ALU.add))
        do(v.reciprocal(den, den))
        do(tt(t1, nr, ar1, ALU.mult))
        do(tt(t2, ni, ai1, ALU.mult))
        do(tt(t1, t1, t2, ALU.add))
        do(tt(one(frfi[:, 0, :]), t1, den, ALU.mult))
        do(tt(t1, ni, ar1, ALU.mult))
        do(tt(t2, nr, ai1, ALU.mult))
        do(tt(t1, t1, t2, ALU.subtract))
        tt(one(frfi[:, 1, :]), t1, den, ALU.mult).then_inc(par_done, 1)
        dve.wait_ge(par_done, 1)

        def split_pair(r, s):
            dve.wait_ge(w_hi, r + 1)
            tt(Wlo[s][:, :, :, :], Wraw[:, :, :, :], f32(Whi[s][:, :, :, :]), ALU.subtract).then_inc(w_lo, 1)

        def split_unit(u, s):
            dve.wait_ge(d_hi, u + 1)
            tt(Dlo[:, s, :], Draw[:, :], f32(Dhi[:, s, :]), ALU.subtract).then_inc(d_lo, 1)

        def rsqrt(dst, src, eps, chain):
            def step(ins):
                dve.wait_ge(chain.sem, chain.up(ins))
            step(ts(NV, src, eps, None, ALU.add))
            step(ts(dst.bitcast(I32), NV.bitcast(I32), -0.5, RSQRT_SEED, ALU.mult, ALU.add))
            for _ in range(3):
                step(stt(NT, dst, -0.5, dst, ALU.mult, ALU.mult))
                step(tt(NT, NT, NV, ALU.mult))
                step(stt(dst, NT, 1.5, dst, ALU.add, ALU.mult))

        def norm(name, gain, split=True):
            nm = norms[name]
            chain = Count(nm["chain"])
            for h in range(2):
                dve.wait_ge(nm["used"], KT * (h + 1))
                rsqrt(RS[h], PU[h][0][:, :], RMS_EPS, chain)
                for k in range(KT + 1 if split else KT):
                    n = KT * h + k
                    if k < KT:
                        if split and n >= 2:
                            dve.wait_ge(nm["lo"], n - 1)
                        dst = G[n % 2][:, :] if split else XT[:, k, hs[h]]
                        stt(dst, XT[:, k, hs[h]], vecs[:, gain * KT + k:gain * KT + k + 1], RS[h], ALU.mult, ALU.mult)\
                            .then_inc(nm["hn"], 1)
                    if split and k >= 1:
                        dve.wait_ge(nm["hi"], n)
                        tt(Hlo[:, k - 1, hs[h]], G[(n - 1) % 2][:, :], f32(Hhi[:, k - 1, hs[h]]), ALU.subtract)\
                            .then_inc(nm["lo"], 1)

        def ffn(n, r0, u0, g0):
            def body(i, last):
                for s in range(2):
                    for h in range(2):
                        dve.wait_ge(g_ready[h], i * 2 + (g0 - n * 2 * FI + s + 1))
                        tt(G[h][:, :], G[h][:, :], PU[h][1][:, :], ALU.mult).then_inc(gu_free[h], 1)
                        dve.wait_ge(gu_free[h], i * 2 + (r0 - n * 2 * FI + s + 1))
                        wait(dve, dn_full, i * 16)
                        v.tensor_copy(Ahi[:, s, hs[h]], G[h][:, :]).then_inc(a_hi[h], 1)
                        dve.wait_ge(a_hi[h], i * 2 + (s + 1))
                        tt(Alo[:, s, hs[h]], G[h][:, :], f32(Ahi[:, s, hs[h]]), ALU.subtract).then_inc(a_lo[h], 1)
                        if s == 0:
                            split_unit(i * 2 + (u0 - n * 2 * FI + h), h)
                    if not last:
                        split_pair(i * 2 + (r0 - n * 2 * FI + s + 2), s)
                for h in range(2):
                    for d in range(KT):
                        z = 8 * h + d
                        dve.wait_ge(dn_full, i * 16 + (z + 1))
                        stt(XT[:, d, hs[h]], PD[z % 4][:, :], 0.5, XT[:, d, hs[h]], ALU.mult, ALU.add)\
                            .then_inc(dn_free[z % 4], 1)

            if n == 0:
                body(0, False)
            with dve.Fori(n * FI + (n == 0), (n + 1) * FI - n) as i:
                body(i, False)
            if n:
                body(2 * FI - 1, True)

        split_pair(0, 0)
        split_pair(1, 1)
        dve.wait_ge(vec_in, 2)
        norm("nf1", 0)
        ffn(0, 0, 0, 0)
        norm("nmx", 1)

        dve.wait_ge(m["x_saved"], 32)
        v.memset(Z[:, :, 0:PAD], 0.0).then_inc(m["mt_zero"], 1)
        v.memset(MTf, 0.0).then_inc(m["mt_zero"], 1)
        v.memset(S[:, :, :, 0:1], 0.0).then_inc(m["s_zero"], 1)
        CVb = CV.rearrange("p (b c) -> p b c", b=J)
        ROT = 5 + 1 + 2 * PR + 6

        def taps(q, s0, s1):
            for s in range(s0, s1):
                z_ = Z[:, J - 1 - s % J:ZB - s % J, PAD - s // J:PAD - s // J + C]
                w_ = wq[:, TAPS - 1 - s:TAPS - s]
                if s == 0:
                    dve.wait_ge(m["z_rep"], q + 1)
                    dve.wait_ge(m["wq"], q * 3 + 3)
                    wait(dve, m["cv_saved"], q * 16)
                    ts(CVb, z_, w_, wq[:, TAPS:TAPS + 1], ALU.mult, ALU.add).then_inc(m["conv"], 1)
                else:
                    dve.wait_ge(m["conv"], q * TAPS + s)
                    stt(CVb, z_, w_, CVb, ALU.mult, ALU.add).then_inc(m["conv"], 1)

        def gelu_in(q):
            dve.wait_ge(m["yc_ld"], q * 16 + 16)
            for h in range(2):
                t_ = TMP[:, h, :]
                tt(t_, YC[:, hs[h]], YC[:, hs[h]], ALU.mult).then_inc(m["gchain"], 1)
                dve.wait_ge(m["gchain"], q * 4 + (2 * h + 1))
                ts(t_, t_, GELU_A, 1.0, ALU.mult, ALU.add).then_inc(m["gchain"], 1)
                dve.wait_ge(m["gchain"], q * 4 + (2 * h + 2))
                tt(t_, t_, YC[:, hs[h]], ALU.mult).then_inc(m["gel"], 1)

        def gelu_out(q):
            for h in range(2):
                dve.wait_ge(m["gelu_sig"], q * 2 + (h + 1))
                tt(YC[:, hs[h]], YC[:, hs[h]], TMP[:, h, :], ALU.mult).then_inc(m["gelu"], 1)

        def mix(q, first):
            r = q * 2 + R_MIX
            wait(dve, m["conv"], q * TAPS)
            wait(dve, m["dd"], q)
            v.tensor_copy(wq[:, 0:TAPS], wdw[:, bass.ds(q, 1), :].rearrange("p a t -> p (a t)")).then_inc(m["wq"], 1)
            v.tensor_copy(wq[:, TAPS:TAPS + 1], vecs[:, bass.ds(q + 4 * KT, 1)]).then_inc(m["wq"], 1)
            v.tensor_copy(dq[:, :], dvec[:, bass.ds(q * GQ, GQ)]).then_inc(m["wq"], 1)
            for h in range(2):
                dve.wait_ge(g_ready[h], q + (FT + 1))
                tt(Z[:, J - 1 + 4 * h:J + 3 + 4 * h, PAD:PAD + C], G[h][:, :].rearrange("p (b c) -> p b c", c=C),
                   PU[h][0][:, :].rearrange("p (b c) -> p b c", c=C), ALU.mult).then_inc(gu_free[h], 1)
                if h == 0:
                    split_unit(q + U_MIX, 0)
            split_pair(r + 2, 0)
            taps(q, 0, 10)
            if not first:
                gelu_in(q - 1)
            taps(q, 10, 14)
            if not first:
                gelu_out(q - 1)
            tt(dd[:, :, :], ident[0:SG, 0:SG].unsqueeze(1).to_broadcast([SG, GQ, SG]),
               dq[:, :].unsqueeze(2).to_broadcast([SG, GQ, SG]), ALU.mult).then_inc(m["dd"], 1)
            dve.wait_ge(m["dd"], q + 1)
            dve.wait_ge(m["k_sb"], q * 2 + 2)
            tt(KK[0:SG, :, 0:SG], KK[0:SG, :, 0:SG], dd[:, :, :], ALU.add).then_inc(m["k_d"], 1)
            taps(q, 14, 22)
            n = 0

            def step(ins):
                nonlocal n
                ins.then_inc(m["chain"], 1)
                n += 1
                dve.wait_ge(m["chain"], q * ROT + n)

            dve.wait_ge(m["delta"], q + 1)
            dve.wait_ge(m["rot_ld"], q * 16 + 16)
            t0, t1, t2 = TMP[:, 0, :], TMP[:, 1, :], TMP[:, 2, :]
            step(tt(t0, PD[2][:, :], COS, ALU.mult))
            step(tt(t1, PD[3][:, :], SIN, ALU.mult))
            step(tt(t0, t0, t1, ALU.add))
            step(tt(t1, PD[3][:, :], COS, ALU.mult))
            step(tt(t2, PD[2][:, :], SIN, ALU.mult))
            step(tt(t1, t1, t2, ALU.subtract))
            for t_ in (t0, t1):
                for pr in range(PR):
                    c_ = slice(pr * C, (pr + 1) * C)
                    step(v.tensor_tensor_scan(t_[:, c_], M8q[:, pr:pr + 1].to_broadcast([P, C]), t_[:, c_], 0.0,
                                              ALU.mult, ALU.add))
            sre, sim = S[:, 0, :, 1:C + 1], S[:, 1, :, 1:C + 1]
            b3 = lambda ap: ap.rearrange("p (r c) -> p r c", c=C)
            if first:
                dve.wait_ge(m["s_zero"], 1)
            else:
                dve.wait_ge(m["y_full"], q)
            step(tt(t2, t0, COS, ALU.mult))
            step(tt(sre, b3(t1), b3(SIN), ALU.mult))
            step(tt(sre, b3(t2), sre, ALU.subtract))
            step(tt(t2, t0, SIN, ALU.mult))
            step(tt(t0, t1, COS, ALU.mult))
            step(tt(sim, b3(t2), b3(t0), ALU.add))
            assert n == ROT
            v.tensor_copy(t2[:, 0:1], t2[:, 0:1]).then_inc(m["rot"], 1)
            taps(q, 22, TAPS)
            split_pair(r + 3, 1)

        mix(0, True)
        with dve.Fori(1, KT) as q:
            mix(q, False)
        gelu_in(KT - 1)
        gelu_out(KT - 1)

        def split_h(src, hi, lo):
            for k in range(KT):
                dve.wait_ge(hi, k + 1)
                tt(Hlo[:, k, :], src(k), f32(Hhi[:, k, :]), ALU.subtract).then_inc(lo, 1)

        split_h(lambda k: glb[k % 2], b_["gl_hi"], b_["gl_lo"])
        with dve.Fori(0, KT // 2) as i:
            for s in range(2):
                for h in range(2):
                    dve.wait_ge(g_ready[h], i * 2 + (FT + KT + s + 1))
                    tt(G[h][:, :], G[h][:, :], PU[h][0][:, :], ALU.mult).then_inc(gu_free[h], 1)
                    dve.wait_ge(gu_free[h], i * 2 + (R_GLU + s + 1))
                    dve.wait_ge(b_["ga_ld"], i * 32 + (16 * s + 16))
                    tt(G[h][:, :], G[h][:, :], GAB[:, hs[h]], ALU.mult).then_inc(b_["t"], 1)
                split_pair(i * 2 + (R_GLU + s + 2), s)
        for n in range(2 * KT):
            dve.wait_ge(l["mean"], n // KT + 1)
            xt = XT[:, n % KT, hs[n // KT]]
            tt(xt, xt, PD[n // KT][:, :], ALU.subtract).then_inc(l["cen"], 1)
        chain = Count(l["chain"])
        for h in range(2):
            dve.wait_ge(l["var"], KT * (h + 1))
            rsqrt(RS[h], PD[2 + h][:, :], LN_EPS, chain)
        for n in range(2 * KT + 1):
            if n < 2 * KT:
                xt = XT[:, n % KT, hs[n // KT]]
                tt(xt, xt, RS[n // KT], ALU.mult).then_inc(l["sum_in"], 1)
            if n:
                k, h = (n - 1) % KT, (n - 1) // KT
                xt = XT[:, k, hs[h]]
                dve.wait_ge(l["ln_sig"], n)
                ts(xt, xt, vecs[:, 5 * KT + k:5 * KT + k + 1], vecs[:, 6 * KT + k:6 * KT + k + 1], ALU.mult, ALU.add)\
                    .then_inc(l["aff"], 1)
                dve.wait_ge(l["aff"], n)
                tt(xt, xt, SQ[(n - 1) % 2], ALU.mult).then_inc(l["sig"], 1)
        split_h(lambda k: XT[:, k, :], b_["p_hi"], b_["p_lo"])
        for n in range(KT // 2):
            dve.wait_ge(b_["gb_ld"], 64 * (n + 1))
            for h in range(2):
                dve.wait_ge(gu_full[h], R_PW + n + 1)
                for a in range(2):
                    tt(XT[:, 2 * n + a, hs[h]], GBB[a][:, hs[h]], PU[h][a][:, :], ALU.mult)\
                        .then_inc(b_["m2"] if a == 0 else gu_free[h], 1)
                dve.wait_ge(b_["m2"], 2 * n + h + 1)
                dve.wait_ge(gu_free[h], R_PW + n + 1)
                for a in range(2):
                    xt = XT[:, 2 * n + a, hs[h]]
                    tt(xt, xt, MAB[a][:, hs[h]], ALU.add).then_inc(b_["m"], 1)
            split_pair(R_PW + n + 2, n % 2)
        split_h(lambda k: XT[:, k, :], b_["m_hi"], b_["m_lo"])
        for n in range(KT // 2):
            dve.wait_ge(b_["xo_ld"], 32 * (n + 1))
            for h in range(2):
                dve.wait_ge(gu_full[h], R_OUT + n + 1)
                for a in range(2):
                    tt(XT[:, 2 * n + a, hs[h]], GBB[a][:, hs[h]], PU[h][a][:, :], ALU.add)\
                        .then_inc(b_["x"] if a == 0 else gu_free[h], 1)
            split_pair(R_OUT + n + 2, n % 2)
        for h in range(2):
            dve.wait_ge(gu_free[h], R_FFN2)
        norm("nf2", 2)
        ffn(1, R_FFN2, U_FFN2, FT + 2 * KT)
        norm("nfi", 3, False)

    ctx.close()


_INS = ["x", "norm_ffn1_g", "w_ffn1_up", "w_ffn1_down", "norm_mix_g", "w_in", "ssm_a_re", "ssm_a_im", "ssm_log_dt",
        "ssm_b_re", "ssm_b_im", "ssm_c_re", "ssm_c_im", "ssm_d", "w_ssm_glu", "conv_dw_w", "conv_dw_b", "conv_ln_g",
        "conv_ln_b", "w_conv_pw", "w_out", "norm_ffn2_g", "w_ffn2_up", "w_ffn2_down", "norm_final_g"]


def kernel(**inputs):
    import numpy as _np
    import concourse.bacc as _bacc
    from concourse import mybir as _mybir
    from concourse.bass_utils import run_bass_kernel_spmd as _run

    nc = _bacc.Bacc("TRN2", target_bir_lowering=False, num_devices=1)
    arrays, args = {}, []
    for name in _INS:
        a = _np.ascontiguousarray(inputs[name])
        arrays[f"in_{name}"] = a
        args.append(nc.dram_tensor(f"in_{name}", a.shape, _mybir.dt.from_np(a.dtype), kind="ExternalInput").ap())
    out = nc.dram_tensor("out", (1, L, D), F32, kind="ExternalOutput").ap()
    build(nc, *args, out)
    r = _run(nc, [arrays], core_ids=[0])
    return r.results[0]["out"]
```

```python
from contextlib import ExitStack
import math

import numpy as np
import concourse.bass as bass
from concourse import mybir
from concourse.alu_op_type import AluOpType as ALU

F32 = mybir.dt.float32
F32R = mybir.dt.float32r
I32 = mybir.dt.int32
ACT = mybir.ActivationFunctionType

P = 128
D = 1024
L = 1024
KT = D // P
DFF = ((8 * D // 3 + 127) // 128) * 128
FT = DFF // P
FI = FT // 2
HW = 512
J = 8
C = L // J
SG = 16
NS = 64
NG = D // SG
GQ = P // SG
PR = GQ // 2
NP = NG // 2
TAPS = 31
PAD = 4
ZB = 2 * J - 1

RMS_EPS = 1e-6
LN_EPS = 1e-5
GELU_A = 0.044715
GELU_S = 2.0 * math.sqrt(2.0 / math.pi)
RINT = 12582912.0
RSQRT_SEED = 1597463007.0

T_BAR, T_BAI = 0, PR * J * SG
T_CAR = 2 * PR * J * SG
T_CAI = T_CAR + PR * (J + 1) * SG
T_COS = T_CAI + PR * (J + 1) * SG
T_SIN = T_COS + PR * C
T_M8 = T_SIN + PR * C
T_ALL = T_M8 + PR


def pieces(x, bits, n):
    out = []
    for _ in range(n - 1):
        e = math.floor(math.log2(abs(x)))
        s = 2.0 ** (bits - 1 - e)
        v = math.floor(abs(x) * s) / s * (1 if x > 0 else -1)
        out.append(v)
        x -= v
    out.append(float(np.float32(x)))
    return out


class Count:

    def __init__(self, sem):
        self.sem, self.n = sem, 0

    def up(self, ins, by=1):
        ins.then_inc(self.sem, by)
        self.n += by
        return self.n


def build(nc, x, norm_ffn1_g, w_ffn1_up, w_ffn1_down, norm_mix_g, w_in, ssm_a_re, ssm_a_im, ssm_log_dt,
          ssm_b_re, ssm_b_im, ssm_c_re, ssm_c_im, ssm_d, w_ssm_glu, conv_dw_w, conv_dw_b, conv_ln_g,
          conv_ln_b, w_conv_pw, w_out, norm_ffn2_g, w_ffn2_up, w_ffn2_down, norm_final_g, out):
    ctx = ExitStack()

    def sb(name, shape, dt=F32):
        return ctx.enter_context(nc.sbuf_tensor(name, shape, dt))

    def sem(name):
        return ctx.enter_context(nc.semaphore(name))

    def sems(name, n):
        return [sem(f"{name}{i}") for i in range(n)]

    def scratch(name, shape):
        return nc.dram_tensor(name, shape, F32).ap()

    d_x = scratch("d_x", [KT, P, L])
    d_tab = scratch("d_tab", [KT, P, T_ALL])
    d_u = scratch("d_u", [P, L])
    d_y = scratch("d_y", [P, L])
    d_gelu = scratch("d_gelu", [KT, P, L])
    d_conv = scratch("d_conv", [KT, P, L])
    d_ga = scratch("d_ga", [KT, P, L])
    d_gb = scratch("d_gb", [KT, P, L])
    d_ma = scratch("d_ma", [KT, P, L])

    XT = sb("XT", [P, KT, L])
    Hhi = sb("Hhi", [P, KT, L], F32R)
    Hlo = sb("Hlo", [P, KT, L], F32R)
    Wraw = sb("Wraw", [P, 2, KT, P])
    Whi = [sb(f"Whi{s}", [P, 2, KT, P], F32R) for s in range(2)]
    Wlo = [sb(f"Wlo{s}", [P, 2, KT, P], F32R) for s in range(2)]
    Draw = sb("Draw", [P, D])
    Dhi = sb("Dhi", [P, 2, D], F32R)
    Dlo = sb("Dlo", [P, 2, D], F32R)
    Ahi = sb("Ahi", [P, 2, L], F32R)
    Alo = sb("Alo", [P, 2, L], F32R)
    G = [sb(f"G{h}", [P, HW]) for h in range(2)]
    TAB = sb("TAB", [P, T_ALL])
    RT = sb("RT", [P, 2, PR, P])
    S = sb("S", [P, 2, PR, C + 1])
    TMP = sb("TMP", [P, 3, HW])
    ones = sb("ones", [P, P])
    ident = sb("ident", [P, P])
    par = sb("par", [P, 3, NP])
    vecs = sb("vecs", [P, 7 * KT])
    wdw = sb("wdw", [P, KT, TAPS])
    dvec = sb("dvec", [SG, NG])
    wq = sb("wq", [P, TAPS + 1])
    dq = sb("dq", [SG, GQ])

    xf = XT[:, :, :].rearrange("p k n -> p (k n)")
    Z = xf[:, 0:ZB * (PAD + C)].rearrange("p (b c) -> p b c", b=ZB)
    o = ZB * (PAD + C)
    CV, UY, UGf, YC, MTf, KKf = [xf[:, o + i * L:o + (i + 1) * L] for i in range(6)]
    UG = UGf.rearrange("p (g c) -> p g c", g=GQ)
    MT = MTf.rearrange("p (g n) -> p g n", g=GQ)
    KK = KKf.rearrange("p (g n) -> p g n", g=GQ)
    nrm = TAB[:, 0:6 * HW].rearrange("p (a n) -> p a n", a=6)
    SQ, RS, NV, NT = [nrm[:, 0, :], nrm[:, 1, :]], [nrm[:, 2, :], nrm[:, 3, :]], nrm[:, 4, :], nrm[:, 5, :]
    tmp12 = TAB[:, 0:12 * 8 * NP].rearrange("p (a e r) -> p a e r", a=12, e=8)
    rt = RT[:, :, :, :].rearrange("p a b c -> p (a b c)")
    sf = S[:, :, :, :].rearrange("p a b c -> p (a b c)")
    tf = TMP[:, :, :].rearrange("p a n -> p (a n)")
    prow = tf[0:NP, 0:3 * P].rearrange("r (a n) -> r a n", a=3)
    rows = tf[0:NG, 3 * P:4 * P + SG]
    ldt = tf[0:NP, 4 * P + SG:4 * P + SG + 2]
    Bb = rt.rearrange("p (a r i) -> p a r i", a=2, i=SG)
    CT = sf[:, 0:2 * NP * SG].rearrange("p (a r i) -> p a r i", a=2, i=SG)
    Cnat = [rt, sf[:, 0:L]]
    PW = tf[:, 0:2 * NP * (J + 1)].rearrange("p (a t r) -> p a t r", a=2, t=J + 1)
    E0 = 2 * NP * (J + 1)
    EE = tf[:, E0:E0 + 14 * NP].rearrange("p (a e r) -> p a e r", a=2, e=7)
    M8 = tf[:, E0 + 14 * NP:E0 + 15 * NP]
    Q0 = E0 + 15 * NP
    pwq = tf[:, Q0:Q0 + 2 * (J + 1) * PR].rearrange("p (a t r) -> p a t r", a=2, t=J + 1)
    Q0 += 2 * (J + 1) * PR
    eeq = tf[:, Q0:Q0 + 14 * PR].rearrange("p (a e r) -> p a e r", a=2, e=7)
    Q0 += 14 * PR
    bbq = tf[:, Q0:Q0 + 2 * PR * SG].rearrange("p (a r i) -> p a r i", a=2, i=SG)
    Q0 += 2 * PR * SG
    ctq = tf[:, Q0:Q0 + 2 * PR * SG].rearrange("p (a r i) -> p a r i", a=2, i=SG)
    assert Q0 + 2 * PR * SG <= 3 * HW
    tok = sb("tok", [P, 4, J])
    diag = [tf[:, 5 * P + i * P:6 * P + i * P] for i in range(2)]
    frfi = sb("frfi", [P, 2, NP])
    Bsc = sb("Bsc", [P, PR * C // 2])
    dd = sb("dd", [SG, GQ, SG])
    BA = TAB[:, T_BAR:T_CAR].rearrange("p (a r n) -> p a r n", a=2, n=J * SG)
    CA = TAB[:, T_CAR:T_COS].rearrange("p (a r n) -> p a r n", a=2, n=(J + 1) * SG)
    COS, SIN = TAB[:, T_COS:T_SIN], TAB[:, T_SIN:T_M8]
    M8q = TAB[:, T_M8:T_ALL]
    GAB = tf[:, 0:L]
    glb = [b[:, h * HW:(h + 1) * HW] for b in (rt, TAB, KKf) for h in range(2)]
    NB = len(glb)
    GBB = [TAB[:, L:2 * L], TAB[:, 2 * L:3 * L]]
    MAB = [rt, tf[:, 0:L]]
    SQ4 = [nrm[:, i, :] for i in range(4)]
    wflat = Wraw[:, :, :, :].rearrange("p s k n -> p (s k n)")
    fin = [wflat[:, 0:D], wflat[:, D:2 * D], Draw[:, :]]
    xs = fin + [TAB[:, 0:D], TAB[:, D:2 * D], TAB[:, 2 * D:3 * D], rt, sf[:, 0:D]]
    dwn = TAB[0:TAPS, 0:D]

    PU = [[ctx.enter_context(nc.psum_tensor(f"PU{h}{s}", [P, HW], F32)) for s in range(2)] for h in range(2)]
    PD = [ctx.enter_context(nc.psum_tensor(f"PD{b}", [P, HW], F32)) for b in range(4)]
    PUf = [PU[0][0], PU[0][1], PU[1][0], PU[1][1]]

    R_MIX = FT
    R_GLU = R_MIX + 2 * KT
    R_PW = R_GLU + KT
    R_OUT = R_PW + KT // 2
    R_FFN2 = R_OUT + KT // 2
    R_END = R_FFN2 + FT
    U_MIX, U_FFN2 = FT, FT + KT
    w_raw, w_hi, w_lo = sem("w_raw"), sem("w_hi"), sem("w_lo")
    d_raw, d_hi, d_lo = sem("d_raw"), sem("d_hi"), sem("d_lo")
    gu_full, gu_free = sems("gu_full", 2), sems("gu_free", 2)
    g_ready = sems("g_ready", 2)
    const = sem("const")
    passed = sem("passed")
    x_ld, x_full, x_evac = sems("x_ld", J), sem("x_full"), sems("x_evac", 2)
    x_sq, x_chain, x_diag = sem("x_sq"), sem("x_chain"), sem("x_diag")
    n_full, n_g, n_hi, n_lo = sem("n_full"), sem("n_g"), sem("n_hi"), sem("n_lo")
    gain_ld, gain_tr = sem("gain_ld"), sem("gain_tr")
    row_ld, row_bc, row_tr, par_in, vec_in = sem("row_ld"), sem("row_bc"), sem("row_tr"), sem("par_in"), sem("vec_in")
    c_ld, c_tr, c_in, b_ld = sem("c_ld"), sem("c_tr"), sem("c_in"), sem("b_ld")
    dw_ld, dw_tr, dw_in = sem("dw_ld"), sem("dw_tr"), sem("dw_in")
    par_chain, par_done = sem("par_chain"), sem("par_done")
    tab_chain, tab_saved = sem("tab_chain"), sem("tab_saved")
    norms = {n: {k: sem(f"{n}_{k}") for k in ("sq", "used", "chain", "hn", "hi", "lo")}
             for n in ("nmx", "nf2", "nfi")}
    a_hi, a_lo = sems("a_hi", 2), sems("a_lo", 2)
    dn_full, dn_free = sem("dn_full"), sems("dn_free", 4)
    m = {k: sem("m_" + k) for k in (
        "x_saved ba_ld ca_ld rot_ld z_rep conv cv_saved u_full0 u_full1 u_sb u_saved ug_ld rt_tr rt k_full k_sb k_d "
        "mt_ld delta rot chain y_full y_sb y_saved yc_ld gel gelu gelu_sig gelu_saved ga_w g_saved0 g_saved1 "
        "wq mt_zero s_zero gchain dd").split()}
    l = {k: sem("l_" + k) for k in (
        "ld sum_in mean cen chain sq var sig ln_sig aff").split()}
    b_ = {k: sem("b_" + k) for k in (
        "gl_hi gl_lo ga_ld t p_hi p_lo gb_ld m m2 m_hi m_lo xo_ld x fin_tr fin_sb").split()}
    gl_ld, ma_saved, out_saved = sems("gl_ld", NB), sems("ma_saved", 2), sems("out_saved", 3)
    block = ctx.enter_context(nc.Block())

    cols = lambda w: w[0].rearrange("(k p) n -> p k n", p=P)
    x_rows = x[0].rearrange("(c j) d -> j c d", j=J)
    out_rows = out[0].rearrange("(c j) d -> j c d", j=J)
    hs = [slice(0, HW), slice(HW, L)]
    f32 = lambda ap: ap.bitcast(F32)

    def wait(eng, sem_, value):
        if not isinstance(value, int) or value > 0:
            eng.wait_ge(sem_, value)

    def alone(eng):
        eng.sem_inc(passed, 1)

    @block.sync
    def _(sp):
        for j in range(6):
            sp.dma_start(xs[j], x_rows[j]).then_inc(x_ld[j], 16)

        def load_pair(src, col0, col1, raw_free):
            if raw_free is not None:
                sp.wait_ge(w_lo, raw_free)
            sp.dma_start(Wraw[:, 0], src[:, :, bass.ds(col0, P)]).then_inc(w_raw, 16)
            sp.dma_start(Wraw[:, 1], src[:, :, bass.ds(col1, P)]).then_inc(w_raw, 16)

        def load_unit(dst, src, raw_free):
            if raw_free is not None:
                sp.wait_ge(d_lo, raw_free)
                alone(sp)
            sp.dma_start(dst, src).then_inc(d_raw, 16)

        def ffn_loads(up, down, r0, u0, first):
            up, down = cols(up), down[0]
            if first:
                sp.wait_ge(n_full, 2 * 2)
                sp.wait_ge(x_sq, 2)
                load_pair(up, 0, DFF, None)
                for j in range(6, J):
                    sp.dma_start(xs[j], x_rows[j]).then_inc(x_ld[j], 16)
                sp.wait_ge(n_full, 2 * 3)
                sp.wait_ge(x_sq, 3)
                load_unit(Draw[:, :], down[0:P, :], None)
                load_pair(up, P, DFF + P, 1)
                load_unit(Draw[:, :], down[P:2 * P, :], 1)
            with sp.Fori(1 if first else 0, FI) as i:
                for s in range(2):
                    load_pair(up, i * (2 * P) + s * P, i * (2 * P) + DFF + s * P, i * 2 + (r0 + s))
                    load_unit(Draw[:, :], down[bass.ds(i * (2 * P) + s * P, P), :], i * 2 + (u0 + s))

        ffn_loads(w_ffn1_up, w_ffn1_down, 0, 0, True)
        wi = cols(w_in)
        def mix_pair(q, s):
            r = q * 2 + (R_MIX + s)
            load_pair(wi, q * P + (1 + 2 * s) * D, q * P + (2 + 2 * s) * D, r)

        def mix_unit(q):
            load_unit(Draw[:, :].rearrange("p (k n) -> p k n", n=P), wi[:, :, bass.ds(q * P, P)], q + U_MIX)

        def glu_pair(p, r):
            load_pair(cols(w_ssm_glu), p * P, p * P + D, r)

        mix_pair(0, 0)
        mix_unit(0)
        mix_pair(0, 1)
        for b in range(4):
            sp.wait_ge(dn_free[b], 4 * FI)
        for h in range(2):
            sp.dma_start(d_x[:, :, hs[h]].rearrange("k p n -> p k n"), XT[:, :, hs[h]]).then_inc(m["x_saved"], 16)

        sp.wait_ge(tab_saved, 16 * KT)
        sp.wait_ge(norms["nmx"]["lo"], 2 * KT)
        sp.dma_start(TAB[:, 0:T_CAR], d_tab[0, :, 0:T_CAR]).then_inc(m["ba_ld"], 16)

        def y_roundtrip(q):
            sp.wait_ge(m["y_sb"], q * 2 + 2)
            dst = d_y.rearrange("(g o) (t c) -> t o g c", g=GQ, t=J)
            for t in range(J):
                sp.dma_start(dst[t], UY[t * SG:(t + 1) * SG, :].rearrange("p (g c) -> p g c", g=GQ))\
                  .then_inc(m["y_saved"], 16)
            sp.wait_ge(m["y_saved"], q * (16 * J) + 16 * J)
            alone(sp)
            wait(sp, m["gelu_saved"], q * 16)
            alone(sp)
            sp.dma_start(YC, d_y).then_inc(m["yc_ld"], 16)

        def gelu_store(q):
            sp.wait_ge(m["gelu"], q * 2 + 2)
            sp.dma_start(d_gelu[q] if isinstance(q, int) else d_gelu[bass.ds(q, 1)].rearrange("a p n -> (a p) n"), YC)\
              .then_inc(m["gelu_saved"], 16)

        def tile_of(t, q):
            return t[q] if isinstance(q, int) else t[bass.ds(q, 1)].rearrange("a p n -> (a p) n")

        def mix_loads(q, first, last):
            if last:
                glu_pair(0, R_GLU)
            else:
                mix_pair(q + 1, 0)
                mix_unit(q + 1)
            if not first:
                sp.wait_ge(m["rot"], q)
            sp.dma_start(TAB[:, T_COS:T_ALL], tile_of(d_tab, q)[:, T_COS:T_ALL]).then_inc(m["rot_ld"], 16)
            if last:
                glu_pair(1, R_GLU + 1)
            else:
                mix_pair(q + 1, 1)
            if not first:
                sp.wait_ge(m["y_full"], q)
            sp.dma_start(TAB[:, T_CAR:T_COS], tile_of(d_tab, q)[:, T_CAR:T_COS]).then_inc(m["ca_ld"], 16)
            if not first:
                y_roundtrip(q - 1)
            sp.wait_ge(m["u_sb"], q * 2 + 2)
            sp.dma_start(d_u, UY).then_inc(m["u_saved"], 16)
            sp.wait_ge(m["u_saved"], q * 16 + 16)
            src = d_u.rearrange("(g i) (j c) -> j i g c", g=GQ, j=J)
            for jr in range(J):
                sp.dma_start(UG[jr * SG:(jr + 1) * SG], src[J - 1 - jr]).then_inc(m["ug_ld"], 16)
            if not last:
                sp.wait_ge(m["k_full"], q + 1)
                sp.dma_start(TAB[:, 0:T_CAR], tile_of(d_tab, q + 1)[:, 0:T_CAR]).then_inc(m["ba_ld"], 16)
            sp.wait_ge(m["k_d"], q + 1)
            for jr in range(J):
                j = J - 1 - jr
                sp.dma_start(MT[jr * SG:(jr + 1) * SG, :, j * SG:P], KK[0:SG, :, 0:(jr + 1) * SG])\
                  .then_inc(m["mt_ld"], 16)
            if not first:
                gelu_store(q - 1)
            for h in range(2):
                for n, dst in enumerate((d_ga, d_gb)):
                    if n == 0:
                        sp.wait_ge(m["ga_w"], q * 2 + (h + 1))
                    else:
                        sp.wait_ge(gu_free[h], q * 2 + (R_MIX + 2))
                    sp.dma_start(tile_of(dst, q)[:, hs[h]], G[n][:, :]).then_inc(m[f"g_saved{n}"], 16)
                if last and h == 0:
                    sp.wait_ge(m["gelu_saved"], 16 * (KT - 1))
                    sp.wait_ge(m["delta"], KT)
                    sp.wait_ge(m["mt_ld"], 16 * J * KT)
                    for n in range(NB):
                        gelu_load(n)
            if last:
                y_roundtrip(q)
            sp.wait_ge(m["conv"], q * TAPS + TAPS)
            sp.dma_start(tile_of(d_conv, q), CV).then_inc(m["cv_saved"], 16)

        def gelu_load(n):
            k, h = n % (KT - 1), n // (KT - 1)
            if n >= NB:
                sp.wait_ge(b_["gl_lo"], n - NB + 1)
            sp.dma_start(glb[n % NB], d_gelu[k, :, hs[h]]).then_inc(gl_ld[n % NB], 16)

        mix_loads(0, True, False)
        with sp.Fori(1, KT - 1) as q:
            mix_loads(q, False, False)
        mix_loads(KT - 1, False, True)
        for n in range(NB, 2 * (KT - 1)):
            gelu_load(n)
        sp.wait_ge(b_["gl_lo"], 2 * KT)
        sp.wait_ge(m["cv_saved"], 16 * KT)
        for h in range(2):
            sp.wait_ge(m[f"g_saved{h}"], 32 * KT)

        def glu_io(p, behind=lambda: None):
            wait(sp, b_["t"], p * 2)
            sp.dma_start(GAB, tile_of(d_ga, p)).then_inc(b_["ga_ld"], 16)
            behind()
            for h in range(2):
                sp.wait_ge(b_["t"], p * 2 + (h + 1))
                sp.dma_start(tile_of(d_ma, p)[:, hs[h]], G[h][:, :]).then_inc(ma_saved[h], 16)

        def conv_loads():
            for k in range(KT):
                sp.dma_start(XT[:, k, :], d_conv[k]).then_inc(l["ld"], 16)

        glu_pair(2, R_GLU + 2)
        glu_io(0, conv_loads)
        with sp.Fori(1, KT - 2) as p:
            glu_pair(p + 2, p + (R_GLU + 2))
            glu_io(p)
        pw, wo = cols(w_conv_pw), cols(w_out)
        for n in range(2):
            load_pair(pw, 2 * n * P, (2 * n + 1) * P, R_PW + n)
            glu_io(KT - 2 + n)
        for h in range(2):
            sp.wait_ge(ma_saved[h], 16 * KT)

        def pw_io(n):
            if n:
                sp.wait_ge(b_["m"], 4 * n)
            for a in range(2):
                sp.dma_start(GBB[a], d_gb[2 * n + a]).then_inc(b_["gb_ld"], 16)
                sp.dma_start(MAB[a], d_ma[2 * n + a]).then_inc(b_["gb_ld"], 16)

        sp.wait_ge(l["sig"], 2 * KT)
        for n in range(KT // 2):
            pw_io(n)
            if n < 2:
                load_pair(pw, 2 * (n + 2) * P, (2 * (n + 2) + 1) * P, R_PW + n + 2)
            else:
                load_pair(wo, 2 * (n - 2) * P, (2 * (n - 2) + 1) * P, R_OUT + n - 2)
        up2, down2 = cols(w_ffn2_up), w_ffn2_down[0]
        for n in range(KT // 2):
            if n == 0:
                sp.wait_ge(b_["m"], 4 * (KT // 2))
            else:
                sp.wait_ge(gu_free[1], R_OUT + n)
            for a in range(2):
                sp.dma_start(GBB[a], d_x[2 * n + a]).then_inc(b_["xo_ld"], 16)
            if n < 2:
                load_pair(wo, 2 * (n + 2) * P, (2 * (n + 2) + 1) * P, R_OUT + n + 2)
            else:
                load_pair(up2, (n - 2) * P, DFF + (n - 2) * P, R_FFN2 + n - 2)
        for s in range(2):
            load_unit(Draw[:, :], down2[s * P:(s + 1) * P, :], U_FFN2 + s)
        with sp.Fori(1, FI) as i:
            for s in range(2):
                load_pair(up2, i * (2 * P) + s * P, i * (2 * P) + DFF + s * P, i * 2 + (R_FFN2 + s))
                load_unit(Draw[:, :], down2[bass.ds(i * (2 * P) + s * P, P), :], i * 2 + (U_FFN2 + s))
        for j in range(J):
            sp.wait_ge(b_["fin_sb"], 2 * (j + 1))
            sp.dma_start(out_rows[j], fin[j % 3]).then_inc(out_saved[j % 3], 16)
        for b in range(3):
            sp.wait_ge(out_saved[b], 16 * len(range(b, J, 3)))
        sp.wait_ge(m["x_saved"], 32)
        sp.wait_ge(m["u_saved"], 16 * KT)
        sp.wait_ge(m["y_saved"], 16 * J * KT)

    @block.gpsimd
    def _(pool):
        g = nc.gpsimd
        g.memset(ones[:, :], 1.0 / D).then_inc(const, 1)
        g.memset(ident[:, :], 0.0).then_inc(const, 1)
        pool.wait_ge(const, 2)
        g.affine_select(out=ident[:, :], in_=ident[:, :], compare_op=ALU.not_equal, fill=1.0, base=0,
                        pattern=[[-1, P]], channel_multiplier=1).then_inc(const, 1)
        n = 0

        def step(ins):
            nonlocal n
            ins.then_inc(tab_chain, 1)
            n += 1
            pool.wait_ge(tab_chain, n)

        def cmul(out_re, out_im, ar, ai, br, bi, t1, t2, do):
            do(g.tensor_tensor(t1, ar, br, ALU.mult))
            do(g.tensor_tensor(t2, ai, bi, ALU.mult))
            do(g.tensor_tensor(out_re, t1, t2, ALU.subtract))
            do(g.tensor_tensor(t1, ar, bi, ALU.mult))
            do(g.tensor_tensor(t2, ai, br, ALU.mult))
            do(g.tensor_tensor(out_im, t1, t2, ALU.add))

        small = [(prow[:, 0, :], ssm_a_re[0].rearrange("(r a) p -> r (a p)", a=2)),
                 (prow[:, 1, :], ssm_a_im[0].rearrange("(r a) p -> r (a p)", a=2)),
                 (ldt[:, :], ssm_log_dt[0].rearrange("(r a) -> r a", a=2)),
                 (rows[0:NG, P:P + SG], ssm_d[0].rearrange("(g i) -> g i", i=SG))]
        vec = [norm_mix_g[0], norm_ffn2_g[0], norm_final_g, conv_dw_b[0], conv_ln_g[0], conv_ln_b[0]]
        small += [(rows[(v + 1) * KT:(v + 2) * KT, 0:P], a.rearrange("(k p) -> k p", p=P)) for v, a in enumerate(vec)]
        for dst, src in small:
            pool.dma_start(dst, src).then_inc(row_ld, 16)
        for b in range(2 * J):
            j, ks = b // 2, slice(4 * (b % 2), 4 * (b % 2) + 4)
            at = slice(j * P, (j + 1) * P)
            pool.wait_ge(n_hi, b + 1)
            g.tensor_tensor(Hlo[:, ks, at], G[b % 2][:, :].rearrange("p (k c) -> p k c", c=P), f32(Hhi[:, ks, at]),
                            ALU.subtract).then_inc(n_lo, 1)
        pool.wait_ge(n_full, 2 * J)
        pool.wait_ge(x_sq, J)
        pool.dma_start(dwn, conv_dw_w[0][:, 0, :]).then_inc(dw_ld, 16)
        for a, c in enumerate((ssm_c_re, ssm_c_im)):
            nat = Cnat[a].rearrange("p (t n) -> p t n", t=KT)
            for z in range(2):
                pool.dma_start(nat[:, :, z * NS:(z + 1) * NS], c[0].rearrange("(t g) o p -> (g o) t p", t=KT))\
                    .then_inc(c_ld, 16)
        pool.wait_ge(c_tr, 4)
        for a, b in enumerate((ssm_b_re, ssm_b_im)):
            pool.dma_start(Bb[:, a], b[0].rearrange("(r a) p i -> (a p) r i", a=2)).then_inc(b_ld, 16)
        pool.wait_ge(par_done, 1)
        pool.wait_ge(b_ld, 32)
        pool.wait_ge(c_in, 8)
        fr = frfi[:, 0, :].unsqueeze(2).to_broadcast([P, NP, SG])
        fi = frfi[:, 1, :].unsqueeze(2).to_broadcast([P, NP, SG])
        big = [TAB[:, i * NP * SG:(i + 1) * NP * SG].rearrange("p (r i) -> p r i", i=SG) for i in range(4)]
        step(g.tensor_tensor(big[0], Bb[:, 0], fr, ALU.mult))
        step(g.tensor_tensor(big[1], Bb[:, 1], fi, ALU.mult))
        step(g.tensor_tensor(big[2], Bb[:, 1], fr, ALU.mult))
        step(g.tensor_tensor(big[3], Bb[:, 0], fi, ALU.mult))
        step(g.tensor_tensor(Bb[:, 0], big[0], big[1], ALU.subtract))
        step(g.tensor_tensor(Bb[:, 1], big[2], big[3], ALU.add))
        base = n
        PER = 4 + 1 + 6 + 7 + 2 + 6 * 7

        def tile_table(q):
            n = 0

            def qstep(ins):
                nonlocal n
                ins.then_inc(tab_chain, 1)
                n += 1
                pool.wait_ge(tab_chain, q * PER + (base + n))
                if n in (17, 18, 19):
                    alone(pool)

            r4 = slice(q * PR, (q + 1) * PR) if isinstance(q, int) else bass.ds(q * PR, PR)
            qstep(g.tensor_copy(pwq, PW[:, :, :, r4]))
            qstep(g.tensor_copy(eeq, EE[:, :, :, r4]))
            qstep(g.tensor_copy(bbq, Bb[:, :, r4, :]))
            qstep(g.tensor_copy(ctq, CT[:, :, r4, :]))
            wait(pool, tab_saved, q * 16)
            qstep(g.tensor_copy(M8q, M8[:, r4]))
            pw_ = [[pwq[:, a, 0:nt, :].rearrange("p t r -> p r t").unsqueeze(3).to_broadcast([P, PR, nt, SG])
                    for a in range(2)] for nt in (J, J + 1)]

            def table(view, nt):
                return [view[:, a].rearrange("p r (t i) -> p r t i", i=SG) for a in range(2)]

            def wide(src, nt):
                return [src[:, a].unsqueeze(2).to_broadcast([P, PR, nt, SG]) for a in range(2)]

            ba, ca = table(BA, J), table(CA, J + 1)
            bw, cw = wide(bbq, J), wide(ctq, J + 1)
            sc = TAB[:, T_COS:T_COS + PR * J * SG].rearrange("p (r t i) -> p r t i", r=PR, i=SG)
            qstep(g.tensor_tensor(ba[0], pw_[0][0], bw[0], ALU.mult))
            qstep(g.tensor_tensor(sc, pw_[0][1], bw[1], ALU.mult))
            qstep(g.tensor_tensor(ba[0], ba[0], sc, ALU.subtract))
            qstep(g.tensor_tensor(ba[1], pw_[0][0], bw[1], ALU.mult))
            qstep(g.tensor_tensor(sc, pw_[0][1], bw[0], ALU.mult))
            qstep(g.tensor_tensor(ba[1], ba[1], sc, ALU.add))
            sc9 = TAB[:, T_COS:T_COS + PR * (J + 1) * SG].rearrange("p (r t i) -> p r t i", r=PR, i=SG)
            qstep(g.tensor_tensor(ca[0], pw_[1][0], cw[0], ALU.mult))
            qstep(g.tensor_tensor(sc9, pw_[1][1], cw[1], ALU.mult))
            qstep(g.tensor_tensor(ca[0], ca[0], sc9, ALU.subtract))
            qstep(g.tensor_tensor(ca[1], pw_[1][0], cw[1], ALU.mult))
            qstep(g.tensor_tensor(sc9, pw_[1][1], cw[0], ALU.mult))
            qstep(g.tensor_tensor(ca[1], ca[1], sc9, ALU.add))
            qstep(g.tensor_scalar(ca[1], ca[1], -1.0, None, ALU.mult))
            co = COS.rearrange("p (r c) -> p r c", c=C)
            si = SIN.rearrange("p (r c) -> p r c", c=C)
            qstep(g.memset(co[:, :, 0:1], 1.0))
            qstep(g.memset(si[:, :, 0:1], 0.0))
            for e in range(7):
                w = 2 ** e
                c1, s1 = [eeq[:, a, e, :].unsqueeze(2).to_broadcast([P, PR, w]) for a in range(2)]
                t1 = Bsc[:, 0:PR * w].rearrange("p (r c) -> p r c", c=w)
                c0, s0 = co[:, :, 0:w], si[:, :, 0:w]
                c2, s2 = co[:, :, w:2 * w], si[:, :, w:2 * w]
                qstep(g.tensor_tensor(c2, c0, c1, ALU.mult))
                qstep(g.tensor_tensor(t1, s0, s1, ALU.mult))
                qstep(g.tensor_tensor(c2, c2, t1, ALU.subtract))
                qstep(g.tensor_tensor(s2, s0, c1, ALU.mult))
                qstep(g.tensor_tensor(t1, c0, s1, ALU.mult))
                qstep(g.tensor_tensor(s2, s2, t1, ALU.add))
            assert n == PER, n
            pool.dma_start(d_tab[bass.ds(q, 1)].rearrange("a p n -> (a p) n"), TAB[:, :]).then_inc(tab_saved, 16)

        tile_table(0)
        with pool.Fori(1, KT) as q:
            tile_table(q)
        pool.wait_ge(tab_saved, 16 * KT)

    @block.tensor
    def _(pe):
        mm, tr = nc.tensor.matmul, nc.tensor.transpose

        pe.wait_ge(const, 3)
        def x_raw(j):
            pe.wait_ge(x_ld[j], 16)
            for kh in range(2):
                b = 2 * j + kh
                if b >= 4:
                    pe.wait_ge(x_evac[kh], j - 1)
                for k in range(4):
                    last = tr(PD[b % 4][:, k * P:(k + 1) * P], xs[j][:, (4 * kh + k) * P:(4 * kh + k + 1) * P],
                              ident[:, :])
                last.then_inc(x_full, 1)

        def x_normed(j):
            pe.wait_ge(x_diag, j + 1)
            for kh in range(2):
                b = 2 * j + kh
                bank = b % 4 if j < 4 else 2 + kh
                if b == 3:
                    pe.wait_ge(vec_in, 1)
                if b >= 4:
                    pe.wait_ge(n_g, b - 3 if j < 4 else b - 1)
                for k in range(4):
                    last = mm(PUf[bank][:, k * P:(k + 1) * P], xs[j][:, (4 * kh + k) * P:(4 * kh + k + 1) * P],
                              diag[j % 2], start=True, stop=True)
                last.then_inc(n_full, 1)

        def params():
            for kh in range(2):
                pe.wait_ge(x_evac[kh], J)
            pe.wait_ge(row_ld, 16 * 10)
            pe.wait_ge(row_bc, 1)
            for v in range(3):
                tr(PD[0][:, v * NP:(v + 1) * NP], prow[:, v, :], ident[0:NP, 0:NP]).then_inc(row_tr, 1)
            tr(PD[0][:, 96:96 + 7 * KT], rows[0:7 * KT, 0:P], ident[0:7 * KT, 0:7 * KT]).then_inc(row_tr, 1)
            tr(PD[0][0:SG, 160:160 + NG], rows[0:NG, P:P + SG], ident[0:NG, 0:NG]).then_inc(row_tr, 1)
            pe.wait_ge(dw_ld, 16)
            for k in range(KT):
                tr(PD[0][:, 256 + k * TAPS:256 + (k + 1) * TAPS], dwn[:, k * P:(k + 1) * P],
                   ident[0:TAPS, 0:TAPS]).then_inc(dw_tr, 1)
            pe.wait_ge(c_ld, 64)
            for n in range(4):
                if n == 3:
                    pe.wait_ge(vec_in, 3)
                    pe.wait_ge(par_in, 1)
                    pe.wait_ge(dw_in, 1)
                for t in range(4):
                    last = tr(PD[(n + 1) % 4][:, t * P:(t + 1) * P],
                              Cnat[n // 2][:, ((n % 2) * 4 + t) * P:((n % 2) * 4 + t + 1) * P], ident[:, :])
                last.then_inc(c_tr, 1)

        def norm_sums(name, r):
            nm = norms[name]
            for h in range(2):
                pe.wait_ge(gu_free[h], r)
            for n in range(2 * KT):
                pe.wait_ge(nm["sq"], n + 1)
                mm(PU[n // KT][0][:, :], ones[:, :], SQ[n % 2], start=n % KT == 0, stop=n % KT == KT - 1)\
                  .then_inc(nm["used"], 1)

        def pair_half(r, s, h, ready, behind={}):
            if h == 0:
                pe.wait_ge(w_lo, r + 1)
            wait(pe, gu_free[h], r)
            for k in range(KT):
                pe.wait_ge(*ready(k, h))
                for side in range(2):
                    o_ = PU[h][side][:, :]
                    mm(o_, Whi[s][:, side, k, :], Hhi[:, k, hs[h]], start=k == 0, stop=False)
                    mm(o_, Whi[s][:, side, k, :], Hlo[:, k, hs[h]], start=False, stop=False)
                    last = mm(o_, Wlo[s][:, side, k, :], Hhi[:, k, hs[h]], start=False, stop=k == KT - 1)
                if k in behind:
                    behind[k]()
            last.then_inc(gu_full[h], 1)

        def ffn(n, r0, u0, ready):
            def body(i):
                for s in range(2):
                    for h in range(2):
                        peeled = isinstance(i, int)
                        pair_half(i * 2 + (r0 - n * 2 * FI + s), s, h, ready, x_last if peeled and s == h == 0 else {})
                        if peeled and s == 0 and h == 1:
                            params()
                if isinstance(i, int):
                    pe.wait_ge(c_in, 8)
                pe.wait_ge(d_lo, i * 2 + (u0 - n * 2 * FI + 2))
                for h in range(2):
                    pe.wait_ge(a_lo[h], i * 2 + 2)
                    for d in range(KT):
                        b = (8 * h + d) % 4
                        wait(pe, dn_free[b], i * 4 + (8 * h + d) // 4)
                        for s in range(2):
                            w = slice(d * P, (d + 1) * P)
                            mm(PD[b][:, :], Dhi[:, s, w], Ahi[:, s, hs[h]], start=s == 0, stop=False)
                            mm(PD[b][:, :], Dhi[:, s, w], Alo[:, s, hs[h]], start=False, stop=False)
                            last = mm(PD[b][:, :], Dlo[:, s, w], Ahi[:, s, hs[h]], start=False, stop=s == 1)
                        last.then_inc(dn_full, 1)

            if n == 0:
                body(0)
            with pe.Fori(n * FI + (n == 0), (n + 1) * FI) as i:
                body(i)

        x_raw(0)
        pe.wait_ge(gain_ld, 16)
        tr(PUf[3][:, 0:KT], rows[0:KT, 0:P], ident[0:KT, 0:KT]).then_inc(gain_tr, 1)
        for j in range(1, 5):
            x_raw(j)
            x_normed(j - 1)

        pe.wait_ge(n_g, J)

        def x_step(j):
            if j < J:
                x_raw(j)
            x_normed(j - 1)

        x_step(5)
        x_last = {0: lambda: x_step(6), 2: lambda: x_step(7), 4: lambda: x_step(8),
                  7: lambda: pe.wait_ge(n_g, 2 * J)}
        ffn(0, 0, 0, lambda k, h: (n_lo, 8 * h + 7 + k // 4))
        norm_sums("nmx", R_MIX)

        mix_ready = lambda k, h: (norms["nmx"]["lo"], KT * h + k + 1)

        def s5_outputs(q):
            pe.wait_ge(m["mt_ld"], q * (16 * J) + 16 * J)
            pe.wait_ge(m["rot"], q + 1)
            for pr in range(PR):
                o_ = [PD[2 + g2][:, pr * P:(pr + 1) * P] for g2 in range(2)]
                half = [slice(NS * g2, NS * g2 + NS) for g2 in range(2)]
                for g2 in range(2):
                    mm(o_[g2], MT[:, 2 * pr + g2, :], UG[:, 2 * pr + g2, :], start=True, stop=False)
                for a in range(2):
                    for g2 in range(2):
                        last = mm(o_[g2], CA[half[g2], a, pr, SG:(J + 1) * SG], S[half[g2], a, pr, 0:C],
                                  start=False, stop=a == 1)
            last.then_inc(m["y_full"], 1)

        def mix(q, first):
            for h in range(2):
                pair_half(q * 2 + R_MIX, 0, h, mix_ready)
            if not first:
                s5_outputs(q - 1)
            pe.wait_ge(d_lo, q + (U_MIX + 1))
            if first:
                for b in range(4):
                    pe.wait_ge(dn_free[b], 4 * FI)
            wait(pe, m["k_sb"], q * 2)
            for h in range(2):
                for k in range(KT):
                    w = slice(k * P, (k + 1) * P)
                    mm(PD[h][:, :], Dhi[:, 0, w], Hhi[:, k, hs[h]], start=k == 0, stop=False)
                    mm(PD[h][:, :], Dhi[:, 0, w], Hlo[:, k, hs[h]], start=False, stop=False)
                    last = mm(PD[h][:, :], Dlo[:, 0, w], Hhi[:, k, hs[h]], start=False, stop=k == KT - 1)
                last.then_inc(m[f"u_full{h}"], 1)
            pe.wait_ge(m["ba_ld"], q * 16 + 16)
            wait(pe, m["y_sb"], q * 2)
            for a in range(2):
                for pr in range(PR):
                    last = tr(PD[2 + a][:, pr * P:(pr + 1) * P], BA[:, a, pr, :], ident[:, :])
                last.then_inc(m["rt_tr"], 1)
            pe.wait_ge(m["ca_ld"], q * 16 + 16)
            pe.wait_ge(m["u_sb"], q * 2 + 2)
            alone(pe)
            for g2 in range(2):
                at = slice(NS * g2, NS * g2 + NS)
                for pr in range(PR):
                    for a in range(2):
                        last = mm(PD[g2][0:SG, pr * P:(pr + 1) * P], BA[at, a, pr, 0:SG], CA[at, a, pr, 0:J * SG],
                                  start=a == 0, stop=a == 1)
            last.then_inc(m["k_full"], 1)
            pair_half(q * 2 + (R_MIX + 1), 1, 0, mix_ready)
            pe.wait_ge(m["ug_ld"], q * (16 * J) + 16 * J)
            pe.wait_ge(m["rt"], q * 2 + 2)
            for g in range(GQ):
                at = slice(NS * (g % 2), NS * (g % 2) + NS)
                for a in range(2):
                    last = mm(PD[2 + a][at, (g // 2) * P:(g // 2 + 1) * P], RT[:, a, g // 2, at], UG[:, g, :],
                              start=True, stop=True)
            last.then_inc(m["delta"], 1)
            pair_half(q * 2 + (R_MIX + 1), 1, 1, mix_ready)

        mix(0, True)
        with pe.Fori(1, KT) as q:
            mix(q, False)
        s5_outputs(KT - 1)

        glu_ready = lambda k, h: (b_["gl_lo"], (KT - 1) * h + k + 1 if k < KT - 1 else 2 * (KT - 1) + 1 + h)

        def glu(i, behind=({},) * 4):
            for s in range(2):
                for h in range(2):
                    pair_half(i * 2 + (R_GLU + s), s, h, glu_ready, behind[2 * s + h])

        def ln_sums(c):
            for n in range(4 * c, 4 * c + 4):
                pe.wait_ge(l["sq"], n + 1)
                mm(PD[2 + n // KT][:, :], ones[:, :], SQ4[n % 4], start=n % KT == 0, stop=n % KT == KT - 1)\
                  .then_inc(l["var"], 1)

        glu(0)
        pe.wait_ge(l["ld"], 16 * KT)
        for h in range(2):
            for k in range(KT):
                last = mm(PD[h][:, :], ones[:, :], XT[:, k, hs[h]], start=k == 0, stop=k == KT - 1)
            last.then_inc(l["mean"], 1)
        glu(1, ({}, {2: lambda: ln_sums(0)}, {2: lambda: ln_sums(1)}, {2: lambda: ln_sums(2)}))
        glu(2, ({2: lambda: ln_sums(3)}, {}, {}, {}))
        glu(3)
        for r0, lo in ((R_PW, b_["p_lo"]), (R_OUT, b_["m_lo"])):
            for n in range(KT // 2):
                for h in range(2):
                    pair_half(r0 + n, n % 2, h, lambda k, h: (lo, KT * h + k + 1))
        norm_sums("nf2", R_FFN2)
        ffn(1, R_FFN2, U_FFN2, lambda k, h: (norms["nf2"]["lo"], KT * h + k + 1))
        norm_sums("nfi", R_END)
        for b in range(4):
            pe.wait_ge(dn_free[b], 8 * FI)
        for j in range(J):
            pe.wait_ge(norms["nfi"]["hn"], KT * (j // 4 + 1))
            for kh in range(2):
                n = 2 * j + kh
                if n >= 4:
                    pe.wait_ge(b_["fin_sb"], n - 3)
                for k in range(4):
                    last = tr(PD[n % 4][:, k * P:(k + 1) * P], XT[:, 4 * kh + k, j * P:(j + 1) * P], ident[:, :])
                last.then_inc(b_["fin_tr"], 1)

    @block.scalar
    def _(act):
        fn = nc.scalar.activation

        act.dma_start(rows[0:KT, 0:P], norm_ffn1_g[0].rearrange("(k p) -> k p", p=P)).then_inc(gain_ld, 16)

        def x_square(j):
            act.wait_ge(x_ld[j], 16)
            if j:
                act.wait_ge(x_sq, j)
            fn(Ahi[:, 0, :], xs[j], ACT.Square, accum_out=tok[:, 0, j:j + 1]).then_inc(x_sq, 1)

        def x_step(j):
            if j < J:
                act.wait_ge(x_full, 2 * j + 1)
                fn(XT[:, 0:4, j * P:(j + 1) * P], PD[2 * j % 4][:, :].rearrange("p (k c) -> p k c", c=P), ACT.Copy)\
                    .then_inc(x_evac[0], 1)
            if j == 0:
                act.wait_ge(gain_tr, 1)
                fn(vecs[:, 0:KT], PUf[3][:, 0:KT], ACT.Copy).then_inc(vec_in, 1)
            if j + 2 < J:
                x_square(j + 2)
            if j:
                for kh in range(2):
                    act.wait_ge(n_g, 2 * (j - 1) + kh + 1)
                    fn(Hhi[:, 4 * kh:4 * kh + 4, (j - 1) * P:j * P], G[kh][:, :].rearrange("p (k c) -> p k c", c=P),
                       ACT.Copy).then_inc(n_hi, 1)

        def params():
            act.wait_ge(row_tr, 5)
            act.wait_ge(dw_tr, KT)
            fn(par[:, :, :].rearrange("p a r -> p (a r)"), PD[0][:, 0:96], ACT.Copy).then_inc(par_in, 1)
            fn(vecs[:, KT:7 * KT], PD[0][:, 96 + KT:96 + 7 * KT], ACT.Copy).then_inc(vec_in, 1)
            fn(dvec[:, :], PD[0][0:SG, 160:160 + NG], ACT.Copy).then_inc(vec_in, 1)
            fn(wdw[:, :, :].rearrange("p k t -> p (k t)"), PD[0][:, 256:256 + KT * TAPS], ACT.Copy).then_inc(dw_in, 1)
            act.wait_ge(c_tr, 4)
            for n in range(4):
                v = PD[(n + 1) % 4][:, :].rearrange("p (r a i) -> p a r i", a=2, i=SG)
                for g2 in range(2):
                    at = slice(NS * g2, NS * g2 + NS)
                    fn(CT[at, n // 2, (n % 2) * 16:(n % 2) * 16 + 16, :], v[at, g2], ACT.Copy).then_inc(c_in, 1)

        def split_pair(r, s, wait_used=True):
            act.wait_ge(w_raw, r * 32 + 32)
            if wait_used:
                act.wait_ge(gu_full[1], r - 1)
            fn(Whi[s][:, :, :, :], Wraw[:, :, :, :], ACT.Copy).then_inc(w_hi, 1)

        def split_unit(u, s, used, value):
            act.wait_ge(d_raw, u * 16 + 16)
            wait(act, used, value)
            fn(Dhi[:, s, :], Draw[:, :], ACT.Copy).then_inc(d_hi, 1)

        def norm(name, xt_ready, split=True):
            nm = norms[name]
            for n in range(2 * KT):
                k, h = n % KT, n // KT
                act.wait_ge(*xt_ready(k, h))
                if n >= 2:
                    act.wait_ge(nm["used"], n - 1)
                fn(SQ[n % 2], XT[:, k, hs[h]], ACT.Square).then_inc(nm["sq"], 1)
            if split:
                for n in range(2 * KT):
                    act.wait_ge(nm["hn"], n + 1)
                    fn(Hhi[:, n % KT, hs[n // KT]], G[n % 2][:, :], ACT.Copy).then_inc(nm["hi"], 1)

        def ffn(n, r0, u0):
            act.wait_ge(norms["nf2"]["lo"] if n else n_lo, 2 * KT)

            def body(i, last):
                for s in range(2):
                    for h in range(2):
                        act.wait_ge(gu_full[h], i * 2 + (r0 - n * 2 * FI + s + 1))
                        wait(act, a_lo[h], i * 2 + s)
                        fn(G[h][:, :], PU[h][0][:, :], ACT.Silu).then_inc(g_ready[h], 1)
                        if s == 0:
                            split_unit(i * 2 + (u0 - n * 2 * FI + h), h, dn_full, i * 16)
                            if h == 1 and isinstance(i, int) and i == 0:
                                params()
                    if not last:
                        split_pair(i * 2 + (r0 - n * 2 * FI + s + 2), s)

            if n == 0:
                body(0, False)
            with act.Fori(n * FI + (n == 0), (n + 1) * FI - n) as i:
                body(i, False)
            if n:
                body(2 * FI - 1, True)

        for j in range(2):
            x_square(j)
        for j in range(5):
            x_step(j)
        split_pair(0, 0, False)
        for j in range(5, J + 1):
            x_step(j)
        split_pair(1, 1, False)
        act.wait_ge(row_ld, 16 * 10)
        fn(prow[:, 2, :].rearrange("r (a p) -> r a p", a=2), ldt[:, :].unsqueeze(2).to_broadcast([NP, 2, NS]),
           ACT.Copy).then_inc(row_bc, 1)
        ffn(0, 0, 0)
        act.wait_ge(tab_saved, 16 * KT)
        norm("nmx", lambda k, h: (dn_free[(8 * h + k) % 4], 4 * (FI - 1) + (8 * h + k) // 4 + 1))

        def mix(q, first):
            r = q * 2 + R_MIX
            if first:
                act.wait_ge(norms["nmx"]["lo"], 2 * KT)
            for h in range(2):
                act.wait_ge(gu_full[h], r + 1)
                wait(act, m[f"g_saved{h}"], q * 32)
                fn(G[h][:, :], PU[h][1][:, :], ACT.Sigmoid).then_inc(g_ready[h], 1)
                if h == 0:
                    if first:
                        split_unit(q + U_MIX, 0, dn_full, 16 * FI)
                    else:
                        split_unit(q + U_MIX, 0, m["u_full1"], q)
            split_pair(r + 2, 0)
            if not first:
                act.wait_ge(m["y_full"], q)
                act.wait_ge(m["u_saved"], q * 16)
                evacuate_y()
            act.wait_ge(gu_free[0], r + 1)
            act.wait_ge(gu_free[1], r + 1)
            if first:
                act.wait_ge(m["mt_zero"], 2)
            fn(Z[:, 0:J - 1, PAD:PAD + C], Z[:, J:ZB, PAD - 1:PAD - 1 + C], ACT.Copy).then_inc(m["z_rep"], 1)
            for h in range(2):
                act.wait_ge(m[f"u_full{h}"], q + 1)
                wait(act, m["y_saved"], q * (16 * J))
                if first:
                    act.wait_ge(m["x_saved"], 32)
                fn(UY[:, hs[h]], PD[h][:, :], ACT.Copy).then_inc(m["u_sb"], 1)
            for a in range(2):
                act.wait_ge(m["rt_tr"], q * 2 + (a + 1))
                fn(RT[:, a].rearrange("p r n -> p (r n)"), PD[2 + a][:, :], ACT.Copy).then_inc(m["rt"], 1)
            act.wait_ge(m["k_full"], q + 1)
            wait(act, m["mt_ld"], q * (16 * J))
            for g2 in range(2):
                fn(KK[0:SG].rearrange("i (r a) n -> i a r n", a=2)[:, g2],
                   PD[g2][0:SG, :].rearrange("i (r n) -> i r n", n=P), ACT.Copy).then_inc(m["k_sb"], 1)
            if not first:
                gelu_sigmoid(q - 1)
            for h in range(2):
                act.wait_ge(gu_full[h], r + 2)
                for n in range(2):
                    if h == 0:
                        act.wait_ge(gu_free[n], r + 1)
                    else:
                        act.wait_ge(m[f"g_saved{n}"], q * 32 + 16)
                    fn(G[n][:, :], PU[h][n][:, :], ACT.Sigmoid).then_inc(m["ga_w"] if n == 0 else gu_free[h], 1)
            split_pair(r + 3, 1)

        def evacuate_y():
            for g2 in range(2):
                fn(UY.rearrange("p (r a c) -> p a r c", a=2, c=C)[:, g2], PD[2 + g2][:, :].rearrange("p (r c) -> p r c", c=C),
                   ACT.Copy).then_inc(m["y_sb"], 1)

        def gelu_sigmoid(q):
            for h in range(2):
                act.wait_ge(m["gel"], q * 2 + (h + 1))
                fn(TMP[:, h, :], TMP[:, h, :], ACT.Sigmoid, scale=GELU_S).then_inc(m["gelu_sig"], 1)

        mix(0, True)
        with act.Fori(1, KT) as q:
            mix(q, False)
        def gelu_hi(n):
            if n < 2 * (KT - 1):
                k, h = n % (KT - 1), n // (KT - 1)
                act.wait_ge(gl_ld[n % NB], 16 * (n // NB + 1))
                src = glb[n % NB]
            else:
                k, h = KT - 1, n - 2 * (KT - 1)
                act.wait_ge(m["gelu"], 2 * (KT - 1) + h + 1)
                src = YC[:, hs[h]]
            fn(Hhi[:, k, hs[h]], src, ACT.Copy).then_inc(b_["gl_hi"], 1)

        act.wait_ge(gu_full[0], R_GLU)
        for n in range(4):
            gelu_hi(n)
        act.wait_ge(m["y_full"], KT)
        act.wait_ge(m["u_saved"], 16 * KT)
        evacuate_y()
        for n in range(4, KT - 1):
            gelu_hi(n)
        act.wait_ge(gu_full[1], R_GLU)
        for n in range(KT - 1, KT + 1):
            gelu_hi(n)
        gelu_sigmoid(KT - 1)
        for n in range(KT + 1, 2 * KT):
            gelu_hi(n)
        for h in range(2):
            act.wait_ge(m[f"g_saved{h}"], 32 * KT)

        def glu(i, behind=lambda s, h: None):
            for s in range(2):
                for h in range(2):
                    act.wait_ge(gu_full[h], i * 2 + (R_GLU + s + 1))
                    wait(act, ma_saved[h], i * 32 + s * 16)
                    fn(G[h][:, :], PU[h][1][:, :], ACT.Sigmoid).then_inc(g_ready[h], 1)
                    if h == 1:
                        split_pair(i * 2 + (R_GLU + s + 2), s)
                    behind(s, h)

        def ln_squares(s, h):
            for n in range(8 * s + 4 * h, 8 * s + 4 * h + 4):
                act.wait_ge(l["cen"], n + 1)
                if n >= 4:
                    act.wait_ge(l["var"], n - 3)
                else:
                    act.wait_ge(b_["gl_lo"], 2 * KT)
                fn(SQ4[n % 4], XT[:, n % KT, hs[n // KT]], ACT.Square).then_inc(l["sq"], 1)

        def ln_sigmoid(c):
            for n in range(4 * c, 4 * c + 4):
                k, h = n % KT, n // KT
                act.wait_ge(l["sum_in"], n + 1)
                if n >= 2:
                    act.wait_ge(l["sig"], n - 1)
                fn(SQ[n % 2], XT[:, k, hs[h]], ACT.Sigmoid, scale=vecs[:, 5 * KT + k:5 * KT + k + 1],
                   bias=vecs[:, 6 * KT + k:6 * KT + k + 1]).then_inc(l["ln_sig"], 1)

        def hi_half(h, free, ready, hi):
            act.wait_ge(gu_full[h], free)
            for k in range(KT):
                act.wait_ge(*ready(k, h))
                fn(Hhi[:, k, hs[h]], XT[:, k, hs[h]], ACT.Copy).then_inc(hi, 1)

        p_hi = lambda h: hi_half(h, R_PW, lambda k, h: (l["sig"], KT * h + k + 1), b_["p_hi"])
        m_hi = lambda h: hi_half(h, R_OUT, lambda k, h: (b_["m"], 4 * (k // 2) + 2 * h + k % 2 + 1), b_["m_hi"])

        glu(0)
        glu(1, ln_squares)
        def ln_end_2(s, h):
            if s == 1 and h == 1:
                ln_sigmoid(0)

        def ln_end_3(s, h):
            c = 2 * s + h
            if c < 3:
                ln_sigmoid(c + 1)
            if c >= 2:
                p_hi(h)

        glu(2, ln_end_2)
        glu(3, ln_end_3)
        for n in range(KT // 2):
            if n == KT // 2 - 1:
                m_hi(0)
            act.wait_ge(gu_full[1], R_PW + n + 1)
            split_pair(R_PW + n + 2, n % 2)
        m_hi(1)
        for n in range(KT // 2):
            act.wait_ge(gu_full[1], R_OUT + n + 1)
            split_pair(R_OUT + n + 2, n % 2)
        norm("nf2", lambda k, h: (gu_free[h], R_OUT + k // 2 + 1))
        ffn(1, R_FFN2, U_FFN2)
        norm("nfi", lambda k, h: (dn_free[(8 * h + k) % 4], 4 * (2 * FI - 1) + (8 * h + k) // 4 + 1), False)
        for n in range(2 * J):
            j = n // 2
            act.wait_ge(b_["fin_tr"], n + 1)
            if j >= 3:
                act.wait_ge(out_saved[j % 3], 16 * (j // 3))
            fn(fin[j % 3][:, (n % 2) * HW:(n % 2 + 1) * HW], PD[n % 4][:, :], ACT.Copy).then_inc(b_["fin_sb"], 1)

    @block.vector
    def _(dve):
        v = nc.vector
        tt, ts, stt = v.tensor_tensor, v.tensor_scalar, v.scalar_tensor_tensor

        n_par = 0

        def do(ins):
            nonlocal n_par
            ins.then_inc(par_chain, 1)
            n_par += 1
            dve.wait_ge(par_chain, n_par)

        def slot(i, e=8):
            return tmp12[:, i, 0:e, :]

        def exp(dst, src, e, t0):
            xx, k, kk, p_ = [slot(t0 + i, e) for i in range(4)]
            do(ts(xx, src, -200.0, 200.0, ALU.max, ALU.min))
            do(ts(k, xx, 1.0 / math.log(2.0), RINT, ALU.mult, ALU.add))
            do(ts(k, k, RINT, None, ALU.subtract))
            ln2 = pieces(math.log(2.0), 12, 3)
            for c in ln2:
                do(stt(xx, k, -c, xx, ALU.mult, ALU.add))
            do(ts(p_, xx, 1.0 / 5040.0, None, ALU.mult))
            for c in (1.0 / 720.0, 1.0 / 120.0, 1.0 / 24.0, 1.0 / 6.0, 0.5, 1.0):
                do(stt(p_, p_, c, xx, ALU.add, ALU.mult))
            do(ts(p_, p_, 1.0, None, ALU.add))
            do(ts(kk, k, -126.0, 127.0, ALU.max, ALU.min))
            do(tt(k, k, kk, ALU.subtract))
            do(ts(k, k, -126.0, 127.0, ALU.max, ALU.min))
            for z in (kk, k):
                do(ts(xx.bitcast(I32), z, 127.0, 8388608.0, ALU.add, ALU.mult))
                do(tt(p_, p_, xx, ALU.mult))
            do(v.tensor_copy(dst, p_))

        a_re, a_im = par[:, 0, :], par[:, 1, :]
        ang, dtr, mag = slot(11), slot(10, 2), slot(9, 2)
        one = lambda ap: ap.unsqueeze(1)
        dt = slot(8, 1)
        k_, r_, r2, sn, cs, t_, q_ = [slot(i) for i in range(7)]

        def par_dt():
            dve.wait_ge(par_in, 1)
            dve.wait_ge(dw_in, 1)
            exp(dt, one(par[:, 2, :]), 1, 0)
            do(tt(dtr[:, 0:1], dt, one(a_re), ALU.mult))
            do(ts(dtr[:, 1:2], dtr[:, 0:1], float(J), None, ALU.mult))
            do(tt(ang[:, 0:1], dt, one(a_im), ALU.mult))
            for e in range(7):
                do(ts(ang[:, e + 1:e + 2], ang[:, 0:1], float(J * 2 ** e), None, ALU.mult))

        def par_mag():
            exp(mag, dtr, 2, 0)

        def par_angles():
            do(ts(k_, ang, 2.0 / math.pi, RINT, ALU.mult, ALU.add))
            do(ts(k_, k_, RINT, None, ALU.subtract))
            do(v.tensor_copy(r_, ang))
            for c in pieces(math.pi / 2, 8, 4):
                do(stt(r_, k_, -c, r_, ALU.mult, ALU.add))
            do(tt(r2, r_, r_, ALU.mult))
            do(ts(sn, r2, -1.9515295891e-4, 8.3321608736e-3, ALU.mult, ALU.add))
            do(tt(sn, sn, r2, ALU.mult))
            do(stt(sn, sn, -1.6666654611e-1, r2, ALU.add, ALU.mult))
            do(tt(sn, sn, r_, ALU.mult))
            do(tt(sn, sn, r_, ALU.add))
            do(ts(cs, r2, 2.443315711809948e-5, -1.388731625493765e-3, ALU.mult, ALU.add))
            do(tt(cs, cs, r2, ALU.mult))
            do(stt(cs, cs, 4.166664568298827e-2, r2, ALU.add, ALU.mult))
            do(stt(cs, cs, -0.5, r2, ALU.add, ALU.mult))
            do(ts(cs, cs, 1.0, None, ALU.add))

        def par_quadrant():
            do(ts(t_, k_, 0.25, RINT, ALU.mult, ALU.add))
            do(ts(t_, t_, RINT, None, ALU.subtract))
            do(stt(k_, t_, -4.0, k_, ALU.mult, ALU.add))
            do(tt(t_, k_, k_, ALU.mult))
            do(ts(r_, t_, 4.0, -1.0, ALU.is_equal, ALU.mult))
            do(ts(r2, t_, 0.0, None, ALU.is_equal))
            do(tt(r_, r_, r2, ALU.add))
            do(ts(t_, t_, 1.0, None, ALU.is_equal))
            do(tt(k_, k_, t_, ALU.mult))
            do(tt(q_, r_, sn, ALU.mult))
            do(tt(t_, k_, cs, ALU.mult))
            do(tt(q_, q_, t_, ALU.add))
            do(tt(t_, r_, cs, ALU.mult))
            do(tt(r2, k_, sn, ALU.mult))
            do(tt(t_, t_, r2, ALU.subtract))

        def par_powers():
            do(v.tensor_copy(EE[:, 0], t_[:, 1:8]))
            do(v.tensor_copy(EE[:, 1], q_[:, 1:8]))
            do(v.tensor_copy(one(M8), mag[:, 1:2]))
            do(v.memset(PW[:, 0, 0:1], 1.0))
            do(v.memset(PW[:, 1, 0:1], 0.0))
            do(tt(PW[:, 0, 1:2], mag[:, 0:1], t_[:, 0:1], ALU.mult))
            do(tt(PW[:, 1, 1:2], mag[:, 0:1], q_[:, 0:1], ALU.mult))
            for w in (1, 2, 4):
                lo_, hi_ = slice(1, w + 1), slice(w + 1, 2 * w + 1)
                br = PW[:, 0, w:w + 1].to_broadcast([P, w, NP])
                bi = PW[:, 1, w:w + 1].to_broadcast([P, w, NP])
                t1, t2 = slot(0, w), slot(1, w)
                do(tt(t1, PW[:, 0, lo_], br, ALU.mult))
                do(tt(t2, PW[:, 1, lo_], bi, ALU.mult))
                do(tt(PW[:, 0, hi_], t1, t2, ALU.subtract))
                do(tt(t1, PW[:, 0, lo_], bi, ALU.mult))
                do(tt(t2, PW[:, 1, lo_], br, ALU.mult))
                do(tt(PW[:, 1, hi_], t1, t2, ALU.add))

        def par_factor():
            ar1, ai1 = one(a_re), one(a_im)
            nr, ni = slot(0, 1), PW[:, 1, 1:2]
            t1, t2, den = slot(1, 1), slot(2, 1), slot(3, 1)
            do(ts(nr, PW[:, 0, 1:2], -1.0, None, ALU.add))
            do(tt(t1, ar1, ar1, ALU.mult))
            do(tt(t2, ai1, ai1, ALU.mult))
            do(tt(den, t1, t2, ALU.add))
            do(v.reciprocal(den, den))
            do(tt(t1, nr, ar1, ALU.mult))
            do(tt(t2, ni, ai1, ALU.mult))
            do(tt(t1, t1, t2, ALU.add))
            do(tt(one(frfi[:, 0, :]), t1, den, ALU.mult))
            do(tt(t1, ni, ar1, ALU.mult))
            do(tt(t2, nr, ai1, ALU.mult))
            do(tt(t1, t1, t2, ALU.subtract))
            tt(one(frfi[:, 1, :]), t1, den, ALU.mult).then_inc(par_done, 1)
            dve.wait_ge(par_done, 1)


        par_steps = {0: {(1, 0): par_dt}, 1: {(0, 0): par_mag, (1, 0): par_angles},
                     2: {(0, 0): par_quadrant, (1, 0): par_powers}, 3: {(0, 0): par_factor}}

        def split_pair(r, s):
            dve.wait_ge(w_hi, r + 1)
            tt(Wlo[s][:, :, :, :], Wraw[:, :, :, :], f32(Whi[s][:, :, :, :]), ALU.subtract).then_inc(w_lo, 1)

        def split_unit(u, s):
            dve.wait_ge(d_hi, u + 1)
            tt(Dlo[:, s, :], Draw[:, :], f32(Dhi[:, s, :]), ALU.subtract).then_inc(d_lo, 1)

        def rsqrt(dst, src, eps, chain):
            def step(ins):
                dve.wait_ge(chain.sem, chain.up(ins))
            step(ts(NV, src, eps, None, ALU.add))
            step(ts(dst.bitcast(I32), NV.bitcast(I32), -0.5, RSQRT_SEED, ALU.mult, ALU.add))
            for _ in range(3):
                step(stt(NT, dst, -0.5, dst, ALU.mult, ALU.mult))
                step(tt(NT, NT, NV, ALU.mult))
                step(stt(dst, NT, 1.5, dst, ALU.add, ALU.mult))

        def norm(name, gain, split=True):
            nm = norms[name]
            chain = Count(nm["chain"])
            for h in range(2):
                dve.wait_ge(nm["used"], KT * (h + 1))
                rsqrt(RS[h], PU[h][0][:, :], RMS_EPS, chain)
                for k in range(KT + 1 if split else KT):
                    n = KT * h + k
                    if k < KT:
                        if split and n >= 2:
                            dve.wait_ge(nm["lo"], n - 1)
                        dst = G[n % 2][:, :] if split else XT[:, k, hs[h]]
                        stt(dst, XT[:, k, hs[h]], vecs[:, gain * KT + k:gain * KT + k + 1], RS[h], ALU.mult, ALU.mult)\
                            .then_inc(nm["hn"], 1)
                    if split and k >= 1:
                        dve.wait_ge(nm["hi"], n)
                        tt(Hlo[:, k - 1, hs[h]], G[(n - 1) % 2][:, :], f32(Hhi[:, k - 1, hs[h]]), ALU.subtract)\
                            .then_inc(nm["lo"], 1)

        def ffn(n, r0, u0, g0):
            def body(i, last):
                fill = par_steps.get(i, {}) if isinstance(i, int) else {}
                for s in range(2):
                    for h in range(2):
                        dve.wait_ge(g_ready[h], i * 2 + (g0 - n * 2 * FI + s + 1))
                        tt(G[h][:, :], G[h][:, :], PU[h][1][:, :], ALU.mult).then_inc(gu_free[h], 1)
                        dve.wait_ge(gu_free[h], i * 2 + (r0 - n * 2 * FI + s + 1))
                        wait(dve, dn_full, i * 16)
                        v.tensor_copy(Ahi[:, s, hs[h]], G[h][:, :]).then_inc(a_hi[h], 1)
                        dve.wait_ge(a_hi[h], i * 2 + (s + 1))
                        tt(Alo[:, s, hs[h]], G[h][:, :], f32(Ahi[:, s, hs[h]]), ALU.subtract).then_inc(a_lo[h], 1)
                        if s == 0:
                            split_unit(i * 2 + (u0 - n * 2 * FI + h), h)
                        if h == 1 and not last:
                            split_pair(i * 2 + (r0 - n * 2 * FI + s + 2), s)
                        if (s, h) in fill:
                            fill[s, h]()
                for h in range(2):
                    for d in range(KT):
                        z = 8 * h + d
                        dve.wait_ge(dn_full, i * 16 + (z + 1))
                        stt(XT[:, d, hs[h]], PD[z % 4][:, :], 0.5, XT[:, d, hs[h]], ALU.mult, ALU.add)\
                            .then_inc(dn_free[z % 4], 1)

            if n == 0:
                for i in par_steps:
                    body(i, False)
            with dve.Fori(n * FI + (0 if n else len(par_steps)), (n + 1) * FI - n) as i:
                body(i, False)
            if n:
                body(2 * FI - 1, True)

        def x_step(j):
            if j < J:
                dve.wait_ge(x_sq, j + 1)
                x_rsqrt(j)
                if j >= 2:
                    dve.wait_ge(n_full, 2 * (j - 1))
                ts(diag[j % 2], ident[:, :], tok[:, 1, j:j + 1], None, ALU.mult).then_inc(x_diag, 1)
            if j == 1:
                dve.wait_ge(vec_in, 1)
            if j:
                for kh in range(2):
                    b = 2 * (j - 1) + kh
                    dve.wait_ge(n_full, b + 1)
                    if b >= 2:
                        dve.wait_ge(n_lo, b - 1)
                    tt(G[kh][:, :].rearrange("p (k c) -> p k c", c=P),
                       PUf[b % 4 if j <= 4 else 2 + kh][:, :].rearrange("p (k c) -> p k c", c=P),
                       vecs[:, 4 * kh:4 * kh + 4].unsqueeze(2).to_broadcast([P, 4, P]), ALU.mult).then_inc(n_g, 1)
            if j < J:
                dve.wait_ge(x_full, 2 * j + 2)
                v.tensor_copy(XT[:, 4:8, j * P:(j + 1) * P], PD[(2 * j + 1) % 4][:, :].rearrange("p (k c) -> p k c", c=P))\
                    .then_inc(x_evac[1], 1)

        rows_chain = Count(x_chain)

        def x_rsqrt(j):
            def step(ins):
                dve.wait_ge(rows_chain.sem, rows_chain.up(ins))
            ss, r, nv, nt = [tok[:, i, j:j + 1] for i in range(4)]
            step(ts(nv, ss, 1.0 / D, RMS_EPS, ALU.mult, ALU.add))
            step(ts(r.bitcast(I32), nv.bitcast(I32), -0.5, RSQRT_SEED, ALU.mult, ALU.add))
            for _ in range(3):
                step(stt(nt, r, -0.5, r, ALU.mult, ALU.mult))
                step(tt(nt, nt, nv, ALU.mult))
                step(stt(r, nt, 1.5, r, ALU.add, ALU.mult))

        dve.wait_ge(const, 3)
        for j in range(5):
            x_step(j)
        split_pair(0, 0)
        for j in range(5, J + 1):
            x_step(j)
        split_pair(1, 1)
        dve.wait_ge(n_lo, 2 * J)
        for kh in range(2):
            dve.wait_ge(x_evac[kh], J)
        ffn(0, 0, 0, 0)
        norm("nmx", 1)

        dve.wait_ge(m["x_saved"], 32)
        v.memset(Z[:, :, 0:PAD], 0.0).then_inc(m["mt_zero"], 1)
        v.memset(MTf, 0.0).then_inc(m["mt_zero"], 1)
        v.memset(S[:, :, :, 0:1], 0.0).then_inc(m["s_zero"], 1)
        CVb = CV.rearrange("p (b c) -> p b c", b=J)
        ROT = 5 + 1 + 2 * PR + 6

        def taps(q, s0, s1):
            for s in range(s0, s1):
                z_ = Z[:, J - 1 - s % J:ZB - s % J, PAD - s // J:PAD - s // J + C]
                w_ = wq[:, TAPS - 1 - s:TAPS - s]
                if s == 0:
                    dve.wait_ge(m["z_rep"], q + 1)
                    dve.wait_ge(m["wq"], q * 3 + 3)
                    wait(dve, m["cv_saved"], q * 16)
                    ts(CVb, z_, w_, wq[:, TAPS:TAPS + 1], ALU.mult, ALU.add).then_inc(m["conv"], 1)
                else:
                    dve.wait_ge(m["conv"], q * TAPS + s)
                    stt(CVb, z_, w_, CVb, ALU.mult, ALU.add).then_inc(m["conv"], 1)

        def gelu_in(q):
            dve.wait_ge(m["yc_ld"], q * 16 + 16)
            for h in range(2):
                t_ = TMP[:, h, :]
                tt(t_, YC[:, hs[h]], YC[:, hs[h]], ALU.mult).then_inc(m["gchain"], 1)
                dve.wait_ge(m["gchain"], q * 4 + (2 * h + 1))
                ts(t_, t_, GELU_A, 1.0, ALU.mult, ALU.add).then_inc(m["gchain"], 1)
                dve.wait_ge(m["gchain"], q * 4 + (2 * h + 2))
                tt(t_, t_, YC[:, hs[h]], ALU.mult).then_inc(m["gel"], 1)

        def gelu_out(q):
            for h in range(2):
                dve.wait_ge(m["gelu_sig"], q * 2 + (h + 1))
                tt(YC[:, hs[h]], YC[:, hs[h]], TMP[:, h, :], ALU.mult).then_inc(m["gelu"], 1)

        def mix(q, first):
            r = q * 2 + R_MIX
            wait(dve, m["conv"], q * TAPS)
            wait(dve, m["dd"], q)
            v.tensor_copy(wq[:, 0:TAPS], wdw[:, bass.ds(q, 1), :].rearrange("p a t -> p (a t)")).then_inc(m["wq"], 1)
            v.tensor_copy(wq[:, TAPS:TAPS + 1], vecs[:, bass.ds(q + 4 * KT, 1)]).then_inc(m["wq"], 1)
            v.tensor_copy(dq[:, :], dvec[:, bass.ds(q * GQ, GQ)]).then_inc(m["wq"], 1)
            for h in range(2):
                dve.wait_ge(g_ready[h], q + (FT + 1))
                tt(Z[:, J - 1 + 4 * h:J + 3 + 4 * h, PAD:PAD + C], G[h][:, :].rearrange("p (b c) -> p b c", c=C),
                   PU[h][0][:, :].rearrange("p (b c) -> p b c", c=C), ALU.mult).then_inc(gu_free[h], 1)
                if h == 0:
                    split_unit(q + U_MIX, 0)
            split_pair(r + 2, 0)
            taps(q, 0, 10)
            if not first:
                gelu_in(q - 1)
            taps(q, 10, 14)
            if not first:
                gelu_out(q - 1)
            tt(dd[:, :, :], ident[0:SG, 0:SG].unsqueeze(1).to_broadcast([SG, GQ, SG]),
               dq[:, :].unsqueeze(2).to_broadcast([SG, GQ, SG]), ALU.mult).then_inc(m["dd"], 1)
            dve.wait_ge(m["dd"], q + 1)
            dve.wait_ge(m["k_sb"], q * 2 + 2)
            tt(KK[0:SG, :, 0:SG], KK[0:SG, :, 0:SG], dd[:, :, :], ALU.add).then_inc(m["k_d"], 1)
            taps(q, 14, 22)
            n = 0

            def step(ins):
                nonlocal n
                ins.then_inc(m["chain"], 1)
                n += 1
                dve.wait_ge(m["chain"], q * ROT + n)

            dve.wait_ge(m["delta"], q + 1)
            dve.wait_ge(m["rot_ld"], q * 16 + 16)
            t0, t1, t2 = TMP[:, 0, :], TMP[:, 1, :], TMP[:, 2, :]
            step(tt(t0, PD[2][:, :], COS, ALU.mult))
            step(tt(t1, PD[3][:, :], SIN, ALU.mult))
            step(tt(t0, t0, t1, ALU.add))
            step(tt(t1, PD[3][:, :], COS, ALU.mult))
            step(tt(t2, PD[2][:, :], SIN, ALU.mult))
            step(tt(t1, t1, t2, ALU.subtract))
            for t_ in (t0, t1):
                for pr in range(PR):
                    c_ = slice(pr * C, (pr + 1) * C)
                    step(v.tensor_tensor_scan(t_[:, c_], M8q[:, pr:pr + 1].to_broadcast([P, C]), t_[:, c_], 0.0,
                                              ALU.mult, ALU.add))
            sre, sim = S[:, 0, :, 1:C + 1], S[:, 1, :, 1:C + 1]
            b3 = lambda ap: ap.rearrange("p (r c) -> p r c", c=C)
            if first:
                dve.wait_ge(m["s_zero"], 1)
            else:
                dve.wait_ge(m["y_full"], q)
            step(tt(t2, t0, COS, ALU.mult))
            step(tt(sre, b3(t1), b3(SIN), ALU.mult))
            step(tt(sre, b3(t2), sre, ALU.subtract))
            step(tt(t2, t0, SIN, ALU.mult))
            step(tt(t0, t1, COS, ALU.mult))
            step(tt(sim, b3(t2), b3(t0), ALU.add))
            assert n == ROT
            v.tensor_copy(t2[:, 0:1], t2[:, 0:1]).then_inc(m["rot"], 1)
            taps(q, 22, TAPS)
            split_pair(r + 3, 1)

        mix(0, True)
        with dve.Fori(1, KT) as q:
            mix(q, False)
        def gelu_lo(n):
            if n < 2 * (KT - 1):
                k, h, src = n % (KT - 1), n // (KT - 1), glb[n % NB]
            else:
                k, h = KT - 1, n - 2 * (KT - 1)
                src = YC[:, hs[h]]
            dve.wait_ge(b_["gl_hi"], n + 1)
            tt(Hlo[:, k, hs[h]], src, f32(Hhi[:, k, hs[h]]), ALU.subtract).then_inc(b_["gl_lo"], 1)

        for n in range(KT - 1):
            gelu_lo(n)
        gelu_in(KT - 1)
        for n in range(KT - 1, 2 * (KT - 1)):
            if n == KT + 3:
                gelu_out(KT - 1)
            gelu_lo(n)
        for n in range(2 * (KT - 1), 2 * KT):
            gelu_lo(n)

        def glu(i, behind=lambda c: None):
            for s in range(2):
                for h in range(2):
                    dve.wait_ge(g_ready[h], i * 2 + (FT + KT + s + 1))
                    tt(G[h][:, :], G[h][:, :], PU[h][0][:, :], ALU.mult).then_inc(gu_free[h], 1)
                    dve.wait_ge(gu_free[h], i * 2 + (R_GLU + s + 1))
                    dve.wait_ge(b_["ga_ld"], i * 32 + (16 * s + 16))
                    tt(G[h][:, :], G[h][:, :], GAB[:, hs[h]], ALU.mult).then_inc(b_["t"], 1)
                    if h == 1:
                        split_pair(i * 2 + (R_GLU + s + 2), s)
                    behind(2 * s + h)

        def ln_center(c):
            for n in range(4 * c, 4 * c + 4):
                dve.wait_ge(l["mean"], n // KT + 1)
                xt = XT[:, n % KT, hs[n // KT]]
                tt(xt, xt, PD[n // KT][:, :], ALU.subtract).then_inc(l["cen"], 1)

        chain = Count(l["chain"])

        def ln_scale(c):
            for n in range(4 * c, 4 * c + 4):
                xt = XT[:, n % KT, hs[n // KT]]
                tt(xt, xt, RS[n // KT], ALU.mult).then_inc(l["sum_in"], 1)
                if n % 4:
                    ln_end(n - 1)
            ln_end(4 * c + 3)

        def ln_end(n):
            k, h = n % KT, n // KT
            xt = XT[:, k, hs[h]]
            dve.wait_ge(l["ln_sig"], n + 1)
            ts(xt, xt, vecs[:, 5 * KT + k:5 * KT + k + 1], vecs[:, 6 * KT + k:6 * KT + k + 1], ALU.mult, ALU.add)\
                .then_inc(l["aff"], 1)
            dve.wait_ge(l["aff"], n + 1)
            tt(xt, xt, SQ[n % 2], ALU.mult).then_inc(l["sig"], 1)

        def lo_half(h, hi, lo):
            for k in range(KT):
                dve.wait_ge(hi, KT * h + k + 1)
                tt(Hlo[:, k, hs[h]], XT[:, k, hs[h]], f32(Hhi[:, k, hs[h]]), ALU.subtract).then_inc(lo, 1)

        def behind_2(c):
            if c in (1, 2):
                dve.wait_ge(l["var"], 2 * KT)
                rsqrt(RS[c - 1], PD[1 + c][:, :], LN_EPS, chain)
            if c == 3:
                ln_scale(0)

        def behind_3(c):
            if c < 3:
                ln_scale(c + 1)
            if c >= 2:
                lo_half(c - 2, b_["p_hi"], b_["p_lo"])

        glu(0)
        glu(1, ln_center)
        glu(2, behind_2)
        glu(3, behind_3)
        for n in range(KT // 2):
            dve.wait_ge(b_["gb_ld"], 64 * (n + 1))
            for h in range(2):
                dve.wait_ge(gu_full[h], R_PW + n + 1)
                for a in range(2):
                    tt(XT[:, 2 * n + a, hs[h]], GBB[a][:, hs[h]], PU[h][a][:, :], ALU.mult)\
                        .then_inc(b_["m2"] if a == 0 else gu_free[h], 1)
                dve.wait_ge(b_["m2"], 2 * n + h + 1)
                dve.wait_ge(gu_free[h], R_PW + n + 1)
                for a in range(2):
                    xt = XT[:, 2 * n + a, hs[h]]
                    tt(xt, xt, MAB[a][:, hs[h]], ALU.add).then_inc(b_["m"], 1)
                if n == KT // 2 - 1:
                    lo_half(h, b_["m_hi"], b_["m_lo"])
            split_pair(R_PW + n + 2, n % 2)
        for n in range(KT // 2):
            dve.wait_ge(b_["xo_ld"], 32 * (n + 1))
            for h in range(2):
                dve.wait_ge(gu_full[h], R_OUT + n + 1)
                for a in range(2):
                    tt(XT[:, 2 * n + a, hs[h]], GBB[a][:, hs[h]], PU[h][a][:, :], ALU.add)\
                        .then_inc(b_["x"] if a == 0 else gu_free[h], 1)
            split_pair(R_OUT + n + 2, n % 2)
        for h in range(2):
            dve.wait_ge(gu_free[h], R_FFN2)
        norm("nf2", 2)
        ffn(1, R_FFN2, U_FFN2, FT + 2 * KT)
        norm("nfi", 3, False)

    ctx.close()


_INS = ["x", "norm_ffn1_g", "w_ffn1_up", "w_ffn1_down", "norm_mix_g", "w_in", "ssm_a_re", "ssm_a_im", "ssm_log_dt",
        "ssm_b_re", "ssm_b_im", "ssm_c_re", "ssm_c_im", "ssm_d", "w_ssm_glu", "conv_dw_w", "conv_dw_b", "conv_ln_g",
        "conv_ln_b", "w_conv_pw", "w_out", "norm_ffn2_g", "w_ffn2_up", "w_ffn2_down", "norm_final_g"]


def kernel(**inputs):
    import numpy as _np
    import concourse.bacc as _bacc
    from concourse import mybir as _mybir
    from concourse.bass_utils import run_bass_kernel_spmd as _run

    nc = _bacc.Bacc("TRN2", target_bir_lowering=False, num_devices=1)
    arrays, args = {}, []
    for name in _INS:
        a = _np.ascontiguousarray(inputs[name])
        arrays[f"in_{name}"] = a
        args.append(nc.dram_tensor(f"in_{name}", a.shape, _mybir.dt.from_np(a.dtype), kind="ExternalInput").ap())
    out = nc.dram_tensor("out", (1, L, D), F32, kind="ExternalOutput").ap()
    build(nc, *args, out)
    r = _run(nc, [arrays], core_ids=[0])
    return r.results[0]["out"]
```

```python
from contextlib import ExitStack
import math

import numpy as np
import concourse.bass as bass
from concourse import mybir
from concourse.alu_op_type import AluOpType as ALU

F32 = mybir.dt.float32
F32R = mybir.dt.float32r
I32 = mybir.dt.int32
ACT = mybir.ActivationFunctionType

P = 128
D = 1024
L = 1024
KT = D // P
DFF = ((8 * D // 3 + 127) // 128) * 128
FT = DFF // P
FI = FT // 2
HW = 512
J = 8
C = L // J
SG = 16
NS = 64
NG = D // SG
GQ = P // SG
PR = GQ // 2
NP = NG // 2
TAPS = 31
PAD = 4
ZB = 2 * J - 1

RMS_EPS = 1e-6
LN_EPS = 1e-5
GELU_A = 0.044715
GELU_S = 2.0 * math.sqrt(2.0 / math.pi)
RINT = 12582912.0
RSQRT_SEED = 1597463007.0

T_BAR, T_BAI = 0, PR * J * SG
T_CAR = 2 * PR * J * SG
T_CAI = T_CAR + PR * (J + 1) * SG
T_COS = T_CAI + PR * (J + 1) * SG
T_SIN = T_COS + PR * C
T_M8 = T_SIN + PR * C
T_ALL = T_M8 + PR


def pieces(x, bits, n):
    out = []
    for _ in range(n - 1):
        e = math.floor(math.log2(abs(x)))
        s = 2.0 ** (bits - 1 - e)
        v = math.floor(abs(x) * s) / s * (1 if x > 0 else -1)
        out.append(v)
        x -= v
    out.append(float(np.float32(x)))
    return out


class Count:

    def __init__(self, sem):
        self.sem, self.n = sem, 0

    def up(self, ins, by=1):
        ins.then_inc(self.sem, by)
        self.n += by
        return self.n


def build(nc, x, norm_ffn1_g, w_ffn1_up, w_ffn1_down, norm_mix_g, w_in, ssm_a_re, ssm_a_im, ssm_log_dt,
          ssm_b_re, ssm_b_im, ssm_c_re, ssm_c_im, ssm_d, w_ssm_glu, conv_dw_w, conv_dw_b, conv_ln_g,
          conv_ln_b, w_conv_pw, w_out, norm_ffn2_g, w_ffn2_up, w_ffn2_down, norm_final_g, out):
    ctx = ExitStack()

    def sb(name, shape, dt=F32):
        return ctx.enter_context(nc.sbuf_tensor(name, shape, dt))

    def sem(name):
        return ctx.enter_context(nc.semaphore(name))

    def sems(name, n):
        return [sem(f"{name}{i}") for i in range(n)]

    def scratch(name, shape):
        return nc.dram_tensor(name, shape, F32).ap()

    d_x = scratch("d_x", [KT, P, L])
    d_tab = scratch("d_tab", [KT, P, T_ALL])
    d_u = scratch("d_u", [P, L])
    d_y = scratch("d_y", [P, L])
    d_gelu = scratch("d_gelu", [KT, P, L])
    d_conv = scratch("d_conv", [KT, P, L])
    d_ga = scratch("d_ga", [KT, P, L])
    d_gb = scratch("d_gb", [KT, P, L])
    d_ma = scratch("d_ma", [KT, P, L])

    XT = sb("XT", [P, KT, L])
    Hhi = sb("Hhi", [P, KT, L], F32R)
    Hlo = sb("Hlo", [P, KT, L], F32R)
    Wraw = sb("Wraw", [P, 2, KT, P])
    Whi = [sb(f"Whi{s}", [P, 2, KT, P], F32R) for s in range(2)]
    Wlo = [sb(f"Wlo{s}", [P, 2, KT, P], F32R) for s in range(2)]
    Draw = sb("Draw", [P, D])
    Dhi = sb("Dhi", [P, 2, D], F32R)
    Dlo = sb("Dlo", [P, 2, D], F32R)
    Ahi = sb("Ahi", [P, 2, L], F32R)
    Alo = sb("Alo", [P, 2, L], F32R)
    G = [sb(f"G{h}", [P, HW]) for h in range(2)]
    TAB = sb("TAB", [P, T_ALL])
    RT = sb("RT", [P, 2, PR, P])
    S = sb("S", [P, 2, PR, C + 1])
    TMP = sb("TMP", [P, 3, HW])
    ones = sb("ones", [P, P])
    ident = sb("ident", [P, P])
    par = sb("par", [P, 3, NP])
    vecs = sb("vecs", [P, 7 * KT])
    wdw = sb("wdw", [P, KT, TAPS])
    dvec = sb("dvec", [SG, NG])
    wq = sb("wq", [P, TAPS + 1])
    dq = sb("dq", [SG, GQ])

    xf = XT[:, :, :].rearrange("p k n -> p (k n)")
    Z = xf[:, 0:ZB * (PAD + C)].rearrange("p (b c) -> p b c", b=ZB)
    o = ZB * (PAD + C)
    CV, UY, UGf, YC, MTf, KKf = [xf[:, o + i * L:o + (i + 1) * L] for i in range(6)]
    UG = UGf.rearrange("p (g c) -> p g c", g=GQ)
    MT = MTf.rearrange("p (g n) -> p g n", g=GQ)
    KK = KKf.rearrange("p (g n) -> p g n", g=GQ)
    nrm = TAB[:, 0:6 * HW].rearrange("p (a n) -> p a n", a=6)
    SQ, RS, NV, NT = [nrm[:, 0, :], nrm[:, 1, :]], [nrm[:, 2, :], nrm[:, 3, :]], nrm[:, 4, :], nrm[:, 5, :]
    NRM_ROOM = {"nmx": (RS, NV, NT)}
    tmp12 = TAB[:, 0:12 * 8 * NP].rearrange("p (a e r) -> p a e r", a=12, e=8)
    rt = RT[:, :, :, :].rearrange("p a b c -> p (a b c)")
    sf = S[:, :, :, :].rearrange("p a b c -> p (a b c)")
    tf = TMP[:, :, :].rearrange("p a n -> p (a n)")
    prow = tf[0:NP, 0:3 * P].rearrange("r (a n) -> r a n", a=3)
    rows = tf[0:NG, 3 * P:4 * P + SG]
    ldt = tf[0:NP, 4 * P + SG:4 * P + SG + 2]
    Bb = rt.rearrange("p (a r i) -> p a r i", a=2, i=SG)
    CT = sf[:, 0:2 * NP * SG].rearrange("p (a r i) -> p a r i", a=2, i=SG)
    Cnat = [rt, sf[:, 0:L]]
    PW = tf[:, 0:2 * NP * (J + 1)].rearrange("p (a t r) -> p a t r", a=2, t=J + 1)
    E0 = 2 * NP * (J + 1)
    EE = tf[:, E0:E0 + 14 * NP].rearrange("p (a e r) -> p a e r", a=2, e=7)
    M8 = tf[:, E0 + 14 * NP:E0 + 15 * NP]
    Q0 = E0 + 15 * NP
    pwq = tf[:, Q0:Q0 + 2 * (J + 1) * PR].rearrange("p (a t r) -> p a t r", a=2, t=J + 1)
    Q0 += 2 * (J + 1) * PR
    eeq = tf[:, Q0:Q0 + 14 * PR].rearrange("p (a e r) -> p a e r", a=2, e=7)
    Q0 += 14 * PR
    bbq = tf[:, Q0:Q0 + 2 * PR * SG].rearrange("p (a r i) -> p a r i", a=2, i=SG)
    Q0 += 2 * PR * SG
    ctq = tf[:, Q0:Q0 + 2 * PR * SG].rearrange("p (a r i) -> p a r i", a=2, i=SG)
    assert Q0 + 2 * PR * SG <= 3 * HW
    tok = sb("tok", [P, 5, J])
    diag = [tf[:, 5 * P + i * P:6 * P + i * P] for i in range(2)]
    frfi = sb("frfi", [P, 2, NP])
    Bsc = sb("Bsc", [P, PR * C // 2])
    dd = sb("dd", [SG, GQ, SG])
    BA = TAB[:, T_BAR:T_CAR].rearrange("p (a r n) -> p a r n", a=2, n=J * SG)
    CA = TAB[:, T_CAR:T_COS].rearrange("p (a r n) -> p a r n", a=2, n=(J + 1) * SG)
    COS, SIN = TAB[:, T_COS:T_SIN], TAB[:, T_SIN:T_M8]
    M8q = TAB[:, T_M8:T_ALL]
    NRM_ROOM["nf2"] = ([tf[:, 0:HW], tf[:, HW:L]], tf[:, L:L + HW], rt[:, 0:HW])
    GN = [G[0][:, :], G[1][:, :], rt[:, HW:L]]
    GAB = tf[:, 0:L]
    glb = [b[:, h * HW:(h + 1) * HW] for b in (TAB, KKf, rt) for h in range(2)]
    NB = len(glb)
    GBB = [TAB[:, L:2 * L], TAB[:, 2 * L:3 * L]]
    MAB = [rt, tf[:, 0:L]]
    SQ4 = [nrm[:, i, :] for i in range(4)]
    LS = [rt[:, 0:HW], rt[:, HW:L]]
    wflat = Wraw[:, :, :, :].rearrange("p s k n -> p (s k n)")
    xs = [wflat[:, 0:D], wflat[:, D:2 * D], Draw[:, :], TAB[:, 0:D], TAB[:, D:2 * D], TAB[:, 2 * D:3 * D], rt, sf[:, 0:D]]
    fin = xs
    GF = tf[:, 0:D]
    dwn = TAB[0:TAPS, 0:D]

    PU = [[ctx.enter_context(nc.psum_tensor(f"PU{h}{s}", [P, HW], F32)) for s in range(2)] for h in range(2)]
    PD = [ctx.enter_context(nc.psum_tensor(f"PD{b}", [P, HW], F32)) for b in range(4)]
    PUf = [PU[0][0], PU[0][1], PU[1][0], PU[1][1]]

    R_MIX = FT
    R_GLU = R_MIX + 2 * KT
    R_PW = R_GLU + KT
    R_OUT = R_PW + KT // 2
    R_FFN2 = R_OUT + KT // 2
    R_END = R_FFN2 + FT
    U_MIX, U_FFN2 = FT, FT + KT
    w_raw, w_hi, w_lo = sem("w_raw"), sem("w_hi"), sem("w_lo")
    d_raw, d_hi, d_lo = sem("d_raw"), sem("d_hi"), sem("d_lo")
    gu_full, gu_free = sems("gu_full", 2), sems("gu_free", 2)
    g_ready = sems("g_ready", 2)
    const = sem("const")
    passed = sem("passed")
    x_ld, x_full, x_evac = sems("x_ld", J), sem("x_full"), sems("x_evac", 2)
    x_sq, x_chain, x_diag = sem("x_sq"), sem("x_chain"), sem("x_diag")
    n_full, n_g, n_hi, n_lo = sem("n_full"), sem("n_g"), sem("n_hi"), sem("n_lo")
    gain_ld, gain_tr = sem("gain_ld"), sem("gain_tr")
    row_ld, row_bc, row_tr, par_in, vec_in = sem("row_ld"), sem("row_bc"), sem("row_tr"), sem("par_in"), sem("vec_in")
    c_ld, c_tr, c_in, b_ld = sem("c_ld"), sem("c_tr"), sem("c_in"), sem("b_ld")
    dw_ld, dw_tr, dw_in = sem("dw_ld"), sem("dw_tr"), sem("dw_in")
    par_chain, par_done = sem("par_chain"), sem("par_done")
    tab_chain, tab_saved = sem("tab_chain"), sem("tab_saved")
    norms = {n: {k: sem(f"{n}_{k}") for k in ("sq", "acc", "used", "chain", "hn", "hi", "lo")}
             for n in ("nmx", "nf2")}
    a_hi, a_lo = sems("a_hi", 2), sems("a_lo", 2)
    dn_full, dn_free = sem("dn_full"), sems("dn_free", 4)
    m = {k: sem("m_" + k) for k in (
        "x_saved ba_ld ca_ld rot_ld z_rep conv cv_saved u_full0 u_full1 u_sb u_saved ug_ld rt_tr rt k_full k_sb k_d "
        "mt_ld delta rot chain y_full y_sb y_saved yc_ld gel gelu gelu_sig gelu_saved ga_w g_saved0 g_saved1 "
        "wq mt_zero s_zero gchain dd").split()}
    l = {k: sem("l_" + k) for k in (
        "ld_early ld macc vacc sum_in mean cen chain sq var sig ln_sig aff").split()}
    b_ = {k: sem("b_" + k) for k in (
        "gl_hi gl_lo ga_ld t p_hi p_lo gb_ld m m2 m_hi m_lo xo_ld x fin_ld fin_tr fin_sb fin_sq fin_chain fin_out").split()}
    gl_ld, ma_saved, out_saved = sems("gl_ld", NB), sems("ma_saved", 2), sem("out_saved")
    block = ctx.enter_context(nc.Block())

    cols = lambda w: w[0].rearrange("(k p) n -> p k n", p=P)
    x_rows = x[0].rearrange("(c j) d -> j c d", j=J)
    out_rows = out[0].rearrange("(c j) d -> j c d", j=J)
    hs = [slice(0, HW), slice(HW, L)]
    f32 = lambda ap: ap.bitcast(F32)

    ORDER = {n: [(k, h) for h in range(2) for k in range(KT)] for n in ("nmx",)}
    ORDER["nf2"] = [(2 * p_ + a, h) for p_ in range(KT // 2) for h in range(2) for a in range(2)]

    FIN = [(b // 2, b % 2) for b in range(J)] + [(J // 2 + b % 4, b // 4) for b in range(J)]

    def added(name, n):
        return sum(k > 0 for k, h in ORDER[name][:n])

    def wait(eng, sem_, value):
        if not isinstance(value, int) or value > 0:
            eng.wait_ge(sem_, value)

    def alone(eng):
        eng.sem_inc(passed, 1)

    @block.sync
    def _(sp):
        for j in range(6):
            sp.dma_start(xs[j], x_rows[j]).then_inc(x_ld[j], 16)

        def load_pair(src, col0, col1, raw_free):
            if raw_free is not None:
                sp.wait_ge(w_lo, raw_free)
            sp.dma_start(Wraw[:, 0], src[:, :, bass.ds(col0, P)]).then_inc(w_raw, 16)
            sp.dma_start(Wraw[:, 1], src[:, :, bass.ds(col1, P)]).then_inc(w_raw, 16)

        def load_unit(dst, src, raw_free):
            if raw_free is not None:
                sp.wait_ge(d_lo, raw_free)
                alone(sp)
            sp.dma_start(dst, src).then_inc(d_raw, 16)

        def ffn_loads(up, down, r0, u0, first):
            up, down = cols(up), down[0]
            if first:
                sp.wait_ge(n_full, 2 * 2)
                sp.wait_ge(x_sq, 2)
                load_pair(up, 0, DFF, None)
                for j in range(6, J):
                    sp.dma_start(xs[j], x_rows[j]).then_inc(x_ld[j], 16)
                sp.wait_ge(n_full, 2 * 3)
                sp.wait_ge(x_sq, 3)
                load_unit(Draw[:, :], down[0:P, :], None)
                load_pair(up, P, DFF + P, 1)
                load_unit(Draw[:, :], down[P:2 * P, :], 1)
            with sp.Fori(1 if first else 0, FI) as i:
                for s in range(2):
                    load_pair(up, i * (2 * P) + s * P, i * (2 * P) + DFF + s * P, i * 2 + (r0 + s))
                    load_unit(Draw[:, :], down[bass.ds(i * (2 * P) + s * P, P), :], i * 2 + (u0 + s))

        ffn_loads(w_ffn1_up, w_ffn1_down, 0, 0, True)
        wi = cols(w_in)
        def mix_pair(q, s):
            r = q * 2 + (R_MIX + s)
            load_pair(wi, q * P + (1 + 2 * s) * D, q * P + (2 + 2 * s) * D, r)

        def mix_unit(q):
            load_unit(Draw[:, :].rearrange("p (k n) -> p k n", n=P), wi[:, :, bass.ds(q * P, P)], q + U_MIX)

        def glu_pair(p, r):
            load_pair(cols(w_ssm_glu), p * P, p * P + D, r)

        mix_pair(0, 0)
        mix_unit(0)
        mix_pair(0, 1)
        for b in range(4):
            sp.wait_ge(dn_free[b], 4 * FI)
        for h in range(2):
            sp.dma_start(d_x[:, :, hs[h]].rearrange("k p n -> p k n"), XT[:, :, hs[h]]).then_inc(m["x_saved"], 16)

        sp.wait_ge(tab_saved, 16 * KT)
        sp.wait_ge(norms["nmx"]["lo"], 2 * KT)
        sp.dma_start(TAB[:, 0:T_CAR], d_tab[0, :, 0:T_CAR]).then_inc(m["ba_ld"], 16)

        def y_roundtrip(q):
            sp.wait_ge(m["y_sb"], q * 2 + 2)
            dst = d_y.rearrange("(g o) (t c) -> t o g c", g=GQ, t=J)
            for t in range(J):
                sp.dma_start(dst[t], UY[t * SG:(t + 1) * SG, :].rearrange("p (g c) -> p g c", g=GQ))\
                  .then_inc(m["y_saved"], 16)
            sp.wait_ge(m["y_saved"], q * (16 * J) + 16 * J)
            alone(sp)
            wait(sp, m["gelu_saved"], q * 16)
            alone(sp)
            sp.dma_start(YC, d_y).then_inc(m["yc_ld"], 16)

        def gelu_store(q):
            sp.wait_ge(m["gelu"], q * 2 + 2)
            sp.dma_start(d_gelu[q] if isinstance(q, int) else d_gelu[bass.ds(q, 1)].rearrange("a p n -> (a p) n"), YC)\
              .then_inc(m["gelu_saved"], 16)

        def tile_of(t, q):
            return t[q] if isinstance(q, int) else t[bass.ds(q, 1)].rearrange("a p n -> (a p) n")

        def mix_loads(q, first, last):
            if last:
                glu_pair(0, R_GLU)
            else:
                mix_pair(q + 1, 0)
                mix_unit(q + 1)
            if not first:
                conv_store(q - 1)
                sp.wait_ge(m["rot"], q)
            sp.dma_start(TAB[:, T_COS:T_ALL], tile_of(d_tab, q)[:, T_COS:T_ALL]).then_inc(m["rot_ld"], 16)
            if last:
                glu_pair(1, R_GLU + 1)
            else:
                mix_pair(q + 1, 1)
            if not first:
                sp.wait_ge(m["y_full"], q)
            sp.dma_start(TAB[:, T_CAR:T_COS], tile_of(d_tab, q)[:, T_CAR:T_COS]).then_inc(m["ca_ld"], 16)
            if not first:
                y_roundtrip(q - 1)
            sp.wait_ge(m["u_sb"], q * 2 + 2)
            sp.dma_start(d_u, UY).then_inc(m["u_saved"], 16)
            sp.wait_ge(m["u_saved"], q * 16 + 16)
            src = d_u.rearrange("(g i) (j c) -> j i g c", g=GQ, j=J)
            for jr in range(J):
                sp.dma_start(UG[jr * SG:(jr + 1) * SG], src[J - 1 - jr]).then_inc(m["ug_ld"], 16)
            if not last:
                sp.wait_ge(m["k_full"], q + 1)
                sp.dma_start(TAB[:, 0:T_CAR], tile_of(d_tab, q + 1)[:, 0:T_CAR]).then_inc(m["ba_ld"], 16)
            if last:
                sp.wait_ge(m["k_full"], KT)
                sp.wait_ge(m["gelu_saved"], 16 * (KT - 2))
                for n in (0, 1):
                    gelu_load(n)
            sp.wait_ge(m["k_d"], q + 1)
            for jr in range(J):
                j = J - 1 - jr
                sp.dma_start(MT[jr * SG:(jr + 1) * SG, :, j * SG:P], KK[0:SG, :, 0:(jr + 1) * SG])\
                  .then_inc(m["mt_ld"], 16)
            if not first:
                gelu_store(q - 1)
            if last:
                sp.wait_ge(m["mt_ld"], 16 * J * KT)
                for n in (2, 3):
                    gelu_load(n)
            for h in range(2):
                for n, dst in enumerate((d_ga, d_gb)):
                    if n == 0:
                        sp.wait_ge(m["ga_w"], q * 2 + (h + 1))
                    else:
                        sp.wait_ge(gu_free[h], q * 2 + (R_MIX + 2))
                    sp.dma_start(tile_of(dst, q)[:, hs[h]], G[n][:, :]).then_inc(m[f"g_saved{n}"], 16)
                if last and h == 0:
                    sp.wait_ge(m["delta"], KT)
                    for n in range(4, 10):
                        gelu_load(n)
            if last:
                for n in range(10, 2 * (KT - 1)):
                    gelu_load(n)
                y_roundtrip(q)

        def conv_store(q):
            sp.wait_ge(m["conv"], q * TAPS + TAPS)
            sp.dma_start(tile_of(d_conv, q), CV).then_inc(m["cv_saved"], 16)

        def gelu_load(n):
            k, h = n % (KT - 1), n // (KT - 1)
            if n >= NB:
                sp.wait_ge(b_["gl_lo"], n - NB + 1)
            if k == KT - 2:
                sp.wait_ge(m["gelu_saved"], 16 * (KT - 1))
            sp.dma_start(glb[n % NB], d_gelu[k, :, hs[h]]).then_inc(gl_ld[n % NB], 16)

        mix_loads(0, True, False)
        with sp.Fori(1, KT - 1) as q:
            mix_loads(q, False, False)
        mix_loads(KT - 1, False, True)
        sp.wait_ge(b_["gl_lo"], 2 * KT)
        for h in range(2):
            sp.wait_ge(m[f"g_saved{h}"], 32 * KT)

        def glu_io(p, between=lambda: None):
            wait(sp, b_["t"], p * 2)
            sp.dma_start(GAB, tile_of(d_ga, p)).then_inc(b_["ga_ld"], 16)
            between()
            for h in range(2):
                sp.wait_ge(b_["t"], p * 2 + (h + 1))
                sp.dma_start(tile_of(d_ma, p)[:, hs[h]], G[h][:, :]).then_inc(ma_saved[h], 16)

        def conv_loads():
            conv_store(KT - 1)
            sp.wait_ge(m["cv_saved"], 16 * KT)
            for k in (0, 1, 2, 3, 7):
                sp.dma_start(XT[:, k, :], d_conv[k]).then_inc(l["ld"], 16)

        glu_pair(2, R_GLU + 2)
        sp.wait_ge(m["cv_saved"], 16 * (KT - 1))
        for k in (4, 5, 6):
            sp.dma_start(XT[:, k, :], d_conv[k]).then_inc(l["ld_early"], 16)
        glu_io(0)
        glu_pair(3, R_GLU + 3)
        glu_io(1, conv_loads)
        with sp.Fori(2, KT - 2) as p:
            glu_pair(p + 2, p + (R_GLU + 2))
            glu_io(p)
        pw, wo = cols(w_conv_pw), cols(w_out)
        for n in range(2):
            load_pair(pw, 2 * n * P, (2 * n + 1) * P, R_PW + n)
            glu_io(KT - 2 + n)
        for h in range(2):
            sp.wait_ge(ma_saved[h], 16 * KT)

        def pw_io(n):
            if n:
                sp.wait_ge(b_["m"], 4 * n)
            for a in range(2):
                sp.dma_start(GBB[a], d_gb[2 * n + a]).then_inc(b_["gb_ld"], 16)
                sp.dma_start(MAB[a], d_ma[2 * n + a]).then_inc(b_["gb_ld"], 16)

        sp.wait_ge(l["sig"], 2 * KT)
        for n in range(KT // 2):
            pw_io(n)
            if n < 2:
                load_pair(pw, 2 * (n + 2) * P, (2 * (n + 2) + 1) * P, R_PW + n + 2)
            else:
                load_pair(wo, 2 * (n - 2) * P, (2 * (n - 2) + 1) * P, R_OUT + n - 2)
        up2, down2 = cols(w_ffn2_up), w_ffn2_down[0]
        for n in range(KT // 2):
            if n == 0:
                sp.wait_ge(b_["m"], 4 * (KT // 2))
            else:
                sp.wait_ge(gu_free[1], R_OUT + n)
            for a in range(2):
                sp.dma_start(GBB[a], d_x[2 * n + a]).then_inc(b_["xo_ld"], 16)
            if n < 2:
                load_pair(wo, 2 * (n + 2) * P, (2 * (n + 2) + 1) * P, R_OUT + n + 2)
            else:
                load_pair(up2, (n - 2) * P, DFF + (n - 2) * P, R_FFN2 + n - 2)
        for s in range(2):
            load_unit(Draw[:, :], down2[s * P:(s + 1) * P, :], U_FFN2 + s)
        with sp.Fori(1, FI) as i:
            for s in range(2):
                load_pair(up2, i * (2 * P) + s * P, i * (2 * P) + DFF + s * P, i * 2 + (R_FFN2 + s))
                load_unit(Draw[:, :], down2[bass.ds(i * (2 * P) + s * P, P), :], i * 2 + (U_FFN2 + s))
        for j in range(J):
            sp.wait_ge(b_["fin_out"], j + 1)
            sp.dma_start(out_rows[j], fin[j]).then_inc(out_saved, 16)
        sp.wait_ge(out_saved, 16 * J)
        sp.wait_ge(m["x_saved"], 32)
        sp.wait_ge(m["u_saved"], 16 * KT)
        sp.wait_ge(m["y_saved"], 16 * J * KT)

    @block.gpsimd
    def _(pool):
        g = nc.gpsimd
        g.memset(ones[:, :], 1.0 / D).then_inc(const, 1)
        g.memset(ident[:, :], 0.0).then_inc(const, 1)
        pool.wait_ge(const, 2)
        g.affine_select(out=ident[:, :], in_=ident[:, :], compare_op=ALU.not_equal, fill=1.0, base=0,
                        pattern=[[-1, P]], channel_multiplier=1).then_inc(const, 1)
        n = 0

        def step(ins):
            nonlocal n
            ins.then_inc(tab_chain, 1)
            n += 1
            pool.wait_ge(tab_chain, n)

        def cmul(out_re, out_im, ar, ai, br, bi, t1, t2, do):
            do(g.tensor_tensor(t1, ar, br, ALU.mult))
            do(g.tensor_tensor(t2, ai, bi, ALU.mult))
            do(g.tensor_tensor(out_re, t1, t2, ALU.subtract))
            do(g.tensor_tensor(t1, ar, bi, ALU.mult))
            do(g.tensor_tensor(t2, ai, br, ALU.mult))
            do(g.tensor_tensor(out_im, t1, t2, ALU.add))

        small = [(prow[:, 0, :], ssm_a_re[0].rearrange("(r a) p -> r (a p)", a=2)),
                 (prow[:, 1, :], ssm_a_im[0].rearrange("(r a) p -> r (a p)", a=2)),
                 (ldt[:, :], ssm_log_dt[0].rearrange("(r a) -> r a", a=2)),
                 (rows[0:NG, P:P + SG], ssm_d[0].rearrange("(g i) -> g i", i=SG))]
        vec = [norm_mix_g[0], norm_ffn2_g[0], norm_final_g, conv_dw_b[0], conv_ln_g[0], conv_ln_b[0]]
        small += [(rows[(v + 1) * KT:(v + 2) * KT, 0:P], a.rearrange("(k p) -> k p", p=P)) for v, a in enumerate(vec)]
        for dst, src in small:
            pool.dma_start(dst, src).then_inc(row_ld, 16)
        for b in range(2 * J):
            j, ks = b // 2, slice(4 * (b % 2), 4 * (b % 2) + 4)
            at = slice(j * P, (j + 1) * P)
            pool.wait_ge(n_hi, b + 1)
            g.tensor_tensor(Hlo[:, ks, at], G[b % 2][:, :].rearrange("p (k c) -> p k c", c=P), f32(Hhi[:, ks, at]),
                            ALU.subtract).then_inc(n_lo, 1)
        pool.wait_ge(n_full, 2 * J)
        pool.wait_ge(x_sq, J)
        pool.dma_start(dwn, conv_dw_w[0][:, 0, :]).then_inc(dw_ld, 16)
        for a, c in enumerate((ssm_c_re, ssm_c_im)):
            nat = Cnat[a].rearrange("p (t n) -> p t n", t=KT)
            for z in range(2):
                pool.dma_start(nat[:, :, z * NS:(z + 1) * NS], c[0].rearrange("(t g) o p -> (g o) t p", t=KT))\
                    .then_inc(c_ld, 16)
        pool.wait_ge(c_tr, 4)
        for a, b in enumerate((ssm_b_re, ssm_b_im)):
            pool.dma_start(Bb[:, a], b[0].rearrange("(r a) p i -> (a p) r i", a=2)).then_inc(b_ld, 16)
        pool.wait_ge(par_done, 1)
        pool.wait_ge(b_ld, 32)
        pool.wait_ge(c_in, 8)
        fr = frfi[:, 0, :].unsqueeze(2).to_broadcast([P, NP, SG])
        fi = frfi[:, 1, :].unsqueeze(2).to_broadcast([P, NP, SG])
        big = [TAB[:, i * NP * SG:(i + 1) * NP * SG].rearrange("p (r i) -> p r i", i=SG) for i in range(4)]
        step(g.tensor_tensor(big[0], Bb[:, 0], fr, ALU.mult))
        step(g.tensor_tensor(big[1], Bb[:, 1], fi, ALU.mult))
        step(g.tensor_tensor(big[2], Bb[:, 1], fr, ALU.mult))
        step(g.tensor_tensor(big[3], Bb[:, 0], fi, ALU.mult))
        step(g.tensor_tensor(Bb[:, 0], big[0], big[1], ALU.subtract))
        step(g.tensor_tensor(Bb[:, 1], big[2], big[3], ALU.add))
        base = n
        PER = 4 + 1 + 6 + 7 + 2 + 6 * 7

        def tile_table(q):
            n = 0

            def qstep(ins):
                nonlocal n
                ins.then_inc(tab_chain, 1)
                n += 1
                pool.wait_ge(tab_chain, q * PER + (base + n))
                if n in (17, 18, 19):
                    alone(pool)

            r4 = slice(q * PR, (q + 1) * PR) if isinstance(q, int) else bass.ds(q * PR, PR)
            qstep(g.tensor_copy(pwq, PW[:, :, :, r4]))
            qstep(g.tensor_copy(eeq, EE[:, :, :, r4]))
            qstep(g.tensor_copy(bbq, Bb[:, :, r4, :]))
            qstep(g.tensor_copy(ctq, CT[:, :, r4, :]))
            wait(pool, tab_saved, q * 16)
            qstep(g.tensor_copy(M8q, M8[:, r4]))
            pw_ = [[pwq[:, a, 0:nt, :].rearrange("p t r -> p r t").unsqueeze(3).to_broadcast([P, PR, nt, SG])
                    for a in range(2)] for nt in (J, J + 1)]

            def table(view, nt):
                return [view[:, a].rearrange("p r (t i) -> p r t i", i=SG) for a in range(2)]

            def wide(src, nt):
                return [src[:, a].unsqueeze(2).to_broadcast([P, PR, nt, SG]) for a in range(2)]

            ba, ca = table(BA, J), table(CA, J + 1)
            bw, cw = wide(bbq, J), wide(ctq, J + 1)
            sc = TAB[:, T_COS:T_COS + PR * J * SG].rearrange("p (r t i) -> p r t i", r=PR, i=SG)
            qstep(g.tensor_tensor(ba[0], pw_[0][0], bw[0], ALU.mult))
            qstep(g.tensor_tensor(sc, pw_[0][1], bw[1], ALU.mult))
            qstep(g.tensor_tensor(ba[0], ba[0], sc, ALU.subtract))
            qstep(g.tensor_tensor(ba[1], pw_[0][0], bw[1], ALU.mult))
            qstep(g.tensor_tensor(sc, pw_[0][1], bw[0], ALU.mult))
            qstep(g.tensor_tensor(ba[1], ba[1], sc, ALU.add))
            sc9 = TAB[:, T_COS:T_COS + PR * (J + 1) * SG].rearrange("p (r t i) -> p r t i", r=PR, i=SG)
            qstep(g.tensor_tensor(ca[0], pw_[1][0], cw[0], ALU.mult))
            qstep(g.tensor_tensor(sc9, pw_[1][1], cw[1], ALU.mult))
            qstep(g.tensor_tensor(ca[0], ca[0], sc9, ALU.subtract))
            qstep(g.tensor_tensor(ca[1], pw_[1][0], cw[1], ALU.mult))
            qstep(g.tensor_tensor(sc9, pw_[1][1], cw[0], ALU.mult))
            qstep(g.tensor_tensor(ca[1], ca[1], sc9, ALU.add))
            qstep(g.tensor_scalar(ca[1], ca[1], -1.0, None, ALU.mult))
            co = COS.rearrange("p (r c) -> p r c", c=C)
            si = SIN.rearrange("p (r c) -> p r c", c=C)
            qstep(g.memset(co[:, :, 0:1], 1.0))
            qstep(g.memset(si[:, :, 0:1], 0.0))
            for e in range(7):
                w = 2 ** e
                c1, s1 = [eeq[:, a, e, :].unsqueeze(2).to_broadcast([P, PR, w]) for a in range(2)]
                t1 = Bsc[:, 0:PR * w].rearrange("p (r c) -> p r c", c=w)
                c0, s0 = co[:, :, 0:w], si[:, :, 0:w]
                c2, s2 = co[:, :, w:2 * w], si[:, :, w:2 * w]
                qstep(g.tensor_tensor(c2, c0, c1, ALU.mult))
                qstep(g.tensor_tensor(t1, s0, s1, ALU.mult))
                qstep(g.tensor_tensor(c2, c2, t1, ALU.subtract))
                qstep(g.tensor_tensor(s2, s0, c1, ALU.mult))
                qstep(g.tensor_tensor(t1, c0, s1, ALU.mult))
                qstep(g.tensor_tensor(s2, s2, t1, ALU.add))
            assert n == PER, n
            pool.dma_start(d_tab[bass.ds(q, 1)].rearrange("a p n -> (a p) n"), TAB[:, :]).then_inc(tab_saved, 16)

        tile_table(0)
        with pool.Fori(1, KT) as q:
            tile_table(q)
        pool.wait_ge(tab_saved, 16 * KT)

        def add_squares(name):
            for n, (k, h) in enumerate(ORDER[name]):
                if k:
                    pool.wait_ge(norms[name]["sq"], n + 1)
                    wait(pool, norms[name]["acc"], added(name, n))
                    acc = NRM_ROOM[name][0][h]
                    g.tensor_tensor(acc, acc, SQ[added(name, n) % 2], ALU.add).then_inc(norms[name]["acc"], 1)

        def lo(name):
            for n in range(2 * KT):
                at = Hlo[:, n % KT, hs[n // KT]]
                pool.wait_ge(norms[name]["hi"], n + 1)
                g.tensor_tensor(at, GN[n % 3], f32(Hhi[:, n % KT, hs[n // KT]]), ALU.subtract)\
                    .then_inc(norms[name]["lo"], 1)

        add_squares("nmx")
        lo("nmx")
        n = 0
        for ks, sem_, value in (((5, 6), l["ld_early"], 16 * 3), ((0, 1, 2, 3, 7), l["ld"], 16 * (KT - 3))):
            pool.wait_ge(sem_, value)
            for h in range(2):
                for k in ks:
                    wait(pool, l["macc"], n)
                    g.tensor_tensor(LS[h], XT[:, 4, hs[h]] if k == 5 else LS[h], XT[:, k, hs[h]], ALU.add)\
                        .then_inc(l["macc"], 1)
                    n += 1
        for n in range(2 * KT):
            if n % KT:
                pool.wait_ge(l["sq"], n + 1)
                wait(pool, l["vacc"], n - 1 - n // KT)
                g.tensor_tensor(LS[n // KT], LS[n // KT], SQ4[n % 4], ALU.add).then_inc(l["vacc"], 1)
        add_squares("nf2")
        lo("nf2")
        pool.wait_ge(norms["nf2"]["hn"], 2 * KT)
        pool.dma_start(GF, norm_final_g.partition_broadcast(P)).then_inc(b_["fin_ld"], 16)

    @block.tensor
    def _(pe):
        mm, tr = nc.tensor.matmul, nc.tensor.transpose

        pe.wait_ge(const, 3)
        def x_raw(j):
            pe.wait_ge(x_ld[j], 16)
            for kh in range(2):
                b = 2 * j + kh
                if b >= 4:
                    pe.wait_ge(x_evac[kh], j - 1)
                for k in range(4):
                    last = tr(PD[b % 4][:, k * P:(k + 1) * P], xs[j][:, (4 * kh + k) * P:(4 * kh + k + 1) * P],
                              ident[:, :])
                last.then_inc(x_full, 1)

        def x_normed(j):
            pe.wait_ge(x_diag, j + 1)
            for kh in range(2):
                b = 2 * j + kh
                bank = b % 4 if j < 4 else 2 + kh
                if b == 3:
                    pe.wait_ge(vec_in, 1)
                if b >= 4:
                    pe.wait_ge(n_g, b - 3 if j < 4 else b - 1)
                for k in range(4):
                    last = mm(PUf[bank][:, k * P:(k + 1) * P], xs[j][:, (4 * kh + k) * P:(4 * kh + k + 1) * P],
                              diag[j % 2], start=True, stop=True)
                last.then_inc(n_full, 1)

        def params():
            for kh in range(2):
                pe.wait_ge(x_evac[kh], J)
            pe.wait_ge(row_ld, 16 * 10)
            pe.wait_ge(row_bc, 1)
            for v in range(3):
                tr(PD[0][:, v * NP:(v + 1) * NP], prow[:, v, :], ident[0:NP, 0:NP]).then_inc(row_tr, 1)
            tr(PD[0][:, 96:96 + 7 * KT], rows[0:7 * KT, 0:P], ident[0:7 * KT, 0:7 * KT]).then_inc(row_tr, 1)
            tr(PD[0][0:SG, 160:160 + NG], rows[0:NG, P:P + SG], ident[0:NG, 0:NG]).then_inc(row_tr, 1)
            pe.wait_ge(dw_ld, 16)
            for k in range(KT):
                tr(PD[0][:, 256 + k * TAPS:256 + (k + 1) * TAPS], dwn[:, k * P:(k + 1) * P],
                   ident[0:TAPS, 0:TAPS]).then_inc(dw_tr, 1)
            pe.wait_ge(c_ld, 64)
            for n in range(4):
                if n == 3:
                    pe.wait_ge(vec_in, 3)
                    pe.wait_ge(par_in, 1)
                    pe.wait_ge(dw_in, 1)
                for t in range(4):
                    last = tr(PD[(n + 1) % 4][:, t * P:(t + 1) * P],
                              Cnat[n // 2][:, ((n % 2) * 4 + t) * P:((n % 2) * 4 + t + 1) * P], ident[:, :])
                last.then_inc(c_tr, 1)

        def norm_sum(name, h):
            nm = norms[name]
            last = max(n for n, (k, half) in enumerate(ORDER[name]) if half == h)
            pe.wait_ge(nm["acc"], added(name, last + 1))
            bank = PD[h] if name == "nf2" else PU[h][0]
            mm(bank[:, :], ones[:, :], NRM_ROOM[name][0][h], start=True, stop=True).then_inc(nm["used"], 1)

        def fin_block(b):
            j, kh = FIN[b]
            if b >= 4:
                pe.wait_ge(b_["fin_sq"], b - 3)
            for k in range(4):
                last = tr(PUf[b % 4][:, k * P:(k + 1) * P], XT[:, 4 * kh + k, j * P:(j + 1) * P], ident[:, :])
            last.then_inc(b_["fin_tr"], 1)

        def pair_half(r, s, h, ready, behind={}):
            pair_waits(r, h)
            pair_tiles(r, s, h, ready, range(KT), behind)

        def pair_waits(r, h):
            if h == 0:
                pe.wait_ge(w_lo, r + 1)
            wait(pe, gu_free[h], r)

        def pair_tiles(r, s, h, ready, ks, behind={}):
            for k in ks:
                pe.wait_ge(*ready(k, h))
                for side in range(2):
                    o_ = PU[h][side][:, :]
                    mm(o_, Whi[s][:, side, k, :], Hhi[:, k, hs[h]], start=k == 0, stop=False)
                    mm(o_, Whi[s][:, side, k, :], Hlo[:, k, hs[h]], start=False, stop=False)
                    last = mm(o_, Wlo[s][:, side, k, :], Hhi[:, k, hs[h]], start=False, stop=k == KT - 1)
                if k in behind:
                    behind[k]()
            if k == KT - 1:
                last.then_inc(gu_full[h], 1)

        def ffn(n, r0, u0, ready, after):
            def body(i, last=False):
                for s in range(2):
                    for h in range(2):
                        peeled = isinstance(i, int) and i == 0
                        pair_half(i * 2 + (r0 - n * 2 * FI + s), s, h, ready, x_last if peeled and s == h == 0 else {})
                        if peeled and s == 0 and h == 1:
                            params()
                if isinstance(i, int) and i == 0:
                    pe.wait_ge(c_in, 8)
                pe.wait_ge(d_lo, i * 2 + (u0 - n * 2 * FI + 2))
                for h in range(2):
                    pe.wait_ge(a_lo[h], i * 2 + 2)
                    for d in range(KT):
                        b = (8 * h + d) % 4
                        wait(pe, dn_free[b], i * 4 + (8 * h + d) // 4)
                        for s in range(2):
                            w = slice(d * P, (d + 1) * P)
                            mm(PD[b][:, :], Dhi[:, s, w], Ahi[:, s, hs[h]], start=s == 0, stop=False)
                            mm(PD[b][:, :], Dhi[:, s, w], Alo[:, s, hs[h]], start=False, stop=False)
                            mm_last = mm(PD[b][:, :], Dlo[:, s, w], Ahi[:, s, hs[h]], start=False, stop=s == 1)
                        mm_last.then_inc(dn_full, 1)
                        if last and n and h == 1 and d:
                            if d == 1:
                                for bank in range(4):
                                    pe.wait_ge(dn_free[bank], i * 4 + 2)
                                pe.wait_ge(gu_free[0], R_END)
                                pe.wait_ge(gu_free[1], R_END)
                            fin_block(d - 1)
                        if last and n == 0 and h == 1 and d == 3:
                            for side in range(2):
                                pe.wait_ge(gu_free[side], r0 + 2 * FI)
                            norm_sum(after, 0)

            if n == 0:
                body(0)
            with pe.Fori(n * FI + (n == 0), (n + 1) * FI - 1) as i:
                body(i)
            body((n + 1) * FI - 1, True)
            if n == 0:
                norm_sum(after, 1)

        x_raw(0)
        pe.wait_ge(gain_ld, 16)
        tr(PUf[3][:, 0:KT], rows[0:KT, 0:P], ident[0:KT, 0:KT]).then_inc(gain_tr, 1)
        for j in range(1, 5):
            x_raw(j)
            x_normed(j - 1)

        pe.wait_ge(n_g, J)

        def x_step(j):
            if j < J:
                x_raw(j)
            x_normed(j - 1)

        x_step(5)
        x_last = {0: lambda: x_step(6), 2: lambda: x_step(7), 4: lambda: x_step(8),
                  7: lambda: pe.wait_ge(n_g, 2 * J)}
        ffn(0, 0, 0, lambda k, h: (n_lo, 8 * h + 7 + k // 4), "nmx")

        mix_ready = lambda k, h: (norms["nmx"]["lo"], KT * h + k + 1)

        def s5_outputs(q):
            pe.wait_ge(m["mt_ld"], q * (16 * J) + 16 * J)
            pe.wait_ge(m["rot"], q + 1)
            for pr in range(PR):
                o_ = [PD[2 + g2][:, pr * P:(pr + 1) * P] for g2 in range(2)]
                half = [slice(NS * g2, NS * g2 + NS) for g2 in range(2)]
                for g2 in range(2):
                    mm(o_[g2], MT[:, 2 * pr + g2, :], UG[:, 2 * pr + g2, :], start=True, stop=False)
                for a in range(2):
                    for g2 in range(2):
                        last = mm(o_[g2], CA[half[g2], a, pr, SG:(J + 1) * SG], S[half[g2], a, pr, 0:C],
                                  start=False, stop=a == 1)
            last.then_inc(m["y_full"], 1)

        def kernel_of_chunk(q):
            pe.wait_ge(m["ca_ld"], q * 16 + 16)
            pe.wait_ge(m["u_sb"], q * 2 + 2)
            alone(pe)
            for g2 in range(2):
                at = slice(NS * g2, NS * g2 + NS)
                for pr in range(PR):
                    for a in range(2):
                        last = mm(PD[g2][0:SG, pr * P:(pr + 1) * P], BA[at, a, pr, 0:SG], CA[at, a, pr, 0:J * SG],
                                  start=a == 0, stop=a == 1)
            last.then_inc(m["k_full"], 1)

        def mix(q, first, end=False):
            for h in range(2):
                pair_half(q * 2 + R_MIX, 0, h, mix_ready)
            if not first:
                s5_outputs(q - 1)
            pe.wait_ge(d_lo, q + (U_MIX + 1))
            if first:
                for b in range(4):
                    pe.wait_ge(dn_free[b], 4 * FI)
            wait(pe, m["k_sb"], q * 2)
            for h in range(2):
                for k in range(KT):
                    w = slice(k * P, (k + 1) * P)
                    mm(PD[h][:, :], Dhi[:, 0, w], Hhi[:, k, hs[h]], start=k == 0, stop=False)
                    mm(PD[h][:, :], Dhi[:, 0, w], Hlo[:, k, hs[h]], start=False, stop=False)
                    last = mm(PD[h][:, :], Dlo[:, 0, w], Hhi[:, k, hs[h]], start=False, stop=k == KT - 1)
                last.then_inc(m[f"u_full{h}"], 1)
            pe.wait_ge(m["ba_ld"], q * 16 + 16)
            wait(pe, m["y_sb"], q * 2)
            for a in range(2):
                for pr in range(PR):
                    last = tr(PD[2 + a][:, pr * P:(pr + 1) * P], BA[:, a, pr, :], ident[:, :])
                last.then_inc(m["rt_tr"], 1)
            if end:
                kernel_of_chunk(q)
            pair_half(q * 2 + (R_MIX + 1), 1, 0, mix_ready)
            if not end:
                kernel_of_chunk(q)
            pe.wait_ge(m["ug_ld"], q * (16 * J) + 16 * J)
            pe.wait_ge(m["rt"], q * 2 + 2)
            for g in range(GQ):
                at = slice(NS * (g % 2), NS * (g % 2) + NS)
                for a in range(2):
                    last = mm(PD[2 + a][at, (g // 2) * P:(g // 2 + 1) * P], RT[:, a, g // 2, at], UG[:, g, :],
                              start=True, stop=True)
            last.then_inc(m["delta"], 1)
            pair_half(q * 2 + (R_MIX + 1), 1, 1, mix_ready)

        mix(0, True)
        with pe.Fori(1, KT - 1) as q:
            mix(q, False)
        mix(KT - 1, False, True)

        glu_ready = lambda k, h: (b_["gl_lo"], (KT - 1) * h + k + 1 if k < KT - 1 else 2 * (KT - 1) + 1 + h)

        def glu(i, behind=({},) * 4):
            for s in range(2):
                for h in range(2):
                    pair_half(i * 2 + (R_GLU + s), s, h, glu_ready, behind[2 * s + h])

        def ln_mean():
            for h in range(2):
                pe.wait_ge(l["macc"], (9, 14)[h])
                mm(PD[h][:, :], ones[:, :], LS[h], start=True, stop=True).then_inc(l["mean"], 1)

        def ln_var(h):
            pe.wait_ge(l["vacc"], (KT - 1) * (h + 1))
            mm(PD[2 + h][:, :], ones[:, :], LS[h], start=True, stop=True).then_inc(l["var"], 1)

        pair_waits(R_GLU, 0)
        pair_tiles(R_GLU, 0, 0, glu_ready, range(KT - 1))
        s5_outputs(KT - 1)
        pair_waits(R_GLU, 1)
        pair_tiles(R_GLU, 0, 1, glu_ready, range(KT - 1))
        for h in range(2):
            pair_tiles(R_GLU, 0, h, glu_ready, [KT - 1])
        for h in range(2):
            pair_half(R_GLU + 1, 1, h, glu_ready)
        glu(1, ({}, {}, {1: ln_mean}, {}))
        glu(2, ({2: lambda: ln_var(0)}, {4: lambda: ln_var(1)}, {}, {}))
        glu(3)

        for r0, lo in ((R_PW, b_["p_lo"]), (R_OUT, b_["m_lo"])):
            for n in range(KT // 2):
                for h in range(2):
                    end = r0 == R_OUT and (n, h) == (KT // 2 - 1, 1)
                    pair_half(r0 + n, n % 2, h, lambda k, h: (lo, KT * h + k + 1),
                              {3: lambda: norm_sum("nf2", 0)} if end else {})
        norm_sum("nf2", 1)
        ffn(1, R_FFN2, U_FFN2, lambda k, h: (norms["nf2"]["lo"], KT * h + k + 1), None)
        fin_block(J - 1)
        for b in range(J, 2 * J):
            for bank in range(4) if b in (J, J + 4) else ():
                pe.wait_ge(dn_free[bank], 8 * FI - (b == J))
            fin_block(b)

    @block.scalar
    def _(act):
        fn = nc.scalar.activation

        act.dma_start(rows[0:KT, 0:P], norm_ffn1_g[0].rearrange("(k p) -> k p", p=P)).then_inc(gain_ld, 16)

        def x_square(j):
            act.wait_ge(x_ld[j], 16)
            if j:
                act.wait_ge(x_sq, j)
            fn(Ahi[:, 0, :], xs[j], ACT.Square, accum_out=tok[:, 0, j:j + 1]).then_inc(x_sq, 1)

        def x_step(j):
            if j < J:
                act.wait_ge(x_full, 2 * j + 1)
                fn(XT[:, 0:4, j * P:(j + 1) * P], PD[2 * j % 4][:, :].rearrange("p (k c) -> p k c", c=P), ACT.Copy)\
                    .then_inc(x_evac[0], 1)
            if j == 0:
                act.wait_ge(gain_tr, 1)
                fn(vecs[:, 0:KT], PUf[3][:, 0:KT], ACT.Copy).then_inc(vec_in, 1)
            if j + 2 < J:
                x_square(j + 2)
            if j:
                for kh in range(2):
                    act.wait_ge(n_g, 2 * (j - 1) + kh + 1)
                    fn(Hhi[:, 4 * kh:4 * kh + 4, (j - 1) * P:j * P], G[kh][:, :].rearrange("p (k c) -> p k c", c=P),
                       ACT.Copy).then_inc(n_hi, 1)

        def params():
            act.wait_ge(row_tr, 5)
            act.wait_ge(dw_tr, KT)
            fn(par[:, :, :].rearrange("p a r -> p (a r)"), PD[0][:, 0:96], ACT.Copy).then_inc(par_in, 1)
            fn(vecs[:, KT:7 * KT], PD[0][:, 96 + KT:96 + 7 * KT], ACT.Copy).then_inc(vec_in, 1)
            fn(dvec[:, :], PD[0][0:SG, 160:160 + NG], ACT.Copy).then_inc(vec_in, 1)
            fn(wdw[:, :, :].rearrange("p k t -> p (k t)"), PD[0][:, 256:256 + KT * TAPS], ACT.Copy).then_inc(dw_in, 1)
            act.wait_ge(c_tr, 4)
            for n in range(4):
                v = PD[(n + 1) % 4][:, :].rearrange("p (r a i) -> p a r i", a=2, i=SG)
                for g2 in range(2):
                    at = slice(NS * g2, NS * g2 + NS)
                    fn(CT[at, n // 2, (n % 2) * 16:(n % 2) * 16 + 16, :], v[at, g2], ACT.Copy).then_inc(c_in, 1)

        def split_pair(r, s, wait_used=True):
            act.wait_ge(w_raw, r * 32 + 32)
            if wait_used:
                act.wait_ge(gu_full[1], r - 1)
            fn(Whi[s][:, :, :, :], Wraw[:, :, :, :], ACT.Copy).then_inc(w_hi, 1)

        def split_unit(u, s, used, value):
            act.wait_ge(d_raw, u * 16 + 16)
            wait(act, used, value)
            fn(Dhi[:, s, :], Draw[:, :], ACT.Copy).then_inc(d_hi, 1)

        def square(name, n, k, h, ready):
            act.wait_ge(*ready)
            j = added(name, n)
            if j >= 2:
                act.wait_ge(norms[name]["acc"], j - 1)
            fn(SQ[j % 2] if k else NRM_ROOM[name][0][h], XT[:, k, hs[h]], ACT.Square).then_inc(norms[name]["sq"], 1)

        def norm(name, xt_ready):
            nm = norms[name]
            if xt_ready:
                for n in range(2 * KT):
                    square(name, n, n % KT, n // KT, xt_ready(n % KT, n // KT))
            for n in range(2 * KT):
                act.wait_ge(nm["hn"], n + 1)
                fn(Hhi[:, n % KT, hs[n // KT]], GN[n % 3], ACT.Copy).then_inc(nm["hi"], 1)

        def ffn(n, r0, u0):
            act.wait_ge(norms["nf2"]["lo"] if n else n_lo, 2 * KT)

            def body(i, last):
                for s in range(2):
                    for h in range(2):
                        act.wait_ge(gu_full[h], i * 2 + (r0 - n * 2 * FI + s + 1))
                        wait(act, a_lo[h], i * 2 + s)
                        fn(G[h][:, :], PU[h][0][:, :], ACT.Silu).then_inc(g_ready[h], 1)
                        if s == 0:
                            split_unit(i * 2 + (u0 - n * 2 * FI + h), h, dn_full, i * 16)
                            if h == 1 and isinstance(i, int) and i == 0:
                                params()
                    if not last:
                        split_pair(i * 2 + (r0 - n * 2 * FI + s + 2), s)

            if n == 0:
                body(0, False)
            with act.Fori(n * FI + (n == 0), (n + 1) * FI - n) as i:
                body(i, False)
            if n:
                body(2 * FI - 1, True)

        for j in range(2):
            x_square(j)
        for j in range(5):
            x_step(j)
        split_pair(0, 0, False)
        for j in range(5, J + 1):
            x_step(j)
        split_pair(1, 1, False)
        act.wait_ge(row_ld, 16 * 10)
        fn(prow[:, 2, :].rearrange("r (a p) -> r a p", a=2), ldt[:, :].unsqueeze(2).to_broadcast([NP, 2, NS]),
           ACT.Copy).then_inc(row_bc, 1)
        ffn(0, 0, 0)
        act.wait_ge(tab_saved, 16 * KT)
        norm("nmx", lambda k, h: (dn_free[(8 * h + k) % 4], 4 * (FI - 1) + (8 * h + k) // 4 + 1))

        def gelu_hi(n):
            if n < 2 * (KT - 1):
                k, h = n % (KT - 1), n // (KT - 1)
                act.wait_ge(gl_ld[n % NB], 16 * (n // NB + 1))
                src = glb[n % NB]
            else:
                k, h = KT - 1, n - 2 * (KT - 1)
                act.wait_ge(m["gelu"], 2 * (KT - 1) + h + 1)
                src = YC[:, hs[h]]
            fn(Hhi[:, k, hs[h]], src, ACT.Copy).then_inc(b_["gl_hi"], 1)

        def kernel_of_chunk(q):
            act.wait_ge(m["k_full"], q + 1)
            wait(act, m["mt_ld"], q * (16 * J))
            for g2 in range(2):
                fn(KK[0:SG].rearrange("i (r a) n -> i a r n", a=2)[:, g2],
                   PD[g2][0:SG, :].rearrange("i (r n) -> i r n", n=P), ACT.Copy).then_inc(m["k_sb"], 1)

        def mix(q, first, last=False):
            r = q * 2 + R_MIX
            if first:
                act.wait_ge(norms["nmx"]["lo"], 2 * KT)
            for h in range(2):
                act.wait_ge(gu_full[h], r + 1)
                wait(act, m[f"g_saved{h}"], q * 32)
                fn(G[h][:, :], PU[h][1][:, :], ACT.Sigmoid).then_inc(g_ready[h], 1)
                if h == 0:
                    if first:
                        split_unit(q + U_MIX, 0, dn_full, 16 * FI)
                    else:
                        split_unit(q + U_MIX, 0, m["u_full1"], q)
            split_pair(r + 2, 0)
            if not first:
                act.wait_ge(m["y_full"], q)
                act.wait_ge(m["u_saved"], q * 16)
                evacuate_y()
            act.wait_ge(gu_free[0], r + 1)
            act.wait_ge(gu_free[1], r + 1)
            if first:
                act.wait_ge(m["mt_zero"], 2)
            fn(Z[:, 0:J - 1, PAD:PAD + C], Z[:, J:ZB, PAD - 1:PAD - 1 + C], ACT.Copy).then_inc(m["z_rep"], 1)
            for h in range(2):
                act.wait_ge(m[f"u_full{h}"], q + 1)
                wait(act, m["y_saved"], q * (16 * J))
                if first:
                    act.wait_ge(m["x_saved"], 32)
                fn(UY[:, hs[h]], PD[h][:, :], ACT.Copy).then_inc(m["u_sb"], 1)
            for a in range(2):
                act.wait_ge(m["rt_tr"], q * 2 + (a + 1))
                fn(RT[:, a].rearrange("p r n -> p (r n)"), PD[2 + a][:, :], ACT.Copy).then_inc(m["rt"], 1)
            if last:
                kernel_of_chunk(q)
            if not first:
                gelu_sigmoid(q - 1)
            for h in range(2):
                act.wait_ge(gu_full[h], r + 2)
                for n in range(2):
                    if h == 0:
                        act.wait_ge(gu_free[n], r + 1)
                    else:
                        act.wait_ge(m[f"g_saved{n}"], q * 32 + 16)
                    fn(G[n][:, :], PU[h][n][:, :], ACT.Sigmoid).then_inc(m["ga_w"] if n == 0 else gu_free[h], 1)
                if h == 0 and not last:
                    kernel_of_chunk(q)
                if last and h == 0:
                    for n in range(KT - 1):
                        gelu_hi(n)
            split_pair(r + 3, 1)

        def evacuate_y():
            for g2 in range(2):
                fn(UY.rearrange("p (r a c) -> p a r c", a=2, c=C)[:, g2], PD[2 + g2][:, :].rearrange("p (r c) -> p r c", c=C),
                   ACT.Copy).then_inc(m["y_sb"], 1)

        def gelu_sigmoid(q):
            for h in range(2):
                act.wait_ge(m["gel"], q * 2 + (h + 1))
                fn(TMP[:, h, :], TMP[:, h, :], ACT.Sigmoid, scale=GELU_S).then_inc(m["gelu_sig"], 1)

        mix(0, True)
        with act.Fori(1, KT - 1) as q:
            mix(q, False)
        mix(KT - 1, False, True)

        for n in range(KT - 1, 2 * KT - 3):
            gelu_hi(n)
        act.wait_ge(m["y_full"], KT)
        act.wait_ge(m["u_saved"], 16 * KT)
        evacuate_y()
        gelu_hi(2 * KT - 3)
        gelu_sigmoid(KT - 1)
        for n in range(2 * KT - 2, 2 * KT):
            gelu_hi(n)
        for h in range(2):
            act.wait_ge(m[f"g_saved{h}"], 32 * KT)

        def glu(i, behind=lambda s, h: None):
            for s in range(2):
                for h in range(2):
                    act.wait_ge(gu_full[h], i * 2 + (R_GLU + s + 1))
                    wait(act, ma_saved[h], i * 32 + s * 16)
                    fn(G[h][:, :], PU[h][1][:, :], ACT.Sigmoid).then_inc(g_ready[h], 1)
                    if h == 1:
                        split_pair(i * 2 + (R_GLU + s + 2), s)
                    behind(s, h)

        def ln_squares(c):
            for n in range(4 * c, 4 * c + 4):
                act.wait_ge(l["cen"], n + 1)
                if n % KT:
                    wait(act, l["vacc"], n - 4 - (n - 4) // KT if n >= 5 else 0)
                    act.wait_ge(b_["gl_lo"], 2 * KT)
                    dst = SQ4[n % 4]
                else:
                    act.wait_ge(l["mean"], 2)
                    dst = LS[n // KT]
                fn(dst, XT[:, n % KT, hs[n // KT]], ACT.Square).then_inc(l["sq"], 1)

        def ln_sigmoid(c):
            for n in range(4 * c, 4 * c + 4):
                k, h = n % KT, n // KT
                act.wait_ge(l["sum_in"], n + 1)
                if n >= 2:
                    act.wait_ge(l["sig"], n - 1)
                fn(SQ[n % 2], XT[:, k, hs[h]], ACT.Sigmoid, scale=vecs[:, 5 * KT + k:5 * KT + k + 1],
                   bias=vecs[:, 6 * KT + k:6 * KT + k + 1]).then_inc(l["ln_sig"], 1)

        def hi_half(h, free, ready, hi):
            act.wait_ge(gu_full[h], free)
            for k in range(KT):
                act.wait_ge(*ready(k, h))
                fn(Hhi[:, k, hs[h]], XT[:, k, hs[h]], ACT.Copy).then_inc(hi, 1)

        p_hi = lambda h: hi_half(h, R_PW, lambda k, h: (l["sig"], KT * h + k + 1), b_["p_hi"])
        m_hi = lambda h: hi_half(h, R_OUT, lambda k, h: (b_["m"], 4 * (k // 2) + 2 * h + k % 2 + 1), b_["m_hi"])

        glu(0)
        def ln_end_1(s, h):
            if s or h:
                ln_squares(2 * s + h - 1)

        def ln_end_2(s, h):
            if s == 0 and h == 0:
                ln_squares(3)
            if s == 1 and h == 1:
                ln_sigmoid(0)

        def ln_end_3(s, h):
            c = 2 * s + h
            if c < 3:
                ln_sigmoid(c + 1)
            if c >= 2:
                p_hi(h)

        glu(1, ln_end_1)
        glu(2, ln_end_2)
        glu(3, ln_end_3)
        for n in range(KT // 2):
            if n == KT // 2 - 1:
                m_hi(0)
            act.wait_ge(gu_full[1], R_PW + n + 1)
            split_pair(R_PW + n + 2, n % 2)
        m_hi(1)
        for n in range(KT // 2):
            for h in range(2):
                if h == 1:
                    act.wait_ge(gu_full[1], R_OUT + n + 1)
                    split_pair(R_OUT + n + 2, n % 2)
                for a in range(2):
                    square("nf2", 4 * n + 2 * h + a, 2 * n + a, h, (gu_free[h], R_OUT + n + 1))
        norm("nf2", None)
        ffn(1, R_FFN2, U_FFN2)
        for b, (j, kh) in enumerate(FIN):
            act.wait_ge(b_["fin_tr"], b + 1)
            fn(fin[j][:, kh * HW:(kh + 1) * HW], PUf[b % 4][:, :], ACT.Copy).then_inc(b_["fin_sb"], 1)
            if b:
                act.wait_ge(b_["fin_sq"], b)
            fn(Hhi[:, 0, 0:HW], PUf[b % 4][:, :], ACT.Square, accum_out=tok[:, 4 * kh, j:j + 1]).then_inc(b_["fin_sq"], 1)

    @block.vector
    def _(dve):
        v = nc.vector
        tt, ts, stt = v.tensor_tensor, v.tensor_scalar, v.scalar_tensor_tensor

        n_par = 0

        def do(ins):
            nonlocal n_par
            ins.then_inc(par_chain, 1)
            n_par += 1
            dve.wait_ge(par_chain, n_par)

        def slot(i, e=8):
            return tmp12[:, i, 0:e, :]

        def exp(dst, src, e, t0):
            xx, k, kk, p_ = [slot(t0 + i, e) for i in range(4)]
            do(ts(xx, src, -200.0, 200.0, ALU.max, ALU.min))
            do(ts(k, xx, 1.0 / math.log(2.0), RINT, ALU.mult, ALU.add))
            do(ts(k, k, RINT, None, ALU.subtract))
            ln2 = pieces(math.log(2.0), 12, 3)
            for c in ln2:
                do(stt(xx, k, -c, xx, ALU.mult, ALU.add))
            do(ts(p_, xx, 1.0 / 5040.0, None, ALU.mult))
            for c in (1.0 / 720.0, 1.0 / 120.0, 1.0 / 24.0, 1.0 / 6.0, 0.5, 1.0):
                do(stt(p_, p_, c, xx, ALU.add, ALU.mult))
            do(ts(p_, p_, 1.0, None, ALU.add))
            do(ts(kk, k, -126.0, 127.0, ALU.max, ALU.min))
            do(tt(k, k, kk, ALU.subtract))
            do(ts(k, k, -126.0, 127.0, ALU.max, ALU.min))
            for z in (kk, k):
                do(ts(xx.bitcast(I32), z, 127.0, 8388608.0, ALU.add, ALU.mult))
                do(tt(p_, p_, xx, ALU.mult))
            do(v.tensor_copy(dst, p_))

        a_re, a_im = par[:, 0, :], par[:, 1, :]
        ang, dtr, mag = slot(11), slot(10, 2), slot(9, 2)
        one = lambda ap: ap.unsqueeze(1)
        dt = slot(8, 1)
        k_, r_, r2, sn, cs, t_, q_ = [slot(i) for i in range(7)]

        def par_dt():
            dve.wait_ge(par_in, 1)
            dve.wait_ge(dw_in, 1)
            exp(dt, one(par[:, 2, :]), 1, 0)
            do(tt(dtr[:, 0:1], dt, one(a_re), ALU.mult))
            do(ts(dtr[:, 1:2], dtr[:, 0:1], float(J), None, ALU.mult))
            do(tt(ang[:, 0:1], dt, one(a_im), ALU.mult))
            for e in range(7):
                do(ts(ang[:, e + 1:e + 2], ang[:, 0:1], float(J * 2 ** e), None, ALU.mult))

        def par_mag():
            exp(mag, dtr, 2, 0)

        def par_angles():
            do(ts(k_, ang, 2.0 / math.pi, RINT, ALU.mult, ALU.add))
            do(ts(k_, k_, RINT, None, ALU.subtract))
            do(v.tensor_copy(r_, ang))
            for c in pieces(math.pi / 2, 8, 4):
                do(stt(r_, k_, -c, r_, ALU.mult, ALU.add))
            do(tt(r2, r_, r_, ALU.mult))
            do(ts(sn, r2, -1.9515295891e-4, 8.3321608736e-3, ALU.mult, ALU.add))
            do(tt(sn, sn, r2, ALU.mult))
            do(stt(sn, sn, -1.6666654611e-1, r2, ALU.add, ALU.mult))
            do(tt(sn, sn, r_, ALU.mult))
            do(tt(sn, sn, r_, ALU.add))
            do(ts(cs, r2, 2.443315711809948e-5, -1.388731625493765e-3, ALU.mult, ALU.add))
            do(tt(cs, cs, r2, ALU.mult))
            do(stt(cs, cs, 4.166664568298827e-2, r2, ALU.add, ALU.mult))
            do(stt(cs, cs, -0.5, r2, ALU.add, ALU.mult))
            do(ts(cs, cs, 1.0, None, ALU.add))

        def par_quadrant():
            do(ts(t_, k_, 0.25, RINT, ALU.mult, ALU.add))
            do(ts(t_, t_, RINT, None, ALU.subtract))
            do(stt(k_, t_, -4.0, k_, ALU.mult, ALU.add))
            do(tt(t_, k_, k_, ALU.mult))
            do(ts(r_, t_, 4.0, -1.0, ALU.is_equal, ALU.mult))
            do(ts(r2, t_, 0.0, None, ALU.is_equal))
            do(tt(r_, r_, r2, ALU.add))
            do(ts(t_, t_, 1.0, None, ALU.is_equal))
            do(tt(k_, k_, t_, ALU.mult))
            do(tt(q_, r_, sn, ALU.mult))
            do(tt(t_, k_, cs, ALU.mult))
            do(tt(q_, q_, t_, ALU.add))
            do(tt(t_, r_, cs, ALU.mult))
            do(tt(r2, k_, sn, ALU.mult))
            do(tt(t_, t_, r2, ALU.subtract))

        def par_powers():
            do(v.tensor_copy(EE[:, 0], t_[:, 1:8]))
            do(v.tensor_copy(EE[:, 1], q_[:, 1:8]))
            do(v.tensor_copy(one(M8), mag[:, 1:2]))
            do(v.memset(PW[:, 0, 0:1], 1.0))
            do(v.memset(PW[:, 1, 0:1], 0.0))
            do(tt(PW[:, 0, 1:2], mag[:, 0:1], t_[:, 0:1], ALU.mult))
            do(tt(PW[:, 1, 1:2], mag[:, 0:1], q_[:, 0:1], ALU.mult))
            for w in (1, 2, 4):
                lo_, hi_ = slice(1, w + 1), slice(w + 1, 2 * w + 1)
                br = PW[:, 0, w:w + 1].to_broadcast([P, w, NP])
                bi = PW[:, 1, w:w + 1].to_broadcast([P, w, NP])
                t1, t2 = slot(0, w), slot(1, w)
                do(tt(t1, PW[:, 0, lo_], br, ALU.mult))
                do(tt(t2, PW[:, 1, lo_], bi, ALU.mult))
                do(tt(PW[:, 0, hi_], t1, t2, ALU.subtract))
                do(tt(t1, PW[:, 0, lo_], bi, ALU.mult))
                do(tt(t2, PW[:, 1, lo_], br, ALU.mult))
                do(tt(PW[:, 1, hi_], t1, t2, ALU.add))

        def par_factor():
            ar1, ai1 = one(a_re), one(a_im)
            nr, ni = slot(0, 1), PW[:, 1, 1:2]
            t1, t2, den = slot(1, 1), slot(2, 1), slot(3, 1)
            do(ts(nr, PW[:, 0, 1:2], -1.0, None, ALU.add))
            do(tt(t1, ar1, ar1, ALU.mult))
            do(tt(t2, ai1, ai1, ALU.mult))
            do(tt(den, t1, t2, ALU.add))
            do(v.reciprocal(den, den))
            do(tt(t1, nr, ar1, ALU.mult))
            do(tt(t2, ni, ai1, ALU.mult))
            do(tt(t1, t1, t2, ALU.add))
            do(tt(one(frfi[:, 0, :]), t1, den, ALU.mult))
            do(tt(t1, ni, ar1, ALU.mult))
            do(tt(t2, nr, ai1, ALU.mult))
            do(tt(t1, t1, t2, ALU.subtract))
            tt(one(frfi[:, 1, :]), t1, den, ALU.mult).then_inc(par_done, 1)
            dve.wait_ge(par_done, 1)


        par_steps = {0: {(1, 0): par_dt}, 1: {(0, 0): par_mag, (1, 0): par_angles},
                     2: {(0, 0): par_quadrant, (1, 0): par_powers}, 3: {(0, 0): par_factor}}

        def split_pair(r, s):
            dve.wait_ge(w_hi, r + 1)
            tt(Wlo[s][:, :, :, :], Wraw[:, :, :, :], f32(Whi[s][:, :, :, :]), ALU.subtract).then_inc(w_lo, 1)

        def split_unit(u, s):
            dve.wait_ge(d_hi, u + 1)
            tt(Dlo[:, s, :], Draw[:, :], f32(Dhi[:, s, :]), ALU.subtract).then_inc(d_lo, 1)

        def rsqrt(dst, src, eps, chain, room=(NV, NT), between={}):
            i = 0

            def step(ins):
                nonlocal i
                chain.up(ins)
                if i in between:
                    between[i]()
                i += 1
                dve.wait_ge(chain.sem, chain.n)
            NV, NT = room
            step(ts(NV, src, eps, None, ALU.add))
            step(ts(dst.bitcast(I32), NV.bitcast(I32), -0.5, RSQRT_SEED, ALU.mult, ALU.add))
            for _ in range(3):
                step(stt(NT, dst, -0.5, dst, ALU.mult, ALU.mult))
                step(tt(NT, NT, NV, ALU.mult))
                step(stt(dst, NT, 1.5, dst, ALU.add, ALU.mult))

        chains = {n: Count(norms[n]["chain"]) for n in norms}

        def norm_rsqrt(name, h, between={}):
            dve.wait_ge(norms[name]["used"], h + 1)
            bank = PD[h] if name == "nf2" else PU[h][0]
            rsqrt(NRM_ROOM[name][0][h], bank[:, :], RMS_EPS, chains[name], NRM_ROOM[name][1:], between)

        def scale(name, gain, n, dst):
            k, h = n % KT, n // KT
            stt(dst, XT[:, k, hs[h]], vecs[:, gain * KT + k:gain * KT + k + 1], NRM_ROOM[name][0][h], ALU.mult, ALU.mult)\
                .then_inc(norms[name]["hn"], 1)

        def norm(name, gain):
            def tile(n):
                if n >= 3:
                    dve.wait_ge(norms[name]["lo"], n - 2)
                scale(name, gain, n, GN[n % 3])

            for n in range(2):
                tile(n)
            norm_rsqrt(name, 1, {i: (lambda n=n: tile(n)) for n, i in zip(range(2, KT), (1, 3, 5, 7, 9, 10))})
            for n in range(KT, 2 * KT):
                tile(n)
            dve.wait_ge(norms[name]["hn"], 2 * KT)

        def ffn(n, r0, u0, g0, after):
            def body(i, last, end=False):
                fill = par_steps.get(i, {}) if isinstance(i, int) else {}
                for s in range(2):
                    for h in range(2):
                        dve.wait_ge(g_ready[h], i * 2 + (g0 - n * 2 * FI + s + 1))
                        tt(G[h][:, :], G[h][:, :], PU[h][1][:, :], ALU.mult).then_inc(gu_free[h], 1)
                        dve.wait_ge(gu_free[h], i * 2 + (r0 - n * 2 * FI + s + 1))
                        wait(dve, dn_full, i * 16)
                        v.tensor_copy(Ahi[:, s, hs[h]], G[h][:, :]).then_inc(a_hi[h], 1)
                        dve.wait_ge(a_hi[h], i * 2 + (s + 1))
                        tt(Alo[:, s, hs[h]], G[h][:, :], f32(Ahi[:, s, hs[h]]), ALU.subtract).then_inc(a_lo[h], 1)
                        if s == 0:
                            split_unit(i * 2 + (u0 - n * 2 * FI + h), h)
                        if h == 1 and not last:
                            split_pair(i * 2 + (r0 - n * 2 * FI + s + 2), s)
                        if (s, h) in fill:
                            fill[s, h]()
                def add(h, d):
                    z = 8 * h + d
                    dve.wait_ge(dn_full, i * 16 + (z + 1))
                    stt(XT[:, d, hs[h]], PD[z % 4][:, :], 0.5, XT[:, d, hs[h]], ALU.mult, ALU.add)\
                        .then_inc(dn_free[z % 4], 1)

                for h in range(2):
                    for d in range(4 if end and h and n == 0 else KT):
                        add(h, d)
                if end and n == 0:
                    norm_rsqrt(after, 0, {1: lambda: add(1, 4), 3: lambda: add(1, 5), 5: lambda: add(1, 6),
                                          7: lambda: add(1, 7)})

            if n == 0:
                for i in par_steps:
                    body(i, False)
            with dve.Fori(n * FI + (0 if n else len(par_steps)), (n + 1) * FI - 1) as i:
                body(i, False)
            body((n + 1) * FI - 1, n == 1, True)

        def x_step(j):
            if j < J:
                dve.wait_ge(x_sq, j + 1)
                x_rsqrt(j)
                if j >= 2:
                    dve.wait_ge(n_full, 2 * (j - 1))
                ts(diag[j % 2], ident[:, :], tok[:, 1, j:j + 1], None, ALU.mult).then_inc(x_diag, 1)
            if j == 1:
                dve.wait_ge(vec_in, 1)
            if j:
                for kh in range(2):
                    b = 2 * (j - 1) + kh
                    dve.wait_ge(n_full, b + 1)
                    if b >= 2:
                        dve.wait_ge(n_lo, b - 1)
                    tt(G[kh][:, :].rearrange("p (k c) -> p k c", c=P),
                       PUf[b % 4 if j <= 4 else 2 + kh][:, :].rearrange("p (k c) -> p k c", c=P),
                       vecs[:, 4 * kh:4 * kh + 4].unsqueeze(2).to_broadcast([P, 4, P]), ALU.mult).then_inc(n_g, 1)
            if j < J:
                dve.wait_ge(x_full, 2 * j + 2)
                v.tensor_copy(XT[:, 4:8, j * P:(j + 1) * P], PD[(2 * j + 1) % 4][:, :].rearrange("p (k c) -> p k c", c=P))\
                    .then_inc(x_evac[1], 1)

        rows_chain = Count(x_chain)

        def x_rsqrt(j):
            def step(ins):
                dve.wait_ge(rows_chain.sem, rows_chain.up(ins))
            ss, r, nv, nt = [tok[:, i, j:j + 1] for i in range(4)]
            step(ts(nv, ss, 1.0 / D, RMS_EPS, ALU.mult, ALU.add))
            step(ts(r.bitcast(I32), nv.bitcast(I32), -0.5, RSQRT_SEED, ALU.mult, ALU.add))
            for _ in range(3):
                step(stt(nt, r, -0.5, r, ALU.mult, ALU.mult))
                step(tt(nt, nt, nv, ALU.mult))
                step(stt(r, nt, 1.5, r, ALU.add, ALU.mult))

        dve.wait_ge(const, 3)
        for j in range(5):
            x_step(j)
        split_pair(0, 0)
        for j in range(5, J + 1):
            x_step(j)
        split_pair(1, 1)
        dve.wait_ge(n_lo, 2 * J)
        for kh in range(2):
            dve.wait_ge(x_evac[kh], J)
        ffn(0, 0, 0, 0, "nmx")
        norm("nmx", 1)

        dve.wait_ge(m["x_saved"], 32)
        v.memset(Z[:, :, 0:PAD], 0.0).then_inc(m["mt_zero"], 1)
        v.memset(MTf, 0.0).then_inc(m["mt_zero"], 1)
        v.memset(S[:, :, :, 0:1], 0.0).then_inc(m["s_zero"], 1)
        CVb = CV.rearrange("p (b c) -> p b c", b=J)
        ROT = 5 + 1 + 2 * PR + 6

        def taps(q, s0, s1):
            for s in range(s0, s1):
                z_ = Z[:, J - 1 - s % J:ZB - s % J, PAD - s // J:PAD - s // J + C]
                w_ = wq[:, TAPS - 1 - s:TAPS - s]
                if s == 0:
                    dve.wait_ge(m["z_rep"], q + 1)
                    dve.wait_ge(m["wq"], q * 3 + 3)
                    wait(dve, m["cv_saved"], q * 16)
                    ts(CVb, z_, w_, wq[:, TAPS:TAPS + 1], ALU.mult, ALU.add).then_inc(m["conv"], 1)
                else:
                    dve.wait_ge(m["conv"], q * TAPS + s)
                    stt(CVb, z_, w_, CVb, ALU.mult, ALU.add).then_inc(m["conv"], 1)

        def gelu_in(q):
            dve.wait_ge(m["yc_ld"], q * 16 + 16)
            for h in range(2):
                t_ = TMP[:, h, :]
                tt(t_, YC[:, hs[h]], YC[:, hs[h]], ALU.mult).then_inc(m["gchain"], 1)
                dve.wait_ge(m["gchain"], q * 4 + (2 * h + 1))
                ts(t_, t_, GELU_A, 1.0, ALU.mult, ALU.add).then_inc(m["gchain"], 1)
                dve.wait_ge(m["gchain"], q * 4 + (2 * h + 2))
                tt(t_, t_, YC[:, hs[h]], ALU.mult).then_inc(m["gel"], 1)

        def gelu_out(q):
            for h in range(2):
                dve.wait_ge(m["gelu_sig"], q * 2 + (h + 1))
                tt(YC[:, hs[h]], YC[:, hs[h]], TMP[:, h, :], ALU.mult).then_inc(m["gelu"], 1)

        def gelu_lo(n):
            if n < 2 * (KT - 1):
                k, h, src = n % (KT - 1), n // (KT - 1), glb[n % NB]
            else:
                k, h = KT - 1, n - 2 * (KT - 1)
                src = YC[:, hs[h]]
            dve.wait_ge(b_["gl_hi"], n + 1)
            tt(Hlo[:, k, hs[h]], src, f32(Hhi[:, k, hs[h]]), ALU.subtract).then_inc(b_["gl_lo"], 1)

        def mix(q, first, last=False):
            r = q * 2 + R_MIX
            wait(dve, m["conv"], q * TAPS)
            wait(dve, m["dd"], q)
            v.tensor_copy(wq[:, 0:TAPS], wdw[:, bass.ds(q, 1), :].rearrange("p a t -> p (a t)")).then_inc(m["wq"], 1)
            v.tensor_copy(wq[:, TAPS:TAPS + 1], vecs[:, bass.ds(q + 4 * KT, 1)]).then_inc(m["wq"], 1)
            v.tensor_copy(dq[:, :], dvec[:, bass.ds(q * GQ, GQ)]).then_inc(m["wq"], 1)
            for h in range(2):
                dve.wait_ge(g_ready[h], q + (FT + 1))
                tt(Z[:, J - 1 + 4 * h:J + 3 + 4 * h, PAD:PAD + C], G[h][:, :].rearrange("p (b c) -> p b c", c=C),
                   PU[h][0][:, :].rearrange("p (b c) -> p b c", c=C), ALU.mult).then_inc(gu_free[h], 1)
                if h == 0:
                    split_unit(q + U_MIX, 0)
            split_pair(r + 2, 0)
            taps(q, 0, 10)
            if not first:
                gelu_in(q - 1)
            taps(q, 10, 14)
            if not first:
                gelu_out(q - 1)
            tt(dd[:, :, :], ident[0:SG, 0:SG].unsqueeze(1).to_broadcast([SG, GQ, SG]),
               dq[:, :].unsqueeze(2).to_broadcast([SG, GQ, SG]), ALU.mult).then_inc(m["dd"], 1)
            dve.wait_ge(m["dd"], q + 1)
            dve.wait_ge(m["k_sb"], q * 2 + 2)
            tt(KK[0:SG, :, 0:SG], KK[0:SG, :, 0:SG], dd[:, :, :], ALU.add).then_inc(m["k_d"], 1)
            n = 0

            def step(ins):
                nonlocal n
                ins.then_inc(m["chain"], 1)
                n += 1
                dve.wait_ge(m["chain"], q * ROT + n)

            dve.wait_ge(m["delta"], q + 1)
            dve.wait_ge(m["rot_ld"], q * 16 + 16)
            if last:
                for half in range(2):
                    gelu_lo(half)
            t0, t1, t2 = TMP[:, 0, :], TMP[:, 1, :], TMP[:, 2, :]
            step(tt(t0, PD[2][:, :], COS, ALU.mult))
            step(tt(t1, PD[3][:, :], SIN, ALU.mult))
            step(tt(t0, t0, t1, ALU.add))
            step(tt(t1, PD[3][:, :], COS, ALU.mult))
            step(tt(t2, PD[2][:, :], SIN, ALU.mult))
            step(tt(t1, t1, t2, ALU.subtract))
            for t_ in (t0, t1):
                for pr in range(PR):
                    c_ = slice(pr * C, (pr + 1) * C)
                    step(v.tensor_tensor_scan(t_[:, c_], M8q[:, pr:pr + 1].to_broadcast([P, C]), t_[:, c_], 0.0,
                                              ALU.mult, ALU.add))
            sre, sim = S[:, 0, :, 1:C + 1], S[:, 1, :, 1:C + 1]
            b3 = lambda ap: ap.rearrange("p (r c) -> p r c", c=C)
            if first:
                dve.wait_ge(m["s_zero"], 1)
            else:
                dve.wait_ge(m["y_full"], q)
            step(tt(t2, t0, COS, ALU.mult))
            step(tt(sre, b3(t1), b3(SIN), ALU.mult))
            step(tt(sre, b3(t2), sre, ALU.subtract))
            step(tt(t2, t0, SIN, ALU.mult))
            step(tt(t0, t1, COS, ALU.mult))
            step(tt(sim, b3(t2), b3(t0), ALU.add))
            assert n == ROT
            v.tensor_copy(t2[:, 0:1], t2[:, 0:1]).then_inc(m["rot"], 1)
            if not last:
                taps(q, 14, 17)
                split_pair(r + 3, 1)
                taps(q, 17, TAPS)

        mix(0, True)
        with dve.Fori(1, KT - 1) as q:
            mix(q, False)
        mix(KT - 1, False, True)
        for n in range(2, 2 * KT - 3):
            gelu_lo(n)
        taps(KT - 1, 14, 24)
        gelu_lo(2 * KT - 3)
        gelu_in(KT - 1)
        gelu_out(KT - 1)
        for n in range(2 * (KT - 1), 2 * KT):
            gelu_lo(n)
        split_pair(R_GLU + 1, 1)

        def glu(i, behind=lambda c: None):
            for s in range(2):
                for h in range(2):
                    dve.wait_ge(g_ready[h], i * 2 + (FT + KT + s + 1))
                    tt(G[h][:, :], G[h][:, :], PU[h][0][:, :], ALU.mult).then_inc(gu_free[h], 1)
                    dve.wait_ge(gu_free[h], i * 2 + (R_GLU + s + 1))
                    dve.wait_ge(b_["ga_ld"], i * 32 + (16 * s + 16))
                    tt(G[h][:, :], G[h][:, :], GAB[:, hs[h]], ALU.mult).then_inc(b_["t"], 1)
                    if h == 1:
                        split_pair(i * 2 + (R_GLU + s + 2), s)
                    behind(2 * s + h)

        def ln_center(c):
            for n in range(4 * c, 4 * c + 4):
                dve.wait_ge(l["mean"], n // KT + 1)
                xt = XT[:, n % KT, hs[n // KT]]
                tt(xt, xt, PD[n // KT][:, :], ALU.subtract).then_inc(l["cen"], 1)

        chain = Count(l["chain"])

        def ln_scale(c):
            for n in range(4 * c, 4 * c + 4):
                xt = XT[:, n % KT, hs[n // KT]]
                tt(xt, xt, RS[n // KT], ALU.mult).then_inc(l["sum_in"], 1)
                if n % 4:
                    ln_end(n - 1)
            ln_end(4 * c + 3)

        def ln_end(n):
            k, h = n % KT, n // KT
            xt = XT[:, k, hs[h]]
            dve.wait_ge(l["ln_sig"], n + 1)
            ts(xt, xt, vecs[:, 5 * KT + k:5 * KT + k + 1], vecs[:, 6 * KT + k:6 * KT + k + 1], ALU.mult, ALU.add)\
                .then_inc(l["aff"], 1)
            dve.wait_ge(l["aff"], n + 1)
            tt(xt, xt, SQ[n % 2], ALU.mult).then_inc(l["sig"], 1)

        def lo_half(h, hi, lo):
            for k in range(KT):
                dve.wait_ge(hi, KT * h + k + 1)
                tt(Hlo[:, k, hs[h]], XT[:, k, hs[h]], f32(Hhi[:, k, hs[h]]), ALU.subtract).then_inc(lo, 1)

        def behind_1(c):
            if c:
                ln_center(c - 1)

        def behind_2(c):
            if c == 0:
                ln_center(3)
            if c in (1, 2):
                dve.wait_ge(l["var"], c)
                dve.wait_ge(l["vacc"], 2 * (KT - 1))
                rsqrt(RS[c - 1], PD[1 + c][:, :], LN_EPS, chain)
            if c == 3:
                ln_scale(0)

        def behind_3(c):
            if c < 3:
                ln_scale(c + 1)
            if c >= 2:
                lo_half(c - 2, b_["p_hi"], b_["p_lo"])

        def behind_0(c):
            if c == 1:
                taps(KT - 1, 24, TAPS)

        glu(0, behind_0)
        glu(1, behind_1)
        glu(2, behind_2)
        glu(3, behind_3)
        for n in range(KT // 2):
            dve.wait_ge(b_["gb_ld"], 64 * (n + 1))
            for h in range(2):
                dve.wait_ge(gu_full[h], R_PW + n + 1)
                for a in range(2):
                    tt(XT[:, 2 * n + a, hs[h]], GBB[a][:, hs[h]], PU[h][a][:, :], ALU.mult)\
                        .then_inc(b_["m2"] if a == 0 else gu_free[h], 1)
                dve.wait_ge(b_["m2"], 2 * n + h + 1)
                dve.wait_ge(gu_free[h], R_PW + n + 1)
                for a in range(2):
                    xt = XT[:, 2 * n + a, hs[h]]
                    tt(xt, xt, MAB[a][:, hs[h]], ALU.add).then_inc(b_["m"], 1)
                if n == KT // 2 - 1:
                    lo_half(h, b_["m_hi"], b_["m_lo"])
            split_pair(R_PW + n + 2, n % 2)
        for n in range(KT // 2):
            dve.wait_ge(b_["xo_ld"], 32 * (n + 1))
            for h in range(2):
                dve.wait_ge(gu_full[h], R_OUT + n + 1)
                for a in range(2):
                    tt(XT[:, 2 * n + a, hs[h]], GBB[a][:, hs[h]], PU[h][a][:, :], ALU.add)\
                        .then_inc(b_["x"] if a == 0 else gu_free[h], 1)
                if n == KT // 2 - 1 and h == 0:
                    norm_rsqrt("nf2", 0)
            split_pair(R_OUT + n + 2, n % 2)
        for h in range(2):
            dve.wait_ge(gu_free[h], R_FFN2)
        norm("nf2", 2)
        ffn(1, R_FFN2, U_FFN2, FT + 2 * KT, None)
        fin_chain = Count(b_["fin_chain"])
        dve.wait_ge(b_["fin_ld"], 16)
        for h in range(2):
            def step(ins):
                dve.wait_ge(fin_chain.sem, fin_chain.up(ins))
            dve.wait_ge(b_["fin_sq"], J * (h + 1))
            dve.wait_ge(b_["fin_sb"], J * (h + 1))
            ss, r, nv, nt, s2 = [tok[:, i, 4 * h:4 * h + 4] for i in range(5)]
            step(tt(ss, ss, s2, ALU.add))
            step(ts(nv, ss, 1.0 / D, RMS_EPS, ALU.mult, ALU.add))
            step(ts(r.bitcast(I32), nv.bitcast(I32), -0.5, RSQRT_SEED, ALU.mult, ALU.add))
            for _ in range(3):
                step(stt(nt, r, -0.5, r, ALU.mult, ALU.mult))
                step(tt(nt, nt, nv, ALU.mult))
                step(stt(r, nt, 1.5, r, ALU.add, ALU.mult))
            for j in range(4 * h, 4 * h + 4):
                stt(fin[j], fin[j], tok[:, 1, j:j + 1], GF, ALU.mult, ALU.mult).then_inc(b_["fin_out"], 1)

    ctx.close()


_INS = ["x", "norm_ffn1_g", "w_ffn1_up", "w_ffn1_down", "norm_mix_g", "w_in", "ssm_a_re", "ssm_a_im", "ssm_log_dt",
        "ssm_b_re", "ssm_b_im", "ssm_c_re", "ssm_c_im", "ssm_d", "w_ssm_glu", "conv_dw_w", "conv_dw_b", "conv_ln_g",
        "conv_ln_b", "w_conv_pw", "w_out", "norm_ffn2_g", "w_ffn2_up", "w_ffn2_down", "norm_final_g"]


def kernel(**inputs):
    import numpy as _np
    import concourse.bacc as _bacc
    from concourse import mybir as _mybir
    from concourse.bass_utils import run_bass_kernel_spmd as _run

    nc = _bacc.Bacc("TRN2", target_bir_lowering=False, num_devices=1)
    arrays, args = {}, []
    for name in _INS:
        a = _np.ascontiguousarray(inputs[name])
        arrays[f"in_{name}"] = a
        args.append(nc.dram_tensor(f"in_{name}", a.shape, _mybir.dt.from_np(a.dtype), kind="ExternalInput").ap())
    out = nc.dram_tensor("out", (1, L, D), F32, kind="ExternalOutput").ap()
    build(nc, *args, out)
    r = _run(nc, [arrays], core_ids=[0])
    return r.results[0]["out"]
```
